# Optimizing a Trainium2 kernel written in Bass

```python
import math
import jax
import jax.numpy as jnp
from jax import lax
import numpy as np

D_MODEL = 1024
BATCH = 1
SEQ = 1024
DEPTH = 1

PLE_DIM = 256
D_MIX = D_MODEL
GLA_WIDTH = D_MIX // 2
GDN_WIDTH = D_MIX - GLA_WIDTH
GLA_HEADS = 4
GLA_DV = GLA_WIDTH // GLA_HEADS
GLA_DK = GLA_DV // 2
GLA_GATE_RANK = 16
GLA_GATE_NORM = 16.0
GDN_HEADS = 4
GDN_DK = GDN_WIDTH // GDN_HEADS
GDN_DV = GDN_WIDTH // GDN_HEADS
GDN_QKV = 2 * GDN_HEADS * GDN_DK + GDN_HEADS * GDN_DV
CONV_WIDTH = 4
CHUNK = 64
N_EXPERTS = 32
TOP_K = 4
D_FF = D_MODEL
SWIGLU_LIMIT = 7.0
SWIGLU_ALPHA = 1.702
MOE_BLOCK = 128
EPS = 1e-6
IN_SPLITS = (GLA_HEADS * GLA_DK, GLA_HEADS * GLA_DK, GLA_WIDTH, GLA_WIDTH, GLA_GATE_RANK,
             GDN_QKV, GDN_WIDTH, GDN_HEADS, GDN_HEADS)
D_IN = 2 * GLA_HEADS * GLA_DK + 2 * GLA_WIDTH + GLA_GATE_RANK + GDN_QKV + GDN_WIDTH + 2 * GDN_HEADS

kernel_name = 'hybrid_gla_gdn_moe_ple_block'

def rmsnorm(x, g):
    xf = x.astype(jnp.float32)
    y = xf * lax.rsqrt(jnp.mean(xf * xf, axis=-1, keepdims=True) + EPS)
    return (y * g.astype(jnp.float32)).astype(x.dtype)

def l2norm(t):
    return t * lax.rsqrt(jnp.sum(t * t, axis=-1, keepdims=True) + EPS)

def to_chunks(t):
    B, S, H, d = t.shape
    return t.reshape(B, S // CHUNK, CHUNK, H, d).transpose(0, 3, 1, 2, 4).astype(jnp.float32)

def to_chunks_scalar(t):
    B, S, H = t.shape
    return t.reshape(B, S // CHUNK, CHUNK, H).transpose(0, 3, 1, 2).astype(jnp.float32)

def from_chunks(o):
    B, H, N, C, d = o.shape
    return o.transpose(0, 2, 3, 1, 4).reshape(B, N * C, H, d)

def causal_dwconv(x, w):
    K, Ch = w.shape
    return lax.conv_general_dilated(x, w[:, None, :].astype(x.dtype), window_strides=(1,),
                                    padding=[(K - 1, 0)], dimension_numbers=('NWC', 'WIO', 'NWC'),
                                    feature_group_count=Ch)

def gla_chunked(q, k, v, log_a):
    C = q.shape[-2]
    causal = jnp.tril(jnp.ones((C, C), bool))[:, :, None]

    def step(S, inp):
        q_c, k_c, v_c, a_c = inp
        b = jnp.cumsum(a_c, axis=-2)
        diff = b[..., :, None, :] - b[..., None, :, :]
        dec = jnp.exp(jnp.where(causal, diff, -jnp.inf))
        attn = jnp.einsum('bhid,bhjd,bhijd->bhij', q_c, k_c, dec)
        o = (jnp.einsum('bhid,bhde->bhie', q_c * jnp.exp(b), S)
             + jnp.einsum('bhij,bhje->bhie', attn, v_c))
        b_last = b[..., -1:, :]
        S = (jnp.exp(b_last)[..., 0, :, None] * S
             + jnp.einsum('bhjd,bhje->bhde', k_c * jnp.exp(b_last - b), v_c))
        return S, o

    B, H = q.shape[:2]
    S0 = jnp.zeros((B, H, q.shape[-1], v.shape[-1]), jnp.float32)
    xs = tuple(jnp.moveaxis(t, 2, 0) for t in (q, k, v, log_a))
    _, o = lax.scan(step, S0, xs)
    return jnp.moveaxis(o, 0, 2)

def gated_delta_chunked(q, k, v, g, beta):
    C = q.shape[-2]
    dv = v.shape[-1]
    strict = jnp.tril(jnp.ones((C, C), bool), -1)
    causal = jnp.tril(jnp.ones((C, C), bool))
    b = jnp.cumsum(g, axis=-1)
    diff = b[..., :, None] - b[..., None, :]
    kk = jnp.einsum('bhnid,bhnjd->bhnij', k, k)
    L = jnp.where(strict, beta[..., :, None] * jnp.exp(jnp.where(strict, diff, 0.0)) * kk, 0.0)
    eye = jnp.eye(C, dtype=jnp.float32)
    rhs = jnp.concatenate([beta[..., None] * v, (beta * jnp.exp(b))[..., None] * k], axis=-1)
    sol = lax.linalg.triangular_solve(eye + L, rhs, left_side=True, lower=True, unit_diagonal=True)
    u, w = sol[..., :dv], sol[..., dv:]
    qk = jnp.einsum('bhnid,bhnjd->bhnij', q, k)
    a_qk = jnp.where(causal, jnp.exp(jnp.where(causal, diff, 0.0)) * qk, 0.0)
    q_dec = q * jnp.exp(b)[..., None]
    k_dec = k * jnp.exp(b[..., -1:] - b)[..., None]
    chunk_dec = jnp.exp(b[..., -1])

    def step(S, inp):
        u_c, w_c, q_c, k_c, a_c, d_c = inp
        delta = u_c - jnp.einsum('bhcd,bhde->bhce', w_c, S)
        o = jnp.einsum('bhcd,bhde->bhce', q_c, S) + jnp.einsum('bhij,bhje->bhie', a_c, delta)
        S = d_c[..., None, None] * S + jnp.einsum('bhcd,bhce->bhde', k_c, delta)
        return S, o

    B, H = q.shape[:2]
    S0 = jnp.zeros((B, H, q.shape[-1], dv), jnp.float32)
    xs = tuple(jnp.moveaxis(t, 2, 0) for t in (u, w, q_dec, k_dec, a_qk, chunk_dec))
    _, o = lax.scan(step, S0, xs)
    return jnp.moveaxis(o, 0, 2)

def moe_ffn(xn, w_router, b_router, w_gate_up, b_gate_up, w_down, b_down):
    B, S, D = xn.shape
    T = B * S
    A = T * TOP_K
    xt = xn.reshape(T, D)
    logits = (xt @ w_router + b_router).astype(jnp.float32)
    top_logit, top_e = lax.top_k(logits, TOP_K)
    gates = jax.nn.softmax(top_logit, axis=-1)
    flat_e = top_e.reshape(A).astype(jnp.int32)
    order = jnp.argsort(flat_e)
    e_sorted = flat_e[order]
    tok_sorted = order // TOP_K
    gate_sorted = gates.reshape(A)[order]
    counts = jnp.zeros((N_EXPERTS,), jnp.int32).at[flat_e].add(1)
    padded = (counts + MOE_BLOCK - 1) // MOE_BLOCK * MOE_BLOCK
    start = jnp.cumsum(counts) - counts
    pad_end = jnp.cumsum(padded)
    pad_start = pad_end - padded
    dest = pad_start[e_sorted] + jnp.arange(A, dtype=jnp.int32) - start[e_sorted]
    n_blocks = -(-A // MOE_BLOCK) + N_EXPERTS
    x_pad = jnp.zeros((n_blocks * MOE_BLOCK, D), xn.dtype).at[dest].set(xt[tok_sorted])
    block_e = jnp.minimum(jnp.searchsorted(pad_end, jnp.arange(n_blocks, dtype=jnp.int32) * MOE_BLOCK,
                                           side='right'), N_EXPERTS - 1)

    def expert_block(args):
        xb, e = args
        hgu = xb @ w_gate_up[e] + b_gate_up[e]
        gate, up = jnp.split(hgu, 2, axis=-1)
        gate = jnp.minimum(gate, SWIGLU_LIMIT)
        up = jnp.clip(up, -SWIGLU_LIMIT, SWIGLU_LIMIT)
        act = (up + 1.0) * gate * jax.nn.sigmoid(SWIGLU_ALPHA * gate)
        return act @ w_down[e] + b_down[e]

    y_pad = lax.map(expert_block, (x_pad.reshape(n_blocks, MOE_BLOCK, D), block_e))
    y_sorted = y_pad.reshape(n_blocks * MOE_BLOCK, D)[dest]
    y = jnp.zeros((T, D), y_sorted.dtype).at[tok_sorted].add(
        y_sorted * gate_sorted[:, None].astype(y_sorted.dtype))
    return y.reshape(B, S, D)

def setup_inputs(seed: int = 0) -> dict:
    key = jax.random.key(seed)
    ks = jax.random.split(key, 24)
    f32 = jnp.float32

    def nrm(k, shape, scale):
        return jax.random.normal(k, shape, f32) * scale

    def gain(k, shape):
        return 1.0 + 0.02 * jax.random.normal(k, shape, f32)

    dt = jnp.exp(jax.random.uniform(ks[9], (DEPTH, GDN_HEADS), f32, math.log(1e-3), math.log(1e-1)))
    return {
        'x': nrm(ks[0], (BATCH, SEQ, D_MODEL), 1.0),
        'p': nrm(ks[1], (DEPTH, BATCH, SEQ, PLE_DIM), 1.0),
        'g_mix': gain(ks[2], (DEPTH, D_MODEL)),
        'w_in': nrm(ks[3], (DEPTH, D_MODEL, D_IN), D_MODEL ** -0.5),
        'w_gla_gate': nrm(ks[4], (DEPTH, GLA_GATE_RANK, GLA_HEADS * GLA_DK), GLA_GATE_RANK ** -0.5),
        'b_gla_gate': nrm(ks[5], (DEPTH, GLA_HEADS * GLA_DK), 0.1),
        'g_gla_out': gain(ks[6], (DEPTH, GLA_DV)),
        'w_conv': nrm(ks[7], (DEPTH, CONV_WIDTH, GDN_QKV), CONV_WIDTH ** -0.5),
        'gdn_a_log': jnp.log(jax.random.uniform(ks[8], (DEPTH, GDN_HEADS), f32, 1.0, 16.0)),
        'gdn_dt_bias': dt + jnp.log(-jnp.expm1(-dt)),
        'g_gdn_out': gain(ks[10], (DEPTH, GDN_DV)),
        'w_out': nrm(ks[11], (DEPTH, D_MIX, D_MODEL), D_MIX ** -0.5),
        'g_moe': gain(ks[12], (DEPTH, D_MODEL)),
        'w_router': nrm(ks[13], (DEPTH, D_MODEL, N_EXPERTS), D_MODEL ** -0.5),
        'b_router': nrm(ks[14], (DEPTH, N_EXPERTS), 0.01),
        'w_gate_up': nrm(ks[15], (DEPTH, N_EXPERTS, D_MODEL, 2 * D_FF), D_MODEL ** -0.5),
        'b_gate_up': nrm(ks[16], (DEPTH, N_EXPERTS, 2 * D_FF), 0.01),
        'w_down': nrm(ks[17], (DEPTH, N_EXPERTS, D_FF, D_MODEL), D_FF ** -0.5),
        'b_down': nrm(ks[18], (DEPTH, N_EXPERTS, D_MODEL), 0.01),
        'g_ple_in': gain(ks[19], (DEPTH, D_MODEL)),
        'w_ple_gate': nrm(ks[20], (DEPTH, D_MODEL, D_MODEL), D_MODEL ** -0.5),
        'w_ple_proj': nrm(ks[21], (DEPTH, PLE_DIM, D_MODEL), PLE_DIM ** -0.5),
        'g_ple_post': gain(ks[22], (DEPTH, D_MODEL)),
        'g_final': gain(ks[23], (D_MODEL,)),
    }

def reference(x, p, g_mix, w_in, w_gla_gate, b_gla_gate, g_gla_out, w_conv, gdn_a_log, gdn_dt_bias,
              g_gdn_out, w_out, g_moe, w_router, b_router, w_gate_up, b_gate_up, w_down, b_down,
              g_ple_in, w_ple_gate, w_ple_proj, g_ple_post, g_final):
    B, S, D = x.shape
    split_idx = np.cumsum(IN_SPLITS)[:-1].tolist()
    h = x
    for i in range(DEPTH):
        n = rmsnorm(h, g_mix[i])
        proj = n @ w_in[i]
        gq, gk, gv, gr, glr, dqkv, dz, da, db = jnp.split(proj, split_idx, axis=-1)

        log_a = jax.nn.log_sigmoid((glr @ w_gla_gate[i] + b_gla_gate[i]).astype(jnp.float32)) / GLA_GATE_NORM
        o_gla = gla_chunked(
            to_chunks(gq.reshape(B, S, GLA_HEADS, GLA_DK).astype(jnp.float32) * GLA_DK ** -0.5),
            to_chunks(gk.reshape(B, S, GLA_HEADS, GLA_DK)),
            to_chunks(gv.reshape(B, S, GLA_HEADS, GLA_DV)),
            to_chunks(log_a.reshape(B, S, GLA_HEADS, GLA_DK)))
        o_gla = rmsnorm(from_chunks(o_gla), g_gla_out[i]).reshape(B, S, GLA_WIDTH) * jax.nn.silu(gr)

        qkv = jax.nn.silu(causal_dwconv(dqkv, w_conv[i]))
        dq = qkv[..., :GDN_HEADS * GDN_DK].reshape(B, S, GDN_HEADS, GDN_DK).astype(jnp.float32)
        dk = qkv[..., GDN_HEADS * GDN_DK:2 * GDN_HEADS * GDN_DK].reshape(B, S, GDN_HEADS, GDN_DK).astype(jnp.float32)
        dv = qkv[..., 2 * GDN_HEADS * GDN_DK:].reshape(B, S, GDN_HEADS, GDN_DV)
        dq = l2norm(dq) * GDN_DK ** -0.5
        dk = l2norm(dk)
        g_dec = -jnp.exp(gdn_a_log[i].astype(jnp.float32)) * jax.nn.softplus(
            (da + gdn_dt_bias[i]).astype(jnp.float32))
        beta = jax.nn.sigmoid(db.astype(jnp.float32))
        o_gdn = gated_delta_chunked(to_chunks(dq), to_chunks(dk), to_chunks(dv),
                                    to_chunks_scalar(g_dec), to_chunks_scalar(beta))
        o_gdn = rmsnorm(from_chunks(o_gdn), g_gdn_out[i]).reshape(B, S, GDN_WIDTH) * jax.nn.silu(dz)

        mixed = jnp.concatenate([o_gla, o_gdn], axis=-1).astype(h.dtype)
        h = h + mixed @ w_out[i]

        h = h + moe_ffn(rmsnorm(h, g_moe[i]), w_router[i], b_router[i], w_gate_up[i], b_gate_up[i],
                        w_down[i], b_down[i])

        pe = rmsnorm(p[i] @ w_ple_proj[i], g_ple_post[i])
        gate = jax.nn.sigmoid(rmsnorm(h, g_ple_in[i]) @ w_ple_gate[i])
        h = h + gate * pe
    return rmsnorm(h, g_final)


_drawn_inputs = setup_inputs


def setup_inputs(seed=0):
    import zlib

    import numpy as np

    out = dict(_drawn_inputs(seed))
    spreads = {}
    factors = {'b_gate_up': 8.0,
     'b_down': 8.0,
     'g_ple_in': 21.683,
     'g_ple_post': 21.101,
     'g_final': 8.476}
    for name, (base, spread) in spreads.items():
        noise = np.random.default_rng([zlib.crc32(name.encode()), seed]).standard_normal(out[name].shape)
        drawn = base * np.exp(spread * noise) if base else spread * noise
        out[name] = jnp.asarray(drawn.astype(out[name].dtype))
    for name, factor in factors.items():
        out[name] = (out[name] * factor).astype(out[name].dtype)
    return out
```

```python
import math
from contextlib import ExitStack, contextmanager

import numpy as np
import concourse.bass as bass
from concourse import mybir

F32 = mybir.dt.float32
BF16 = mybir.dt.bfloat16
I32 = mybir.dt.int32
U32 = mybir.dt.uint32
ALU = mybir.AluOpType
ACT = mybir.ActivationFunctionType
AX = mybir.AxisListType

P = 128
T, D = 1024, 1024
NT, KT = T // P, D // P
C = 64
NC = T // C
NH = 4
GK = 64
PLE = 256
E, TOPK, FF = 32, 4, 1024
EPS = 1e-6
HALF = 512

C_GQK, C_GV, C_GR, C_GLR, C_QKV, C_DZ, C_DAB = 0, 512, 1024, 1536, 1552, 3088, 3600
NQKV = 12
TAPS = 4

CAP = 192
ROUNDS = -(-T // CAP)
Y_FIRST, Y_ROUND = (E + 1) * CAP, E * CAP
LEVELS = 6
K_ID, K_TRI, K_CHUNK, K_HALF, K_STRICT, K_ONES, K_LEVEL = 0, 128, 256, 384, 640, 768, 896
K_IOTA = K_LEVEL + LEVELS * P
K_TOK = K_IOTA + CAP
K_SLOT = K_TOK + 2 * NT
K_E = K_SLOT + E
K_END = K_E + E
R_MIX, R_PLE, R_BG, R_GLA, R_GDN, R_CONV = 0, 8, 16, 18, 19, 20
R_END = R_CONV + TAPS * NQKV


def constants():
    i = np.arange(P)
    same = (i[:, None] // C) == (i[None, :] // C)
    k = np.zeros((P, K_END), np.float32)
    k[:, K_ID:K_ID + P] = np.eye(P)
    k[:, K_TRI:K_TRI + P] = same & (i[:, None] <= i[None, :])
    k[:, K_CHUNK:K_CHUNK + P] = same
    for r in range(2):
        k[:, K_HALF + r * P:K_HALF + (r + 1) * P] = (i[:, None] // C) == r
    k[:, K_STRICT:K_STRICT + P] = i[:, None] < i[None, :]
    k[:, K_ONES:K_ONES + P] = 1.0
    for l in range(LEVELS):
        m = 1 << l
        block = (i[:, None] // (2 * m)) == (i[None, :] // (2 * m))
        k[:, K_LEVEL + l * P:K_LEVEL + (l + 1) * P] = block & (i[:, None] % (2 * m) < m) & (i[None, :] % (2 * m) >= m)
    k[:, K_IOTA:K_IOTA + CAP] = np.arange(CAP)
    for t in range(NT):
        k[:, K_TOK + 2 * t] = t * P
        k[:, K_TOK + 2 * t + 1] = i
    k[:, K_SLOT:K_SLOT + E] = (np.arange(E) + 1) * CAP
    k[:, K_E:K_E + E] = np.arange(E)
    return k


@contextmanager
def stage_signals(nc, stage):
    sems = []

    def sem(name):
        sems.append(nc.alloc_semaphore(name=f"{stage}_{name}"))
        return sems[-1]

    yield sem
    nc.clear_and_free_semaphores(sems)
    nc.all_engine_barrier()


def project(nc, g, sem):
    WAYS = [("gqk", j, h) for h in range(2) for j in range(4)] + [("glr", 0, h) for h in range(2)]
    WAYS += [("qkv", j, h) for j in range(NQKV) for h in range(2)] + [("dab", 0, 0)]
    WAYS += [(kind, 0, t) for kind in ("gv", "gr", "dz") for t in range(NT)]
    BANKS = 6
    CHUNK_COLS = [C_GQK, C_QKV, C_QKV + HALF, C_QKV + 2 * HALF, C_GV, C_GR, C_DZ]

    def chunk_of(kind, j):
        return {"gqk": 0, "qkv": 1 + j // 4, "gv": 4, "gr": 5, "dz": 6}.get(kind)

    last_unit = {}
    for u, (kind, j, _) in enumerate(WAYS):
        if chunk_of(kind, j) is not None:
            last_unit[chunk_of(kind, j)] = u
    act_units = [u for u, w in enumerate(WAYS) if w[0] not in ("gr", "dz")]
    dve_units = [u for u, w in enumerate(WAYS) if w[0] in ("gr", "dz")]

    with ExitStack() as ph:
        def sb(name, shape, dt=F32):
            return ph.enter_context(nc.sbuf_tensor(name, shape, dt))

        nT = sb("nT", [P, KT, T])
        w = sb("w_in_chunks", [P, 2, KT, HALF])
        w_small = sb("w_in_small", [P, KT, 24])
        work = sb("project_work", [P, 6, T + 4])
        par_rows = sb("par_rows", [R_END, P])
        stat = sb("norm_stat", [P, 3, NT])
        ps = ph.enter_context(nc.psum_tensor("project_psum", [P, 8, HALF], F32))

        x_in = [sem(f"x_in{i}") for i in range(2)]
        w_in_s = [sem(f"w_chunk{i}") for i in range(2)]
        small_in, consts_in, par_in = sem("w_small_in"), sem("consts_in"), sem("par_in")
        squared, mean_done, root_done, rs_done, scaled = (sem(n) for n in ("squared", "mean_done", "root_done", "rs_done", "scaled"))
        turned, norm_ready, par_turned, par_ready = (sem(n) for n in ("x_turned", "norm_ready", "par_turned", "par_ready"))
        unit_done, act_emptied, dve_emptied = sem("unit_done"), sem("act_emptied"), sem("dve_emptied")
        pad_ready, tap_done, sig_done, silu_done = (sem(n) for n in ("pad_ready", "tap_done", "conv_sigmoid", "silu_done"))
        sq_done, ss_done, l2_root, l2_inv, l2_done = (sem(n) for n in ("l2_squares", "l2_sums", "l2_root", "l2_inverse", "l2_done"))
        gate_sig, gate_out = sem("gate_sigmoid"), [sem(f"gate_out{i}") for i in range(2)]

        ident = g.k[:, K_ID:K_ID + P]
        xt = [work[:, i, 0:D] for i in range(2)]
        xs = [work[:, 2 + i, 0:D] for i in range(2)]
        junk = work[:, 4, 0:D]
        raw = [work[:, i, :] for i in range(2)]
        acc = [work[:, 2 + i, 0:T] for i in range(2)]
        sg = work[:, 4, 0:T]
        sq = [work[:, 5, 0:T], work[:, 4, 0:T]]
        rt = [work[:, 2, 0:T], work[:, 3, 0:T]]
        gate = [work[:, i, 0:HALF] for i in range(2)]
        gsig = [work[:, i, HALF:2 * HALF] for i in range(2)]
        w_dram = g.w_in.rearrange("(k p) n -> p k n", p=P)
        x_dram = g.x.rearrange("(t p) d -> t p d", p=P)
        block = ph.enter_context(nc.Block())

        @block.sync
        def _(sp):
            def chunk(c):
                if c >= 2:
                    sp.wait_ge(unit_done, last_unit[c - 2] + 1)
                sp.dma_start(w[:, c % 2], w_dram[:, :, CHUNK_COLS[c]:CHUNK_COLS[c] + HALF]).then_inc(w_in_s[c % 2], 16)

            def x_tile(t):
                if t >= 2:
                    sp.wait_ge(squared, t - 1)
                    sp.wait_ge(scaled, t - 1)
                sp.dma_start(xt[t % 2], x_dram[t]).then_inc(x_in[t % 2], 16)

            sp.dma_start(g.k[:], g.consts).then_inc(consts_in, 16)
            x_tile(0)
            x_tile(1)
            for (row, src, n) in ((R_MIX, g.g_mix, 8), (R_PLE, g.g_ple_in, 8), (R_BG, g.b_gla_gate, 2), (R_GLA, g.g_gla_out, 1),
                                  (R_GDN, g.g_gdn_out, 1), (R_CONV, g.w_conv, TAPS * NQKV)):
                sp.dma_start(par_rows[row:row + n, :], src.rearrange("a (r p) -> (a r) p", p=P)).then_inc(par_in, 16)
            chunk(0)
            for t in range(2, NT):
                x_tile(t)
            with nc.allow_non_contiguous_dma(reason="24 narrow columns of w_in"):
                sp.dma_start(w_small[:, :, 0:16], w_dram[:, :, C_GLR:C_GLR + 16]).then_inc(small_in, 16)
                sp.dma_start(w_small[:, :, 16:24], w_dram[:, :, C_DAB:C_DAB + 8]).then_inc(small_in, 16)
            for c in range(1, 7):
                chunk(c)

        @block.gpsimd
        def _(pool):
            for n, u in enumerate(dve_units):
                kind, _, t = WAYS[u]
                pool.wait_ge(dve_emptied, n + 1)
                dst = g.gates_dram[0 if kind == "gr" else 1].rearrange("(t p) d -> t p d", p=P)[t]
                pool.dma_start(dst, gate[n % 2]).then_inc(gate_out[n % 2], 16)
            for s in gate_out:
                pool.wait_ge(s, 16 * NT)

        @block.tensor
        def _(pe):
            def turn_tile(t):
                pe.wait_ge(scaled, t + 1)
                for q in range(2):
                    n = 2 * t + q
                    if n >= 2:
                        pe.wait_ge(norm_ready, n - 1)
                    for i in range(4):
                        k = 4 * q + i
                        mm = pe.transpose(ps[:, q, i * P:(i + 1) * P], xs[t % 2][:, k * P:(k + 1) * P], ident)
                    mm.then_inc(turned, 1)

            def unit(u):
                kind, j, part = WAYS[u]
                bank = 2 + u % BANKS
                if u >= BANKS:
                    before = u - BANKS
                    if before in act_units:
                        pe.wait_ge(act_emptied, act_units.index(before) + 1)
                    else:
                        pe.wait_ge(dve_emptied, dve_units.index(before) + 1)
                c = chunk_of(kind, j)
                if c is not None:
                    pe.wait_ge(w_in_s[c % 2], 16 * (c // 2 + 1))
                else:
                    pe.wait_ge(small_in, 32)
                if kind in ("gqk", "glr", "qkv"):
                    pe.wait_ge(norm_ready, 8 * (part + 1))
                    M = 16 if kind == "glr" else P
                    for k in range(KT):
                        lhs = w_small[:, k, 0:16] if kind == "glr" else w[:, c % 2, k, (j % 4) * P:(j % 4 + 1) * P]
                        mm = pe.matmul(ps[0:M, bank, :], lhs, nT[:, k, part * HALF:(part + 1) * HALF],
                                       start=(k == 0), stop=(k == KT - 1))
                elif kind == "dab":
                    for t in range(NT):
                        for k in range(KT):
                            mm = pe.matmul(ps[:, bank, 8 * t:8 * t + 8], nT[:, k, t * P:(t + 1) * P], w_small[:, k, 16:24],
                                           start=(k == 0), stop=(k == KT - 1))
                else:
                    for k in range(KT):
                        mm = pe.matmul(ps[:, bank, :], nT[:, k, part * P:(part + 1) * P], w[:, c % 2, k, :],
                                       start=(k == 0), stop=(k == KT - 1))
                mm.then_inc(unit_done, 1)

            def l2_sums(j):
                pe.wait_ge(sq_done, j + 1)
                for h in range(2):
                    if j >= 1:
                        pe.wait_ge(l2_root, 2 * (j - 1) + h + 1)
                    pe.matmul(ps[:, h, :], g.k[:, K_ONES:K_ONES + P], sq[j % 2][:, h * HALF:(h + 1) * HALF],
                              start=True, stop=True).then_inc(ss_done, 1)

            pe.wait_ge(consts_in, 16)
            pe.wait_ge(par_in, 16 * 6)
            pe.transpose(ps[:, 2, 0:R_END], par_rows[:], g.k[0:R_END, K_ID:K_ID + R_END]).then_inc(par_turned, 1)
            for t in range(4):
                turn_tile(t)
            pe.wait_ge(par_ready, 1)
            for u in range(4):
                unit(u)
            for t in range(4, NT):
                turn_tile(t)
            first_gv = WAYS.index(("gv", 0, 0))
            for u in range(4, len(WAYS)):
                unit(u)
                if first_gv + 2 <= u < first_gv + 10:
                    l2_sums(u - first_gv - 2)

        @block.scalar
        def _(act):
            for t in range(NT):
                act.wait_ge(x_in[t % 2], 16 * (t // 2 + 1))
                act.activation(junk, xt[t % 2], ACT.Square, accum_out=stat[:, 0, t:t + 1]).then_inc(squared, 1)
                act.wait_ge(mean_done, t + 1)
                act.activation(stat[:, 1, t:t + 1], stat[:, 2, t:t + 1], ACT.Sqrt).then_inc(root_done, 1)

            def l2_square(j):
                act.wait_ge(silu_done, j + 1)
                act.wait_ge(silu_done, NQKV)
                if j >= 2:
                    act.wait_ge(ss_done, 2 * (j - 1))
                act.activation(sq[j % 2], g.qkvT[:, j, :], ACT.Square).then_inc(sq_done, 1)

            def l2_roots(j):
                if j >= 2:
                    act.wait_ge(l2_done, j - 1)
                for h in range(2):
                    act.wait_ge(ss_done, 2 * j + h + 1)
                    act.activation(rt[j % 2][:, h * HALF:(h + 1) * HALF], ps[:, h, :], ACT.Sqrt,
                                   bias=g.eps[:, 0:1]).then_inc(l2_root, 1)

            def conv_sigmoid(j):
                act.wait_ge(tap_done, TAPS * (j + 1))
                if j >= 1:
                    act.wait_ge(silu_done, j)
                act.activation(sg, acc[j % 2], ACT.Sigmoid).then_inc(sig_done, 1)

            act.wait_ge(g.setup_done, 1)
            gates = 0
            for u, (kind, j, part) in enumerate(WAYS):
                bank = 2 + u % BANKS
                src = ps[:, bank, :]
                act.wait_ge(unit_done, u + 1)
                cols = slice(part * HALF, (part + 1) * HALF)
                if kind == "gqk":
                    act.activation(g.gqkT[:, j, cols], src, ACT.Copy,
                                   scale=GK ** -0.5 if j < 2 else 1.0).then_inc(act_emptied, 1)
                elif kind == "glr":
                    act.copy(g.glrT[:, cols], ps[0:16, bank, :]).then_inc(act_emptied, 1)
                elif kind == "qkv":
                    if part == 0:
                        if j >= 2:
                            act.wait_ge(tap_done, TAPS * (j - 1))
                        else:
                            act.wait_ge(pad_ready, 2)
                    act.copy(raw[j % 2][:, 3 + part * HALF:3 + (part + 1) * HALF], src).then_inc(act_emptied, 1)
                    if part == 0 and j >= 1:
                        conv_sigmoid(j - 1)
                elif kind == "dab":
                    act.copy(g.dab[:], ps[:, bank, 0:8 * NT].rearrange("p (t c) -> p t c", t=NT)).then_inc(act_emptied, 1)
                    conv_sigmoid(NQKV - 1)
                    l2_square(0)
                    l2_square(1)
                elif kind == "gv":
                    act.copy(g.gv[:, part, :], src).then_inc(act_emptied, 1)
                    if part >= 2:
                        l2_roots(part - 2)
                        l2_square(part)
                else:
                    if kind == "gr" and part < 2:
                        l2_roots(part + 6)
                    if gates >= 2:
                        act.wait_ge(dve_emptied, gates - 1)
                    act.activation(gsig[gates % 2], src, ACT.Sigmoid).then_inc(gate_sig, 1)
                    gates += 1

        @block.vector
        def _(dve):
            dve.memset(g.eps[:], EPS).then_inc(g.setup_done, 1)
            for t in range(NT):
                dve.wait_ge(squared, t + 1)
                dve.tensor_scalar(stat[:, 2, t:t + 1], stat[:, 0, t:t + 1], 1.0 / D, EPS, ALU.mult, ALU.add).then_inc(mean_done, 1)
                dve.wait_ge(root_done, t + 1)
                dve.reciprocal(stat[:, 1, t:t + 1], stat[:, 1, t:t + 1]).then_inc(rs_done, 1)
                dve.wait_ge(rs_done, t + 1)
                if t >= 2:
                    dve.wait_ge(turned, 2 * (t - 1))
                dve.tensor_scalar(xs[t % 2], xt[t % 2], stat[:, 1, t:t + 1], None, ALU.mult).then_inc(scaled, 1)
                if t == 0:
                    dve.wait_ge(par_turned, 1)
                    dve.tensor_copy(g.par[:], ps[:, 2, 0:R_END]).then_inc(par_ready, 1)
                    dve.wait_ge(par_ready, 1)
                for q in range(2):
                    dve.wait_ge(turned, 2 * t + q + 1)
                    dve.tensor_tensor(nT[:, 4 * q:4 * q + 4, t * P:(t + 1) * P], ps[:, q, :].rearrange("p (k c) -> p k c", k=4),
                                      g.par[:, R_MIX + 4 * q:R_MIX + 4 * q + 4].unsqueeze(2).to_broadcast([P, 4, P]),
                                      ALU.mult).then_inc(norm_ready, 1)

            for i in range(2):
                dve.memset(raw[i][:, 0:3], 0.0).then_inc(pad_ready, 1)
            for j in range(NQKV):
                for tap in range(TAPS):
                    col = g.par[:, R_CONV + tap * NQKV + j:R_CONV + tap * NQKV + j + 1]
                    seen = raw[j % 2][:, tap:tap + T]
                    if tap == 0:
                        dve.wait_ge(act_emptied, act_units.index(WAYS.index(("qkv", j, 1))) + 1)
                        dve.tensor_scalar(acc[j % 2], seen, col, None, ALU.mult).then_inc(tap_done, 1)
                    else:
                        dve.wait_ge(tap_done, TAPS * j + tap)
                        dve.scalar_tensor_tensor(out=acc[j % 2], in0=seen, scalar=col, in1=acc[j % 2],
                                                 op0=ALU.mult, op1=ALU.add).then_inc(tap_done, 1)
                dve.wait_ge(sig_done, j + 1)
                dve.tensor_tensor(g.qkvT[:, j, :], acc[j % 2], sg, ALU.mult).then_inc(silu_done, 1)

            def l2_scale(j):
                dve.wait_ge(l2_root, 2 * (j + 1))
                dve.reciprocal(rt[j % 2], rt[j % 2]).then_inc(l2_inv, 1)
                dve.wait_ge(l2_inv, j + 1)
                dve.scalar_tensor_tensor(out=g.qkvT[:, j, :], in0=g.qkvT[:, j, :], scalar=P ** -0.5 if j < NH else 1.0,
                                         in1=rt[j % 2], op0=ALU.mult, op1=ALU.mult).then_inc(l2_done, 1)

            def gate_product(n):
                u = dve_units[n]
                dve.wait_ge(gate_sig, n + 1)
                if n >= 2:
                    dve.wait_ge(gate_out[n % 2], 16 * (n // 2))
                dve.tensor_tensor(gate[n % 2], ps[:, 2 + u % BANKS, :], gsig[n % 2], ALU.mult).then_inc(dve_emptied, 1)

            for j in range(6):
                l2_scale(j)
            for n in range(2 * NT):
                if n < 2:
                    l2_scale(6 + n)
                gate_product(n)


def gla(nc, g, sem):
    SLOTS = 4 * 2
    STEPS = [("diag", p) for p in range(2)] + [(l, p) for l in range(LEVELS) for p in range(2)]

    with ExitStack() as ph:
        def sb(name, shape, dt=F32):
            return ph.enter_context(nc.sbuf_tensor(name, shape, dt))

        w_gate = sb("w_gla_gate", [16, 2 * P])
        b = sb("gla_b", [P, 2, T])
        A = sb("gla_scores", [P, NH, NT, P])
        dist = sb("gla_dist", [P, 2, T])
        Q = sb("gla_q_level", [P, 2, T])
        K = sb("gla_k_level", [P, 2, T])
        qe = sb("gla_q_decayed", [P, NH, T])
        kdn = sb("gla_k_decayed", [P, NT, 2 * P])
        S = sb("gla_states", [P, 2, NC, P])
        dec = sb("gla_chunk_decay", [P, 2, NC])
        stat = sb("gla_stat", [P, 2, NT, NH])
        gate = sb("gla_gate_in", [P, 2, HALF])
        on = sb("gla_out_normed", [P, 2, HALF])
        one = sb("gla_one", [P, 1])
        ps = ph.enter_context(nc.psum_tensor("gla_psum", [P, 8, HALF], F32))

        wg_in, gate_in = sem("w_gate_in"), [sem(f"gate_in{i}") for i in range(2)]
        prep, pre, act_pre, low, logs, run_sum = sem("prepared"), sem("gate_product"), sem("act_softplus"), sem("low"), sem("logs"), sem("running_sum")
        zeroed, dist_done, decay_done, q_done, k_done = sem("zeroed"), sem("distance"), sem("level_decay"), sem("q_level"), sem("k_level")
        score_done, kept = sem("scores"), sem("scores_kept")
        edge_exp, chunk_exp, qe_done, last_dist, kd_done = sem("edge_exp"), sem("chunk_exp"), sem("q_decayed"), sem("last_dist"), sem("k_decayed")
        k_turned, k_natural, added, state_done = sem("k_turned"), sem("k_natural"), sem("state_added"), sem("state_done")
        out_done, squares, roots, inverses, normed, o_turned, o_kept = (sem(n) for n in ("out", "out_squares", "out_roots", "out_inverse", "out_normed", "out_turned", "out_kept"))

        ident = g.k[:, K_ID:K_ID + P]
        block = ph.enter_context(nc.Block())

        def bank_of(step, half, parity):
            return 4 * (step % 2) + 2 * half + parity

        @block.sync
        def _(sp):
            sp.dma_start(w_gate[:], g.w_gla_gate.rearrange("a k n -> (a k) n")).then_inc(wg_in, 16)
            for t in range(NT):
                if t >= 2:
                    sp.wait_ge(normed, NH * (t - 1))
                sp.dma_start(gate[:, t % 2, :], g.gates_dram[0].rearrange("(t p) d -> t p d", p=P)[t]).then_inc(gate_in[t % 2], 16)

        @block.gpsimd
        def _(pool):
            pool.memset(A[:], 0.0).then_inc(zeroed, 1)
            pool.memset(qe[:], 0.0).then_inc(zeroed, 1)
            pool.memset(S[:, :, 0, :], 0.0).then_inc(zeroed, 1)
            for n in range(2, len(STEPS)):
                level, p = STEPS[n]
                pool.wait_ge(decay_done, n - 1)
                if n >= 4:
                    pool.wait_ge(score_done, 4 * (n - 1))
                pool.tensor_tensor(K[:, n % 2, :], g.gqkT[:, 2 + p, :], dist[:, n % 2, :], ALU.mult).then_inc(k_done, 1)

        @block.tensor
        def _(pe):
            pe.wait_ge(wg_in, 16)
            for p in range(2):
                for h in range(2):
                    pe.matmul(ps[:, 2 * p + h, :], w_gate[:, p * P:(p + 1) * P], g.glrT[:, h * HALF:(h + 1) * HALF],
                              start=True, stop=True).then_inc(pre, 1)
            for n, (level, p) in enumerate(STEPS):
                if n == 0:
                    pe.wait_ge(logs, 2)
                    pe.wait_ge(low, 2)
                if n >= 2:
                    pe.wait_ge(q_done, n - 1)
                    pe.wait_ge(k_done, n - 1)
                    pe.wait_ge(kept, 4 * (n - 1))
                for half in range(2):
                    for parity in range(2):
                        rows = slice(GK * parity, GK * (parity + 1))
                        for i in range(4):
                            t = 4 * half + i
                            cols = slice(t * P, (t + 1) * P)
                            kk, qq = (g.gqkT[rows, 2 + p, cols], g.gqkT[rows, p, cols]) if level == "diag" else (K[rows, n % 2, cols], Q[rows, n % 2, cols])
                            mm = pe.matmul(ps[:, bank_of(n, half, parity), i * P:(i + 1) * P], kk, qq, start=True, stop=True)
                        mm.then_inc(score_done, 1)
            for q in range(4):
                p, half = q // 2, q % 2
                pe.wait_ge(kd_done, p + 1)
                pe.wait_ge(kept, 4 * len(STEPS))
                for i in range(4):
                    t = 4 * half + i
                    mm = pe.transpose(ps[:, q, i * P:(i + 1) * P], K[:, p, t * P:(t + 1) * P], ident)
                mm.then_inc(k_turned, 1)
            for c in range(NC - 1):
                t, r = c // 2, c % 2
                rows = slice(C * r, C * (r + 1))
                if c == 0:
                    pe.wait_ge(k_natural, 4)
                if c >= 4:
                    pe.wait_ge(state_done, 2 * (c - 3))
                for h in range(NH):
                    p, e = h // 2, h % 2
                    mm = pe.matmul(ps[GK * e:GK * (e + 1), c % 4, p * P:(p + 1) * P], kdn[rows, t, p * P + GK * e:p * P + GK * (e + 1)],
                                   g.gv[rows, t, h * P:(h + 1) * P], start=True, stop=True)
                mm.then_inc(added, 1)

            def turn_out(t):
                pe.wait_ge(normed, NH * (t + 1))
                if t >= 2:
                    pe.wait_ge(o_kept, t - 1)
                for h in range(NH):
                    mm = pe.transpose(ps[:, 6 + t % 2, h * P:(h + 1) * P], on[:, t % 2, h * P:(h + 1) * P], ident)
                mm.then_inc(o_turned, 1)

            for t in range(NT):
                if t >= 1:
                    pe.wait_ge(state_done, 2 * min(2 * t + 1, NC - 1))
                else:
                    pe.wait_ge(state_done, 2)
                    pe.wait_ge(qe_done, 4)
                if t >= 2:
                    pe.wait_ge(normed, NH * (t - 1))
                bank = 4 + t % 2
                for h in range(NH):
                    pe.matmul(ps[:, bank, h * P:(h + 1) * P], A[:, h, t, :], g.gv[:, t, h * P:(h + 1) * P],
                              start=(h == 0), stop=False, skip_group_check=True)
                    for r in range(2):
                        mm = pe.matmul(ps[C * r:C * (r + 1), bank, h * P:(h + 1) * P], qe[:, h, t * P + C * r:t * P + C * (r + 1)],
                                       S[:, h // 2, 2 * t + r, :], start=False, stop=(h == NH - 1), skip_group_check=True)
                mm.then_inc(out_done, 1)
                if t >= 1:
                    turn_out(t - 1)
            turn_out(NT - 1)

        @block.scalar
        def _(act):
            act.wait_ge(prep, 1)
            for p in range(2):
                act.wait_ge(pre, 2 * p + 2)
                src = ps[:, 2 * p:2 * p + 2, :].rearrange("p a c -> p (a c)")
                act.activation(dist[:, p, :], src, ACT.Abs, bias=g.par[:, R_BG + p:R_BG + p + 1]).then_inc(act_pre, 1)
                act.wait_ge(act_pre, 3 * p + 1)
                act.activation(dist[:, p, :], dist[:, p, :], ACT.Exp, scale=-1.0).then_inc(act_pre, 1)
                act.wait_ge(act_pre, 3 * p + 2)
                act.activation(dist[:, p, :], dist[:, p, :], ACT.Ln, bias=one[:, 0:1]).then_inc(act_pre, 1)
                act.wait_ge(act_pre, 3 * p + 3)
            for n in range(2, len(STEPS)):
                act.wait_ge(dist_done, n - 1)
                act.activation(dist[:, n % 2, :], dist[:, n % 2, :], ACT.Abs).then_inc(edge_exp, 1)
                act.wait_ge(edge_exp, n - 1)
                act.activation(dist[:, n % 2, :], dist[:, n % 2, :], ACT.Exp, scale=-1.0 / 16).then_inc(decay_done, 1)
            act.wait_ge(q_done, len(STEPS) - 2)
            act.wait_ge(k_done, len(STEPS) - 2)
            for p in range(2):
                act.activation(dist[:, p, :], b[:, p, :], ACT.Exp, scale=1.0 / 16).then_inc(chunk_exp, 1)
            act.activation(dec[:], b[:].rearrange("p a (c i) -> p a c i", i=C)[:, :, :, C - 1], ACT.Exp, scale=1.0 / 16).then_inc(chunk_exp, 1)
            for p in range(2):
                act.wait_ge(last_dist, p + 1)
                act.activation(Q[:, p, :], Q[:, p, :], ACT.Exp, scale=1.0 / 16).then_inc(chunk_exp, 1)
            for t in range(NT):
                act.wait_ge(out_done, t + 1)
                for h in range(NH):
                    act.activation(dist[:, 0, h * P:(h + 1) * P], ps[:, 4 + t % 2, h * P:(h + 1) * P], ACT.Square,
                                   accum_out=stat[:, 0, t, h:h + 1]).then_inc(squares, 1)
                act.wait_ge(squares, NH * (t + 1))
                act.activation(stat[:, 1, t, :], stat[:, 0, t, :], ACT.Sqrt, scale=1.0 / P, bias=g.eps[:, 0:1]).then_inc(roots, 1)
                if t >= 1:
                    act.wait_ge(o_turned, t)
                    act.activation(g.mixA[:, :, (t - 1) * P:t * P], ps[:, 6 + (t - 1) % 2, :].rearrange("p (h c) -> p h c", h=NH),
                                   ACT.Copy, scale=g.par[:, R_GLA:R_GLA + 1]).then_inc(o_kept, 1)
            act.wait_ge(o_turned, NT)
            act.activation(g.mixA[:, :, (NT - 1) * P:T], ps[:, 6 + (NT - 1) % 2, :].rearrange("p (h c) -> p h c", h=NH),
                           ACT.Copy, scale=g.par[:, R_GLA:R_GLA + 1]).then_inc(o_kept, 1)

        @block.vector
        def _(dve):
            reset = K[:, 0, :]
            dve.memset(one[:], 1.0).then_inc(prep, 1)
            dve.memset(reset, 1.0).then_inc(prep, 1)
            dve.wait_ge(prep, 2)
            dve.memset(reset.rearrange("p (c i) -> p c i", i=C)[:, :, 0:1], 0.0).then_inc(prep, 1)
            for p in range(2):
                dve.wait_ge(act_pre, 3 * p + 3)
                src = ps[:, 2 * p:2 * p + 2, :].rearrange("p a c -> p (a c)")
                dve.tensor_scalar(Q[:, p, :], src, g.par[:, R_BG + p:R_BG + p + 1], 0.0, ALU.add, ALU.min).then_inc(low, 1)
                dve.wait_ge(low, p + 1)
                dve.tensor_tensor(Q[:, p, :], Q[:, p, :], dist[:, p, :], ALU.subtract).then_inc(logs, 1)
                dve.wait_ge(logs, p + 1)
                dve.wait_ge(prep, 3)
                dve.tensor_tensor_scan(b[:, p, :], reset, Q[:, p, :], 0.0, ALU.mult, ALU.add).then_inc(run_sum, 1)
            dve.wait_ge(run_sum, 2)
            dve.wait_ge(zeroed, 3)

            def distance(n):
                level, p = STEPS[n]
                m = 1 << level
                v = b[:, p, :].rearrange("p (a i) -> p a i", i=2 * m)
                if n >= 4:
                    dve.wait_ge(q_done, n - 3)
                    dve.wait_ge(k_done, n - 3)
                dve.tensor_tensor(dist[:, n % 2, :].rearrange("p (a i) -> p a i", i=2 * m), v,
                                  v[:, :, m - 1:m].to_broadcast([P, T // (2 * m), 2 * m]), ALU.subtract).then_inc(dist_done, 1)

            def q_level(n):
                level, p = STEPS[n]
                dve.wait_ge(decay_done, n - 1)
                if n >= 4:
                    dve.wait_ge(score_done, 4 * (n - 1))
                dve.tensor_tensor(Q[:, n % 2, :], g.gqkT[:, p, :], dist[:, n % 2, :], ALU.mult).then_inc(q_done, 1)

            def keep(n):
                level, p = STEPS[n]
                mask = g.k[:, K_ID:K_ID + P] if level == "diag" else g.k[:, K_LEVEL + level * P:K_LEVEL + (level + 1) * P]
                for half in range(2):
                    for parity in range(2):
                        dve.wait_ge(score_done, 4 * n + 2 * half + parity + 1)
                        dve.copy_predicated(A[:, 2 * p + parity, 4 * half:4 * half + 4, :],
                                            mask.bitcast(I32).unsqueeze(1).to_broadcast([P, 4, P]),
                                            ps[:, bank_of(n, half, parity), :].rearrange("p (t c) -> p t c", t=4)).then_inc(kept, 1)

            distance(2)
            distance(3)
            for n in range(len(STEPS)):
                keep(n)
                if n + 2 < len(STEPS):
                    q_level(n + 2)
                if n + 4 < len(STEPS):
                    distance(n + 4)
            for p in range(2):
                dve.wait_ge(chunk_exp, p + 1)
                for e in range(2):
                    rows = slice(GK * e, GK * (e + 1))
                    dve.tensor_tensor(qe[rows, 2 * p + e, :], g.gqkT[rows, p, :], dist[rows, p, :], ALU.mult).then_inc(qe_done, 1)
                v = b[:, p, :].rearrange("p (a i) -> p a i", i=C)
                dve.wait_ge(score_done, 4 * len(STEPS))
                dve.tensor_tensor(Q[:, p, :].rearrange("p (a i) -> p a i", i=C), v[:, :, C - 1:C].to_broadcast([P, NC, C]), v,
                                  ALU.subtract).then_inc(last_dist, 1)
            for p in range(2):
                dve.wait_ge(chunk_exp, 4 + p)
                dve.tensor_tensor(K[:, p, :], g.gqkT[:, 2 + p, :], Q[:, p, :], ALU.mult).then_inc(kd_done, 1)
            for q in range(4):
                p, half = q // 2, q % 2
                dve.wait_ge(k_turned, q + 1)
                dve.tensor_copy(kdn[:, 4 * half:4 * half + 4, p * P:(p + 1) * P], ps[:, q, :].rearrange("p (t c) -> p t c", t=4)).then_inc(k_natural, 1)
            for c in range(NC - 1):
                dve.wait_ge(added, c + 1)
                if c >= 1:
                    dve.wait_ge(state_done, 2 * c)
                for p in range(2):
                    dve.scalar_tensor_tensor(out=S[:, p, c + 1, :], in0=S[:, p, c, :], scalar=dec[:, p, c:c + 1],
                                             in1=ps[:, c % 4, p * P:(p + 1) * P], op0=ALU.mult, op1=ALU.add).then_inc(state_done, 1)
            for t in range(NT):
                dve.wait_ge(roots, t + 1)
                dve.reciprocal(stat[:, 1, t, :], stat[:, 1, t, :]).then_inc(inverses, 1)
                dve.wait_ge(inverses, t + 1)
                dve.wait_ge(gate_in[t % 2], 16 * (t // 2 + 1))
                if t >= 2:
                    dve.wait_ge(o_turned, t - 1)
                for h in range(NH):
                    cols = slice(h * P, (h + 1) * P)
                    dve.scalar_tensor_tensor(out=on[:, t % 2, cols], in0=ps[:, 4 + t % 2, cols], scalar=stat[:, 1, t, h:h + 1],
                                             in1=gate[:, t % 2, cols], op0=ALU.mult, op1=ALU.mult).then_inc(normed, 1)


def delta(nc, g, sem):
    with ExitStack() as ph:
        def sb(name, shape, dt=F32):
            return ph.enter_context(nc.sbuf_tensor("dn_" + name, shape, dt))

        G = NH * P
        E_ = sb("pair_decay", [P, NT, G])
        LT = sb("lower_T", [P, NT, G])
        inv_T = sb("inv_T", [P, NT, G])
        inv = sb("inv", [P, NT, G])
        aqk = sb("scores_T", [P, NT, G])
        bk = sb("beta_k", [P, NT, G])
        tmp = sb("tmp", [P, 6, G])
        small = sb("small", [P, 10, NT, NH])
        S = sb("state", [P, 2, G])
        stat = sb("stat", [P, 2, NT, NH])
        decS = sb("chunk_decay", [P, 2, NT, NH])
        par = sb("head_parameters", [P, 2, NH])
        one = sb("one", [P, 1])
        ps = ph.enter_context(nc.psum_tensor("dn_psum", [P, 8, HALF], F32))
        wT, u = E_, LT
        Y, Ybeta, GN, BETA, BN, EBN, KDS, BKE, SP, AB = range(10)
        ident, tri = g.k[:, K_ID:K_ID + P], g.k[:, K_TRI:K_TRI + P]

        def heads(ap):
            return ap.rearrange("p (h c) -> p h c", h=NH)

        def over(ap):
            return ap.unsqueeze(2).to_broadcast([P, NH, P])

        par_in, gate_in = sem("par_in"), [sem(f"gate_in{i}") for i in range(2)]
        one_set, y_ready, soft, gn_ready, sums, small_ready, small_exp, bke_ready = (sem(n) for n in (
            "one_set", "y_ready", "softplus", "log_decay", "sums", "sums_kept", "sums_exp", "beta_decay"))
        scaled, rows_done, kq_done, kv_turned = sem("scaled_triangles"), sem("rows"), sem("kk_qk"), sem("kv_turned")
        row_exp, apart, pair_exp, prod, masked, qd_done, nat_done, v_done = (sem(n) for n in (
            "row_exp", "apart", "pair_exp", "products", "scores_masked", "q_decayed", "k_natural", "v_natural"))
        cut0, inv0, first_turned, first_kept = sem("first_cut"), sem("inv_T_first"), sem("first_turned"), sem("first_kept")
        cut, x_done, x_kept, z_done, z_used, t_done, t_kept = (sem(n) for n in (
            "cut", "x_done", "x_kept", "z_done", "z_used", "inv_turned", "inv_kept"))
        sol_done, w_kept, u_kept = sem("sol_done"), sem("w_kept"), sem("u_kept")
        s_zero, ws_done, delta_done, upd_done, s_decayed, s_done = (sem(n) for n in (
            "state_zero", "ws_done", "delta", "update", "state_decayed", "state"))
        out_done, squares, roots, inverses, normed, o_turned, o_kept = (sem(n) for n in (
            "out", "out_squares", "out_roots", "out_inverse", "out_normed", "out_turned", "out_kept"))
        ROWS, BROW, KK, QK, KN, VN, TURN = 0, 1, 2, 3, 4, 5, 6
        STEPS = [(l, t) for l in range(1, LEVELS) for t in range(NT)]
        NORM_GATE, NORM_ON = [4, 5], [2, 3]
        block = ph.enter_context(nc.Block())

        @block.sync
        def _(sp):
            sp.dma_start(par[:, 0, :], g.gdn_a_log.rearrange("a h -> (a h)").partition_broadcast(P)).then_inc(par_in, 16)
            sp.dma_start(par[:, 1, :], g.gdn_dt_bias.rearrange("a h -> (a h)").partition_broadcast(P)).then_inc(par_in, 16)
            sp.wait_ge(w_kept, NT)
            for t in range(NT):
                if t >= 2:
                    sp.wait_ge(normed, NH * (t - 1))
                sp.dma_start(tmp[:, NORM_GATE[t % 2], :], g.gates_dram[1].rearrange("(t p) d -> t p d", p=P)[t]).then_inc(gate_in[t % 2], 16)

        @block.gpsimd
        def _(pool):
            pool.memset(S[:, 0, :], 0.0).then_inc(s_zero, 1)
            for t in range(NT):
                pool.wait_ge(prod, 3 * (t + 1))
                pool.tensor_tensor(heads(aqk[:, t, :]), heads(aqk[:, t, :]), tri.unsqueeze(1).to_broadcast([P, NH, P]), ALU.mult).then_inc(masked, 1)
            for s, (l, t) in enumerate(STEPS):
                if s == 0:
                    pool.wait_ge(cut0, NT)
                    pool.wait_ge(inv0, NT)
                if s >= 2:
                    pool.wait_ge(x_done, s - 1)
                mask = g.k[:, K_LEVEL + l * P:K_LEVEL + (l + 1) * P]
                pool.tensor_tensor(heads(tmp[:, s % 2, :]), heads(LT[:, t, :]), mask.unsqueeze(1).to_broadcast([P, NH, P]), ALU.mult).then_inc(cut, 1)

        @block.tensor
        def _(pe):
            def mm4(bank, lhs, rhs, **kw):
                for h in range(NH):
                    mm = pe.matmul(ps[:, bank, h * P:(h + 1) * P], lhs(h), rhs(h), start=True, stop=True)
                return mm

            pe.wait_ge(gn_ready, 1)
            gn = small[:, GN, :, :].rearrange("p t h -> p (t h)")
            for i, col in enumerate((K_TRI, K_CHUNK, K_HALF, K_HALF + P)):
                pe.matmul(ps[:, 7, 32 * i:32 * i + 32], g.k[:, col:col + P], gn, start=True, stop=True).then_inc(sums, 1)
            ones = g.k[:, K_ONES:K_ONES + P]
            for t in range(NT):
                cols = slice(t * P, (t + 1) * P)
                pe.wait_ge(scaled, 2 * t + 2)
                if t >= 1:
                    pe.wait_ge(prod, 3 * t)
                    pe.wait_ge(row_exp, t)
                    pe.wait_ge(apart, NH * t)
                pe.matmul(ps[:, ROWS, :], ones, tmp[:, 0, :], start=True, stop=True).then_inc(rows_done, 1)
                pe.matmul(ps[:, BROW, :], ones, tmp[:, 1, :], start=True, stop=True).then_inc(rows_done, 1)
                mm4(KK, lambda h: g.qkvT[:, NH + h, cols], lambda h: g.qkvT[:, NH + h, cols]).then_inc(kq_done, 1)
                mm4(QK, lambda h: g.qkvT[:, NH + h, cols], lambda h: g.qkvT[:, h, cols]).then_inc(kq_done, 1)
                if t >= 1:
                    pe.wait_ge(nat_done, 2 * t)
                    pe.wait_ge(v_done, NH * t)
                for bank, at in ((KN, NH), (VN, 2 * NH)):
                    for h in range(NH):
                        mm = pe.transpose(ps[:, bank, h * P:(h + 1) * P], g.qkvT[:, at + h, cols], ident)
                    mm.then_inc(kv_turned, 1)
            for t in range(NT):
                pe.wait_ge(inv0, t + 1)
                if t >= 1:
                    pe.wait_ge(first_kept, t)
                for h in range(NH):
                    mm = pe.transpose(ps[:, TURN, h * P:(h + 1) * P], inv_T[:, t, h * P:(h + 1) * P], ident)
                mm.then_inc(first_turned, 1)

            def part(ap, h):
                return ap[:, h * P:(h + 1) * P]

            N = len(STEPS)
            for s in range(N + 2):
                if s < N:
                    l, t = STEPS[s]
                    pe.wait_ge(cut, s + 1)
                    if s < NT:
                        pe.wait_ge(first_kept, t + 1)
                    else:
                        pe.wait_ge(t_kept, s - NT + 1)
                    if s >= 2:
                        pe.wait_ge(x_kept, s - 1)
                    mm4(s % 2, lambda h: part(tmp[:, s % 2, :], h), lambda h: part(inv[:, t, :], h)).then_inc(x_done, 1)
                if 1 <= s <= N:
                    q = s - 1
                    l, t = STEPS[q]
                    pe.wait_ge(x_kept, q + 1)
                    if q >= 2:
                        pe.wait_ge(z_used, q - 1)
                    mm4(2 + q % 2, lambda h: part(tmp[:, 2 + q % 2, :], h), lambda h: part(inv_T[:, t, :], h)).then_inc(z_done, 1)
                if s >= 2 and STEPS[s - 2][0] < LEVELS - 1:
                    q = s - 2
                    l, t = STEPS[q]
                    pe.wait_ge(z_used, q + 1)
                    if q >= 2:
                        pe.wait_ge(t_kept, q - 1)
                    for h in range(NH):
                        mm = pe.transpose(ps[:, 4 + q % 2, h * P:(h + 1) * P], part(inv_T[:, t, :], h), ident)
                    mm.then_inc(t_done, 1)
            for t in range(NT):
                cols = slice(t * P, (t + 1) * P)
                if t == 0:
                    pe.wait_ge(z_used, N)
                    pe.wait_ge(t_kept, N - NT)
                if t >= 2:
                    pe.wait_ge(w_kept, t - 1)
                    pe.wait_ge(u_kept, t - 1)
                mm4(4 + t % 2, lambda h: part(bk[:, t, :], h), lambda h: part(inv_T[:, t, :], h)).then_inc(sol_done, 1)
                mm4(6 + t % 2, lambda h: part(inv_T[:, t, :], h), lambda h: g.qkvT[:, 2 * NH + h, cols]).then_inc(sol_done, 1)

            def turn_out(t):
                pe.wait_ge(normed, NH * (t + 1))
                if t >= 1:
                    pe.wait_ge(o_kept, t)
                for h in range(NH):
                    mm = pe.transpose(ps[:, 6, h * P:(h + 1) * P], part(tmp[:, NORM_ON[t % 2], :], h), ident)
                mm.then_inc(o_turned, 1)

            for c in range(NC):
                t, r = c // 2, c % 2
                rows = slice(C * r, C * (r + 1))
                cols = slice(t * P + C * r, t * P + C * (r + 1))
                if c == 0:
                    pe.wait_ge(s_zero, 1)
                    pe.wait_ge(w_kept, NT)
                    pe.wait_ge(u_kept, NT)
                    pe.wait_ge(qd_done, NT)
                else:
                    pe.wait_ge(s_done, c)
                if c >= 2:
                    pe.wait_ge(delta_done, c - 1)
                state = S[:, c % 2, :]
                for h in range(NH):
                    mm = pe.matmul(ps[rows, c % 2, h * P:(h + 1) * P], wT[:, t, h * P + C * r:h * P + C * (r + 1)], part(state, h),
                                   start=True, stop=True)
                mm.then_inc(ws_done, 1)
                if r == 0 and t >= 2:
                    pe.wait_ge(normed, NH * (t - 1))
                for h in range(NH):
                    mm = pe.matmul(ps[rows, 4 + t % 2, h * P:(h + 1) * P], g.qkvT[:, h, cols], part(state, h),
                                   start=(h == 0), stop=False, skip_group_check=True)
                pe.wait_ge(delta_done, c + 1)
                if c < NC - 1:
                    if c >= 2:
                        pe.wait_ge(s_done, c - 1)
                    for h in range(NH):
                        mm = pe.matmul(ps[:, 2 + c % 2, h * P:(h + 1) * P], g.qkvT[rows, NH + h, t * P:(t + 1) * P],
                                       tmp[rows, t % 2, h * P:(h + 1) * P], start=True, stop=True)
                    mm.then_inc(upd_done, 1)
                if r == 1:
                    pe.wait_ge(masked, NT)
                    for h in range(NH):
                        mm = pe.matmul(ps[:, 4 + t % 2, h * P:(h + 1) * P], part(aqk[:, t, :], h), part(tmp[:, t % 2, :], h),
                                       start=False, stop=(h == NH - 1), skip_group_check=True)
                    mm.then_inc(out_done, 1)
                    if t >= 1:
                        turn_out(t - 1)
            turn_out(NT - 1)

        @block.scalar
        def _(act):
            act.wait_ge(y_ready, 1)
            act.wait_ge(one_set, 1)
            act.activation(small[:, BETA], g.dab[:, :, NH:2 * NH], ACT.Sigmoid).then_inc(soft, 1)
            act.activation(small[:, AB], small[:, Y], ACT.Abs).then_inc(soft, 1)
            act.wait_ge(soft, 2)
            act.activation(small[:, AB], small[:, AB], ACT.Exp, scale=-1.0).then_inc(soft, 1)
            act.wait_ge(soft, 3)
            act.activation(small[:, AB], small[:, AB], ACT.Ln, bias=one[:, 0:1]).then_inc(soft, 1)
            act.activation(par[:, 0, :], par[:, 0, :], ACT.Exp).then_inc(soft, 1)
            act.wait_ge(small_ready, 2)
            act.activation(small[:, EBN], small[:, BN], ACT.Exp).then_inc(small_exp, 1)
            act.activation(small[:, KDS], small[:, KDS], ACT.Exp).then_inc(small_exp, 1)
            act.activation(decS[:].rearrange("p r t h -> p (r t h)"), ps[:, 7, 64:128], ACT.Exp).then_inc(small_exp, 1)
            for t in range(NT):
                act.wait_ge(rows_done, 2 * t + 1)
                if t >= 2:
                    act.wait_ge(qd_done, t - 1)
                act.activation(tmp[:, 2 + t % 2, :], ps[:, ROWS, :], ACT.Exp).then_inc(row_exp, 1)
                act.wait_ge(apart, NH * (t + 1))
                act.activation(E_[:, t, :], E_[:, t, :], ACT.Exp).then_inc(pair_exp, 1)
                act.wait_ge(kv_turned, 2 * t + 2)
                for h in range(NH):
                    act.activation(g.qkvT[:, 2 * NH + h, t * P:(t + 1) * P], ps[:, VN, h * P:(h + 1) * P], ACT.Copy,
                                   scale=small[:, BETA, t, h:h + 1]).then_inc(v_done, 1)
            for t in range(NT):
                act.wait_ge(first_turned, t + 1)
                act.copy(inv[:, t, :], ps[:, TURN, :]).then_inc(first_kept, 1)
            N = len(STEPS)
            for s in range(N + 2):
                if s >= 2 and STEPS[s - 2][0] < LEVELS - 1:
                    q = s - 2
                    act.wait_ge(t_done, q + 1)
                    act.copy(inv[:, STEPS[q][1], :], ps[:, 4 + q % 2, :]).then_inc(t_kept, 1)
                if s < N:
                    act.wait_ge(x_done, s + 1)
                    if s >= 2:
                        act.wait_ge(z_done, s - 1)
                    act.copy(tmp[:, 2 + s % 2, :], ps[:, s % 2, :]).then_inc(x_kept, 1)
            for t in range(NT):
                act.wait_ge(sol_done, 2 * t + 1)
                act.copy(wT[:, t, :], ps[:, 4 + t % 2, :]).then_inc(w_kept, 1)

            def keep_out(t):
                act.wait_ge(o_turned, t + 1)
                act.activation(g.mixB[:, :, t * P:(t + 1) * P], heads(ps[:, 6, :]), ACT.Copy, scale=g.par[:, R_GDN:R_GDN + 1]).then_inc(o_kept, 1)

            for t in range(NT):
                act.wait_ge(out_done, t + 1)
                for h in range(NH):
                    act.activation(bk[:, 0, h * P:(h + 1) * P], ps[:, 4 + t % 2, h * P:(h + 1) * P], ACT.Square,
                                   accum_out=stat[:, 0, t, h:h + 1]).then_inc(squares, 1)
                act.wait_ge(squares, NH * (t + 1))
                act.activation(stat[:, 1, t, :], stat[:, 0, t, :], ACT.Sqrt, scale=1.0 / P, bias=g.eps[:, 0:1]).then_inc(roots, 1)
                if t >= 1:
                    keep_out(t - 1)
            keep_out(NT - 1)

        @block.vector
        def _(dve):
            dve.memset(one[:], 1.0).then_inc(one_set, 1)
            dve.wait_ge(par_in, 32)
            dve.tensor_tensor(small[:, Y], g.dab[:, :, 0:NH], par[:, 1:2, :].to_broadcast([P, NT, NH]), ALU.add).then_inc(y_ready, 1)
            dve.wait_ge(soft, 5)
            dve.scalar_tensor_tensor(out=small[:, SP], in0=small[:, Y], scalar=0.0, in1=small[:, AB], op0=ALU.max, op1=ALU.add).then_inc(y_ready, 1)
            dve.wait_ge(y_ready, 2)
            dve.scalar_tensor_tensor(out=small[:, GN], in0=small[:, SP], scalar=-1.0, in1=par[:, 0:1, :].to_broadcast([P, NT, NH]),
                                     op0=ALU.mult, op1=ALU.mult).then_inc(gn_ready, 1)
            dve.wait_ge(sums, 4)
            dve.tensor_copy(small[:, BN].rearrange("p t h -> p (t h)"), ps[:, 7, 0:32]).then_inc(small_ready, 1)
            dve.wait_ge(small_ready, 1)
            dve.tensor_tensor(small[:, KDS].rearrange("p t h -> p (t h)"), ps[:, 7, 32:64], small[:, BN].rearrange("p t h -> p (t h)"),
                              ALU.subtract).then_inc(small_ready, 1)
            dve.wait_ge(small_exp, 3)
            dve.tensor_tensor(small[:, BKE], small[:, EBN], small[:, BETA], ALU.mult).then_inc(bke_ready, 1)
            dve.wait_ge(bke_ready, 1)
            for t in range(NT):
                cols = slice(t * P, (t + 1) * P)
                if t >= 1:
                    dve.wait_ge(rows_done, 2 * t)
                for slot, what, by in ((0, tri, GN), (1, ident, BETA)):
                    dve.tensor_tensor(heads(tmp[:, slot, :]), what.unsqueeze(1).to_broadcast([P, NH, P]), over(small[:, by, t, :]),
                                      ALU.mult).then_inc(scaled, 1)
                dve.wait_ge(row_exp, t + 1)
                for h in range(NH):
                    dve.tensor_scalar(E_[:, t, h * P:(h + 1) * P], ps[:, ROWS, h * P:(h + 1) * P], small[:, BN, t, h:h + 1], 0.0,
                                      ALU.subtract, ALU.min).then_inc(apart, 1)
                dve.wait_ge(kv_turned, 2 * t + 1)
                dve.tensor_tensor(heads(bk[:, t, :]), heads(ps[:, KN, :]), over(small[:, BKE, t, :]), ALU.mult).then_inc(nat_done, 1)
                dve.tensor_tensor(g.qkvT[:, NH:2 * NH, cols], heads(ps[:, KN, :]), over(small[:, KDS, t, :]), ALU.mult).then_inc(nat_done, 1)
                dve.wait_ge(kq_done, 2 * t + 2)
                dve.tensor_tensor(g.qkvT[:, 0:NH, cols], g.qkvT[:, 0:NH, cols], heads(tmp[:, 2 + t % 2, :]), ALU.mult).then_inc(qd_done, 1)
                dve.wait_ge(pair_exp, t + 1)
                dve.wait_ge(rows_done, 2 * t + 2)
                dve.tensor_tensor(aqk[:, t, :], ps[:, QK, :], E_[:, t, :], ALU.mult).then_inc(prod, 1)
                if t >= 1:
                    dve.wait_ge(cut0, t)
                dve.tensor_tensor(tmp[:, 4, :], ps[:, BROW, :], E_[:, t, :], ALU.mult).then_inc(prod, 1)
                dve.wait_ge(prod, 3 * t + 2)
                dve.tensor_tensor(LT[:, t, :], ps[:, KK, :], tmp[:, 4, :], ALU.mult).then_inc(prod, 1)
                dve.wait_ge(prod, 3 * t + 3)
                if t >= 1:
                    dve.wait_ge(inv0, t)
                dve.tensor_tensor(heads(tmp[:, 5, :]), heads(LT[:, t, :]), g.k[:, K_LEVEL:K_LEVEL + P].unsqueeze(1).to_broadcast([P, NH, P]),
                                  ALU.mult).then_inc(cut0, 1)
                dve.wait_ge(cut0, t + 1)
                dve.tensor_tensor(heads(inv_T[:, t, :]), ident.unsqueeze(1).to_broadcast([P, NH, P]), heads(tmp[:, 5, :]),
                                  ALU.subtract).then_inc(inv0, 1)
            for s, (l, t) in enumerate(STEPS):
                dve.wait_ge(z_done, s + 1)
                if s >= NT and l < LEVELS:
                    dve.wait_ge(t_done, s - NT + 1)
                dve.tensor_tensor(inv_T[:, t, :], inv_T[:, t, :], ps[:, 2 + s % 2, :], ALU.subtract).then_inc(z_used, 1)
            for t in range(NT):
                dve.wait_ge(sol_done, 2 * t + 2)
                dve.tensor_copy(u[:, t, :], ps[:, 6 + t % 2, :]).then_inc(u_kept, 1)

            def norm_out(t):
                dve.wait_ge(roots, t + 1)
                dve.reciprocal(stat[:, 1, t, :], stat[:, 1, t, :]).then_inc(inverses, 1)
                dve.wait_ge(inverses, t + 1)
                dve.wait_ge(gate_in[t % 2], 16 * (t // 2 + 1))
                if t >= 2:
                    dve.wait_ge(o_turned, t - 1)
                for h in range(NH):
                    cols = slice(h * P, (h + 1) * P)
                    dve.scalar_tensor_tensor(out=tmp[:, NORM_ON[t % 2], cols], in0=ps[:, 4 + t % 2, cols], scalar=stat[:, 1, t, h:h + 1],
                                             in1=tmp[:, NORM_GATE[t % 2], cols], op0=ALU.mult, op1=ALU.mult).then_inc(normed, 1)

            dve.wait_ge(u_kept, NT)
            dve.wait_ge(s_zero, 1)
            for c in range(NC):
                t, r = c // 2, c % 2
                rows = slice(C * r, C * (r + 1))
                dve.wait_ge(ws_done, c + 1)
                if r == 0 and t >= 2:
                    dve.wait_ge(out_done, t - 1)
                dve.tensor_tensor(tmp[rows, t % 2, :], u[rows, t, :], ps[rows, c % 2, :], ALU.subtract).then_inc(delta_done, 1)
                if c < NC - 1:
                    if c >= 1:
                        dve.wait_ge(s_done, c)
                    dve.tensor_tensor(heads(S[:, (c + 1) % 2, :]), heads(S[:, c % 2, :]), over(decS[:, r, t, :]), ALU.mult).then_inc(s_decayed, 1)
                    dve.wait_ge(s_decayed, c + 1)
                    dve.wait_ge(upd_done, c + 1)
                    dve.tensor_tensor(S[:, (c + 1) % 2, :], S[:, (c + 1) % 2, :], ps[:, 2 + c % 2, :], ALU.add).then_inc(s_done, 1)
                if r == 0 and t >= 1:
                    norm_out(t - 1)
            norm_out(NT - 1)

def route(nc, g, sem):
    with ExitStack() as ph:
        def sb(name, shape, dt=F32):
            return ph.enter_context(nc.sbuf_tensor("rt_" + name, shape, dt))

        w_out = g.ring[:, 8:12].rearrange("p s n -> p (s n)").rearrange("p (k n) -> p k n", k=KT)
        w_router = sb("w_router", [P, KT, E])
        xt = sb("x", [P, 2, D])
        xn = sb("xn", [P, 2, D])
        xnT = sb("xnT", [P, KT, P])
        gain = sb("g_moe", [P, D])
        b_router = sb("b_router", [P, E])
        rows = xnT[:, 0:6]
        stat = sb("stat", [P, 3, NT])
        logit = sb("logit", [P, NT, E])
        top = sb("top", [P, NT, 8])
        top_e = sb("top_e", [P, NT, 8], U32)
        top_f = sb("top_f", [P, NT, TOPK])
        hot = sb("hot", [P, NT, TOPK, E])
        chosen = sb("chosen", [P, NT, E])
        spot = sb("spot", [P, E])
        step = sb("step", [P, 2, NT, E])
        weigh = xnT[:].rearrange("p t (k e) -> p t k e", k=TOPK)
        neg = sb("neg", [P, NT, 2])
        ps = ph.enter_context(nc.psum_tensor("rt_psum", [P, 8, HALF], F32))
        ident = g.k[:, K_ID:K_ID + P]

        w_in_s, bc_in, rows_in = sem("weights_in"), sem("broadcasts_in"), sem("bias_rows_in")
        x_in, xn_out = [sem(f"x_in{i}") for i in range(2)], [sem(f"xn_out{i}") for i in range(2)]
        b_turned, b_kept = sem("bias_turned"), sem("bias_kept")
        proj, summed, squared, rooted, inv_done, normed = (sem(n) for n in ("projected", "summed", "squared", "rooted", "inverse", "normed"))
        turned, kept, logits, logit_sb, top_done, index_done, index_f, hot_done, chosen_done = (sem(n) for n in (
            "turned", "kept", "logits", "logit_kept", "top", "top_index", "top_index_f", "hot", "chosen"))
        places, spot_done, place_done, slot_step, slot_prod, slot_done, neg_done, exp_done, share_inv, share_done, list_done = (sem(n) for n in (
            "places", "spot", "place_kept", "slot_steps", "slot_products", "slots", "neg_top", "exp_top", "share_inverse", "shares", "lists"))
        totals, total_done = sem("totals"), sem("counts")
        block = ph.enter_context(nc.Block())

        @block.sync
        def _(sp):
            sp.dma_start(w_out, g.w_out.rearrange("a (k p) n -> p (a k) n", p=P)).then_inc(w_in_s, 16)
            for t in range(2):
                sp.dma_start(xt[:, t], g.x.rearrange("(t p) d -> t p d", p=P)[t]).then_inc(x_in[t], 16)
            sp.dma_start(w_router[:], g.w_router.rearrange("a (k p) n -> p (a k) n", p=P)).then_inc(w_in_s, 16)
            sp.dma_start(gain[:], g.g_moe.rearrange("a d -> (a d)").partition_broadcast(P)).then_inc(bc_in, 16)
            sp.dma_start(b_router[:], g.b_router.rearrange("a d -> (a d)").partition_broadcast(P)).then_inc(bc_in, 16)
            sp.dma_start(rows[:, 0:4], g.b_gate_up.rearrange("a e (j c) -> (a e j) c", c=P).rearrange("(q r) c -> r q c", r=P)).then_inc(rows_in, 16)
            sp.dma_start(rows[:, 4:6], g.b_down.rearrange("a e (j c) -> (a e j) c", c=P).rearrange("(q r) c -> r q c", r=P)).then_inc(rows_in, 16)
            for i in range(8):
                sp.dma_start(g.ring[:, i].rearrange("p (k n) -> p k n", k=KT), weight_source(g, 0, i)).then_inc(g.w_in_ring[i], 16)
            for t in range(NT):
                if t >= 2:
                    sp.wait_ge(summed, t - 1)
                    sp.dma_start(xt[:, t % 2], g.x.rearrange("(t p) d -> t p d", p=P)[t]).then_inc(x_in[t % 2], 16)
                if t >= 1:
                    sp.wait_ge(normed, t)
                    sp.dma_start(g.xn_dram.rearrange("(t p) d -> t p d", p=P)[t - 1], xn[:, (t - 1) % 2]).then_inc(xn_out[(t - 1) % 2], 16)
            sp.wait_ge(normed, NT)
            sp.dma_start(g.xn_dram.rearrange("(t p) d -> t p d", p=P)[NT - 1], xn[:, (NT - 1) % 2]).then_inc(xn_out[(NT - 1) % 2], 16)
            for s in xn_out:
                sp.wait_ge(s, 16 * NT // 2)

        @block.tensor
        def _(pe):
            pe.wait_ge(rows_in, 32)
            for q in range(6):
                mm = pe.transpose(ps[:, 6 + q // 4, (q % 4) * P:(q % 4 + 1) * P], rows[:, q], ident)
            mm.then_inc(b_turned, 1)
            pe.wait_ge(w_in_s, 32)

            def project_tile(t):
                if t >= 2:
                    pe.wait_ge(summed, t - 1)
                for half in range(2):
                    for k in range(KT):
                        mix = (g.mixA if k < NH else g.mixB)[:, k % NH, t * P:(t + 1) * P]
                        mm = pe.matmul(ps[:, 2 * (t % 2) + half, :], mix, w_out[:, k, half * HALF:(half + 1) * HALF],
                                       start=(k == 0), stop=(k == KT - 1))
                mm.then_inc(proj, 1)

            def router_tile(t):
                pe.wait_ge(normed, t + 1)
                if t >= 1:
                    pe.wait_ge(kept, 2 * t)
                for q in range(2):
                    for i in range(4):
                        mm = pe.transpose(ps[:, 4 + q, i * P:(i + 1) * P], xn[:, t % 2, (4 * q + i) * P:(4 * q + i + 1) * P], ident)
                    mm.then_inc(turned, 1)
                pe.wait_ge(kept, 2 * (t + 1))
                if t == 0:
                    pe.wait_ge(b_kept, 2)
                else:
                    pe.wait_ge(logit_sb, t)
                for k in range(KT):
                    mm = pe.matmul(ps[:, 6, 0:E], xnT[:, k, :], w_router[:, k, :], start=(k == 0), stop=(k == KT - 1))
                mm.then_inc(logits, 1)

            def place_tile(t):
                pe.wait_ge(chosen_done, t + 1)
                if t >= 1:
                    pe.wait_ge(spot_done, t)
                for s in range(t + 1):
                    tri = K_STRICT if s == t else K_ONES
                    mm = pe.matmul(ps[:, 7, 0:E], g.k[:, tri:tri + P], chosen[:, s, :], start=(s == 0), stop=(s == t))
                mm.then_inc(places, 1)

            project_tile(0)
            for t in range(NT):
                if t + 1 < NT:
                    project_tile(t + 1)
                router_tile(t)
                if t >= 1:
                    place_tile(t - 1)
            place_tile(NT - 1)
            pe.wait_ge(spot_done, NT)
            for s in range(NT):
                mm = pe.matmul(ps[:, 7, 0:E], g.k[:, K_ONES:K_ONES + P], chosen[:, s, :], start=(s == 0), stop=(s == NT - 1))
            mm.then_inc(totals, 1)

        @block.scalar
        def _(act):
            def keep_turned(t):
                for q in range(2):
                    act.wait_ge(turned, 2 * t + q + 1)
                    if t >= 1:
                        act.wait_ge(logits, t)
                    act.copy(xnT[:, 4 * q:4 * q + 4, :], ps[:, 4 + q, :].rearrange("p (k c) -> p k c", k=4)).then_inc(kept, 1)

            for t in range(NT):
                act.wait_ge(summed, t + 1)
                if t >= 2:
                    act.wait_ge(turned, 2 * (t - 1))
                    act.wait_ge(xn_out[t % 2], 16 * (t // 2))
                act.activation(xn[:, t % 2], g.h[:, t, :], ACT.Square, accum_out=stat[:, 0, t:t + 1]).then_inc(squared, 1)
                act.wait_ge(squared, t + 1)
                act.activation(stat[:, 1, t:t + 1], stat[:, 0, t:t + 1], ACT.Sqrt, scale=1.0 / D, bias=g.eps[:, 0:1]).then_inc(rooted, 1)
                keep_turned(t)
            for t in range(NT):
                act.wait_ge(neg_done, t + 1)
                act.activation(top[:, t, 0:TOPK], top[:, t, 0:TOPK], ACT.Exp, bias=neg[:, t, 0:1], accum_out=neg[:, t, 1:2]).then_inc(exp_done, 1)

        @block.vector
        def _(dve):
            dve.wait_ge(b_turned, 1)
            dve.tensor_copy(g.b_gu[:].rearrange("p e j -> p (e j)"), ps[:, 6, :]).then_inc(b_kept, 1)
            dve.tensor_copy(g.b_dn[:].rearrange("p e j -> p (e j)"), ps[:, 7, 0:2 * P]).then_inc(b_kept, 1)
            dve.wait_ge(bc_in, 32)
            iota_e = g.k[:, K_E:K_E + E]

            def norm(t):
                dve.wait_ge(proj, t + 1)
                dve.wait_ge(x_in[t % 2], 16 * (t // 2 + 1))
                dve.tensor_tensor(g.h[:, t, :], ps[:, 2 * (t % 2):2 * (t % 2) + 2, :].rearrange("p a c -> p (a c)"), xt[:, t % 2],
                                  ALU.add).then_inc(summed, 1)
                dve.wait_ge(rooted, t + 1)
                dve.reciprocal(stat[:, 1, t:t + 1], stat[:, 1, t:t + 1]).then_inc(inv_done, 1)
                dve.wait_ge(inv_done, t + 1)
                dve.scalar_tensor_tensor(out=xn[:, t % 2], in0=g.h[:, t, :], scalar=stat[:, 1, t:t + 1], in1=gain[:],
                                         op0=ALU.mult, op1=ALU.mult).then_inc(normed, 1)

            def choose(t):
                dve.wait_ge(logits, t + 1)
                dve.tensor_tensor(logit[:, t, :], ps[:, 6, 0:E], b_router[:], ALU.add).then_inc(logit_sb, 1)
                dve.wait_ge(logit_sb, t + 1)
                dve.max(top[:, t, :], logit[:, t, :]).then_inc(top_done, 1)
                dve.wait_ge(top_done, t + 1)
                dve.max_index(top_e[:, t, :], top[:, t, :], logit[:, t, :]).then_inc(index_done, 1)
                dve.wait_ge(index_done, t + 1)
                dve.tensor_scalar(neg[:, t, 0:1], top[:, t, 0:1], -1.0, None, ALU.mult).then_inc(neg_done, 1)
                dve.tensor_copy(top_f[:, t, :], top_e[:, t, 0:TOPK]).then_inc(index_f, 1)
                dve.wait_ge(index_f, t + 1)
                dve.tensor_tensor(hot[:, t], iota_e.unsqueeze(1).to_broadcast([P, TOPK, E]), top_f[:, t, :].unsqueeze(2).to_broadcast([P, TOPK, E]),
                                  ALU.is_equal).then_inc(hot_done, 1)
                dve.wait_ge(hot_done, t + 1)
                dve.tensor_reduce(chosen[:, t, :], hot[:, t].rearrange("p k e -> p e k"), AX.X, ALU.add).then_inc(chosen_done, 1)

            def place(t):
                dve.wait_ge(places, t + 1)
                if t >= 1:
                    dve.wait_ge(place_done, t)
                dve.scalar_tensor_tensor(out=spot[:], in0=ps[:, 7, 0:E], scalar=1.0, in1=chosen[:, t, :], op0=ALU.add, op1=ALU.mult).then_inc(spot_done, 1)
                dve.wait_ge(spot_done, t + 1)
                dve.tensor_scalar(g.place[:, t, 0:E], spot[:], -1.0, None, ALU.add).then_inc(place_done, 1)

            def slots():
                dve.wait_ge(place_done, NT)
                dve.wait_ge(logits, NT)
                place_of = g.place[:, :, 0:E]
                dve.tensor_tensor(step[:, 0], place_of, g.k[:, K_SLOT:K_SLOT + E].unsqueeze(1).to_broadcast([P, NT, E]),
                                  ALU.add).then_inc(slot_step, 1)
                for r in range(1, ROUNDS):
                    dve.tensor_scalar(step[:, 1], place_of, float(r * CAP), float(Y_ROUND - CAP), ALU.is_ge, ALU.mult).then_inc(slot_step, 1)
                    dve.wait_ge(slot_step, 2 * r)
                    dve.tensor_tensor(step[:, 0], step[:, 0], step[:, 1], ALU.add).then_inc(slot_step, 1)
                    dve.wait_ge(slot_step, 2 * r + 1)
                for k in range(TOPK):
                    dve.tensor_tensor(weigh[:, :, k, :], hot[:, :, k, :], step[:, 0], ALU.mult).then_inc(slot_prod, 1)
                dve.wait_ge(slot_prod, TOPK)
                with nc.allow_low_precision(reason="whole numbers below 2**24, summed in float32"):
                    dve.tensor_reduce(g.slot[:].rearrange("p t k -> p (t k)"), weigh.rearrange("p t k e -> p (t k) e"), AX.X,
                                      ALU.add).then_inc(slot_done, 1)

            dve.memset(g.place[:, :, E:E + 1], -1.0).then_inc(list_done, 1)
            norm(0)
            for t in range(NT):
                if t + 1 < NT:
                    norm(t + 1)
                choose(t)
                if t >= 1:
                    place(t - 1)
            place(NT - 1)
            for t in range(NT):
                dve.wait_ge(exp_done, t + 1)
                dve.reciprocal(neg[:, t, 1:2], neg[:, t, 1:2]).then_inc(share_inv, 1)
                dve.wait_ge(share_inv, t + 1)
                dve.tensor_scalar(g.share[:, t, :], top[:, t, 0:TOPK], neg[:, t, 1:2], None, ALU.mult).then_inc(share_done, 1)
            dve.wait_ge(totals, 1)
            dve.tensor_copy(g.count[:, 0:E], ps[:, 7, 0:E]).then_inc(total_done, 1)
            with nc.allow_low_precision(reason="whole numbers below 2**24"):
                dve.tensor_reduce(g.count[:, E:E + 1], ps[:, 7, 0:E], AX.X, ALU.max).then_inc(total_done, 1)
            slots()


def weight_source(g, e, i):
    if i < 8:
        col = (i % 2) * FF + (i // 2) * 256
        return g.w_gate_up[e].rearrange("(k p) n -> p k n", p=P)[:, :, col:col + 256]
    return g.w_down[e].rearrange("(k p) n -> p k n", p=P)[:, :, (i - 8) * 256:(i - 7) * 256]


class Experts:

    GATE_UP = [(0, 1), (2, 3)]
    DOWN = (4, 5)
    TURN, LIST = 6, 7

    def __init__(self, nc, g, sem, ph):
        self.nc, self.g = nc, g

        def sb(name, shape, dt=F32):
            return ph.enter_context(nc.sbuf_tensor("ex_" + name, shape, dt))

        self.xT = sb("xT", [P, KT, CAP])
        self.hT = sb("hT", [P, FF // P, CAP])
        self.yT = sb("yT", [P, KT, CAP])
        self.rows_a = sb("rows_a", [P, D])
        self.rows_b = sb("rows_b", [CAP - P, D])
        self.y_a = sb("y_a", [P, D])
        self.y_b = sb("y_b", [CAP - P, D])
        self.mark = sb("mark", [P, NT, CAP], BF16)
        self.token = sb("token", [P, 2 * NT], BF16)
        self.list_a = sb("list_a", [P, 1], U32)
        self.list_b = sb("list_b", [CAP - P, 1], U32)
        self.gate = sb("gate", [P, 2, 2, CAP])
        self.up = sb("up", [P, 2, 2, CAP])
        self.sig = sb("sig", [P, 2, 2, CAP])
        self.ps = ph.enter_context(nc.psum_tensor("ex_psum", [P, 8, HALF], F32))
        self.marked = sem("marked")
        self.list_summed = sem("list_summed")
        self.listed = sem("listed")
        self.rows_in = [sem("rows_a_in"), sem("rows_b_in")]
        self.turned = sem("bank6_filled")
        self.turn_kept = sem("bank6_emptied")
        self.x_kept = sem("xT_kept")
        self.gu_done = sem("gate_up_done")
        self.gu_kept = sem("gate_up_kept")
        self.sig_done = sem("sigmoid")
        self.act_step = sem("activation_steps")
        self.h_done = sem("hT")
        self.dn_done = sem("down_done")
        self.yT_kept = sem("yT_kept")
        self.y_out = [sem("y_a_out"), sem("y_b_out")]
        self.ready = sem("ready")
        self.rows_free, self.bank6_free, self.pass_stored, self.fill_seen, self.shift_seen = (
            sem(n) for n in ("gather_rows_free", "bank6_free", "pass_stored", "fill_seen", "shift_seen"))
        self.shifted = sem("places_shifted")
        self.filled = sem("round_rows_filled")
        self.ident = g.k[:, K_ID:K_ID + P]

    def dve_find(self, dve, x, e):
        dve.wait_ge(self.list_summed, x)
        dve.tensor_tensor(self.mark[:], self.g.k[:, K_IOTA:K_IOTA + CAP].unsqueeze(1).to_broadcast([P, NT, CAP]),
                          self.g.place[:, :, bass.ds(e, 1)].to_broadcast([P, NT, CAP]), ALU.is_equal).then_inc(self.marked, 1)

    def gather(self, pool, x, fill):
        pool.wait_ge(self.listed, 2 * x + 2)
        pool.wait_ge(self.turned, fill).then_inc(self.rows_free, 1)
        for rows, index, n in ((self.rows_a, self.list_a, 0), (self.rows_b, self.list_b, 1)):
            pool.indirect_dma_start(out=rows[:], out_offset=None, in_=self.g.xn_dram,
                                    in_offset=bass.IndirectOffsetOnAxis(ap=index[:, 0:1], axis=0)).then_inc(self.rows_in[n], 16)

    def pe_list(self, pe, x):
        pe.wait_ge(self.marked, x + 1)
        pe.wait_ge(self.listed, 2 * x)
        for width, lo, at in ((P, 0, 0), (CAP - P, P, 2)):
            for t in range(NT):
                mm = pe.matmul(self.ps[0:width, self.LIST, at:at + 2], self.mark[:, t, lo:lo + width],
                               self.token[:, 2 * t:2 * t + 2], start=(t == 0), stop=(t == NT - 1))
        mm.then_inc(self.list_summed, 1)

    def dve_list(self, dve, x):
        dve.wait_ge(self.list_summed, x + 1)
        for r in self.rows_in:
            dve.wait_ge(r, 16 * x)
        for width, to, at in ((P, self.list_a, 0), (CAP - P, self.list_b, 2)):
            with self.nc.allow_low_precision(reason="token numbers, summed in float32"):
                dve.tensor_reduce(to[0:width, 0:1], self.ps[0:width, self.LIST, at:at + 2], AX.X, ALU.add).then_inc(self.listed, 1)

    def pe_turn_x(self, pe, x, fill, q):
        if q == 0:
            for r in self.rows_in:
                pe.wait_ge(r, 16 * x + 16)
        pe.wait_ge(self.turn_kept, fill + q)
        for i in range(2):
            k = 2 * q + i
            pe.transpose(self.ps[:, self.TURN, i * CAP:i * CAP + P], self.rows_a[:, k * P:(k + 1) * P], self.ident)
            mm = pe.transpose(self.ps[:, self.TURN, i * CAP + P:(i + 1) * CAP], self.rows_b[:, k * P:(k + 1) * P],
                              self.g.k[0:CAP - P, K_ID:K_ID + CAP - P])
        mm.then_inc(self.turned, 1)

    def act_keep_x(self, act, x, fill, q, after):
        act.wait_ge(self.turned, fill + q + 1)
        act.wait_ge(self.gu_done, after)
        act.copy(self.xT[:, 2 * q:2 * q + 2, :], self.ps[:, self.TURN, 0:2 * CAP].rearrange("p (i c) -> p i c", i=2)).then_inc(self.turn_kept, 1)

    def pe_gate_up(self, pe, m, fill_x, c, width):
        gate_bank, up_bank = self.GATE_UP[c % 2]
        if c == 0:
            pe.wait_ge(self.turn_kept, fill_x)
        pe.wait_ge(self.gu_kept, 16 * m + 4 * c + 4)
        for half, bank in ((0, gate_bank), (1, up_bank)):
            slot = 2 * c + half
            w = self.g.ring[:, slot].rearrange("p (k n) -> p k n", k=KT)
            pe.wait_ge(self.g.w_in_ring[slot], 16 * m + 16)
            for i in range(2):
                for k in range(KT):
                    mm = pe.matmul(self.ps[:, bank, i * CAP:i * CAP + width], w[:, k, i * P:(i + 1) * P], self.xT[:, k, 0:width],
                                   start=(k == 0), stop=(k == KT - 1))
            mm.then_inc(self.gu_done, 1)

    def dve_gate_up(self, dve, m, e, c):
        gate_bank, up_bank = self.GATE_UP[c % 2]
        gate, up = self.gate[:, c % 2], self.up[:, c % 2]
        dve.wait_ge(self.gu_done, 8 * m + 2 * c + 1)
        for i in range(2):
            bias = self.g.b_gu[:, bass.ds(e, 1), 2 * c + i:2 * c + i + 1].rearrange("p a b -> p (a b)")
            dve.tensor_scalar(gate[:, i], self.ps[:, gate_bank, i * CAP:(i + 1) * CAP], bias, 7.0, ALU.add, ALU.min).then_inc(self.gu_kept, 1)
        dve.wait_ge(self.gu_done, 8 * m + 2 * c + 2)
        for i in range(2):
            bias = self.g.b_gu[:, bass.ds(e, 1), 8 + 2 * c + i:8 + 2 * c + i + 1].rearrange("p a b -> p (a b)")
            dve.tensor_scalar(up[:, i], self.ps[:, up_bank, i * CAP:(i + 1) * CAP], bias, -7.0, ALU.add, ALU.max).then_inc(self.gu_kept, 1)
        dve.wait_ge(self.gu_kept, 16 * m + 4 * c + 4 + 8)
        dve.tensor_scalar(up, up, 7.0, 1.0, ALU.min, ALU.add).then_inc(self.act_step, 1)
        dve.wait_ge(self.sig_done, 4 * m + c + 1)
        dve.tensor_tensor(gate, gate, self.sig[:, c % 2], ALU.mult).then_inc(self.act_step, 1)
        dve.wait_ge(self.act_step, 8 * m + 2 * c + 4)
        if c == 0:
            dve.wait_ge(self.yT_kept, 8 * m + 4)
        dve.tensor_tensor(self.hT[:, 2 * c:2 * c + 2, :], up, gate, ALU.mult).then_inc(self.h_done, 1)

    def act_sigmoid(self, act, m, c):
        act.wait_ge(self.gu_kept, 16 * m + 4 * c + 2 + 8)
        act.wait_ge(self.act_step, 8 * m + 2 * c + 2)
        act.activation(self.sig[:, c % 2], self.gate[:, c % 2], ACT.Sigmoid, scale=1.702).then_inc(self.sig_done, 1)

    def pe_down(self, pe, m, c, width):
        w = self.g.ring[:, 8 + c].rearrange("p (k n) -> p k n", k=KT)
        bank = self.DOWN[c % 2]
        pe.wait_ge(self.g.w_in_ring[8 + c], 16 * m + 16)
        pe.wait_ge(self.yT_kept, 8 * m + 2 * c + 2)
        for k in range(KT):
            if c == 0 and k % 2 == 0:
                pe.wait_ge(self.h_done, 4 * m + k // 2 + 1)
            for i in range(2):
                mm = pe.matmul(self.ps[:, bank, i * CAP:i * CAP + width], w[:, k, i * P:(i + 1) * P], self.hT[:, k, 0:width],
                               start=(k == 0 and i == 0), stop=(k == KT - 1), skip_group_check=True)
        mm.then_inc(self.dn_done, 1)

    def act_down(self, act, m, e, c):
        act.wait_ge(self.dn_done, 4 * m + c + 1)
        for i in range(2):
            bias = self.g.b_dn[:, bass.ds(e, 1), 2 * c + i:2 * c + i + 1].rearrange("p a b -> p (a b)")
            act.activation(self.yT[:, 2 * c + i, :], self.ps[:, self.DOWN[c % 2], i * CAP:(i + 1) * CAP], ACT.Identity,
                           bias=bias).then_inc(self.yT_kept, 1)

    def pe_turn_y(self, pe, fill, kept, q):
        if q == 0:
            pe.wait_ge(self.yT_kept, kept)
        if q < 2:
            pe.wait_ge(self.turn_kept, fill + q)
        else:
            pe.wait_ge(self.turn_kept, fill + q).then_inc(self.bank6_free, 1)
        tokens = slice(0, P) if q < 2 else slice(P, CAP)
        n = P if q < 2 else CAP - P
        for i in range(4):
            mm = pe.transpose(self.ps[0:n, self.TURN, i * P:(i + 1) * P], self.yT[:, 4 * (q % 2) + i, tokens], self.ident)
        mm.then_inc(self.turned, 1)

    def dve_keep_y(self, dve, y, fill, q):
        dve.wait_ge(self.turned, fill + q + 1)
        n, to = (P, self.y_a) if q < 2 else (CAP - P, self.y_b)
        dve.wait_ge(self.y_out[q // 2], 16 * y + 16)
        dve.tensor_copy(to[0:n, (q % 2) * HALF:(q % 2 + 1) * HALF], self.ps[0:n, self.TURN, :]).then_inc(self.turn_kept, 1)

    def store(self, sp, fill, dst_a, dst_b):
        sp.wait_ge(self.turn_kept, fill + 4)
        sp.dma_start(dst_a, self.y_a[:]).then_inc(self.y_out[0], 16)
        sp.dma_start(dst_b, self.y_b[:]).then_inc(self.y_out[1], 16)


WIDTHS = (128, 144, 160, 176, CAP)


def experts(nc, g, sem):
    with ExitStack() as ph:
        x = Experts(nc, g, sem, ph)
        block = ph.enter_context(nc.Block())

        def rows(region):
            part = g.y_dram.rearrange("(r n) d -> r n d", n=CAP)[bass.ds(region, 1)].rearrange("a n d -> (a n) d")
            return part[0:P, :], part[P:CAP, :]

        def load(sp, e, i):
            if i < 8:
                src = g.w_gate_up[bass.ds(e, 1)].rearrange("a (k p) n -> p (a k) n", p=P)[:, :, (i % 2) * FF + (i // 2) * 256:(i % 2) * FF + (i // 2) * 256 + 256]
            else:
                src = g.w_down[bass.ds(e, 1)].rearrange("a (k p) n -> p (a k) n", p=P)[:, :, (i - 8) * 256:(i - 7) * 256]
            sp.dma_start(g.ring[:, i].rearrange("p (k n) -> p k n", k=KT), src).then_inc(g.w_in_ring[i], 16)

        def overflow(eng, body, start=None):
            most = eng.value_load(g.count[0:1, E:E + 1], min_val=0, max_val=T)
            with eng.If(most > CAP):
                n_reg = eng.alloc_register("n_" + str(eng.engine).split(".")[-1])
                eng.reg_mov(n_reg, 0)
                with eng.Fori(1, ROUNDS) as r:
                    if start is not None:
                        start(r)
                    with eng.Fori(0, E) as e:
                        count = eng.value_load(g.count[0:1, bass.ds(e, 1)], min_val=0, max_val=T)
                        with eng.If(count > r * CAP):
                            n = eng.snap(n_reg, min_val=0, max_val=E * ROUNDS)
                            body(n, r, e)
                            eng.reg_add(n_reg, n_reg, 1)

        @block.sync
        def _(sp):
            for i in range(8, 12):
                load(sp, 0, i)
            with sp.Fori(0, E - 1) as e:
                for i in range(12):
                    if i < 8:
                        sp.wait_ge(x.gu_done, 8 * e + i + 1)
                    else:
                        sp.wait_ge(x.dn_done, 4 * e + i - 7)
                    load(sp, e + 1, i)
                    if i == 7:
                        x.store(sp, 8 * e + 4, *rows(e))
            for y in range(E - 1, E + 1):
                x.store(sp, 8 * y + 4, *rows(y))

            def body(n, r, e):
                sp.wait_ge(x.dn_done, 4 * n + 4 * E)
                for i in range(12):
                    load(sp, e, i)
                x.store(sp, 8 * n + 8 * (E + 1) + 4, *rows(r * E + e + 1))
                sp.wait_ge(x.y_out[0], 16 * n + 16 * (E + 3))
                sp.wait_ge(x.y_out[1], 16 * n + 16 * (E + 3)).then_inc(x.pass_stored, 1)

            def fill(r):
                into = g.y_dram[Y_FIRST:, :].rearrange("(r n p) d -> r p n d", r=ROUNDS - 1, p=P)[bass.ds(r - 1, 1)]
                sp.dma_start(into.rearrange("a p n d -> (a p) n d"),
                             x.y_a[:].unsqueeze(1).to_broadcast([P, Y_ROUND // P, D])).then_inc(x.filled, 16)
                sp.wait_ge(x.filled, 16 * r).then_inc(x.fill_seen, 1)

            overflow(sp, body, fill)
            for s in x.y_out:
                sp.wait_ge(s, 16 * (E + 2))

        @block.gpsimd
        def _(pool):
            x.gather(pool, 0, 0)
            with pool.Fori(0, E) as e:
                x.gather(pool, e + 1, 8 * e + 4)

            def body(n, r, e):
                x.gather(pool, n + E + 1, 8 * n + 8 * (E + 1))
                for s in x.rows_in:
                    pool.wait_ge(s, 16 * n + 16 * (E + 2))

            overflow(pool, body)
            for s in x.rows_in:
                pool.wait_ge(s, 16 * (E + 1))

        @block.tensor
        def _(pe):
            pe.wait_ge(x.ready, 1)
            x.pe_list(pe, 0)
            for q in range(4):
                x.pe_turn_x(pe, 0, 0, q)

            def one_pass(e, width):
                for c in range(4):
                    x.pe_gate_up(pe, e, 8 * e + 4, c, width)
                    if c == 0:
                        x.pe_list(pe, e + 1)
                    x.pe_turn_y(pe, 8 * e + 4, 8 * e + 4, c)
                for c in range(4):
                    x.pe_turn_x(pe, e + 1, 8 * e + 8, c)
                    x.pe_down(pe, e, c, width)

            def by_width(count, widths, body):
                if len(widths) == 1:
                    body(widths[0])
                    return
                with pe.If(count <= widths[0]):
                    body(widths[0])
                with pe.Else():
                    by_width(count, widths[1:], body)

            with pe.Fori(0, E) as e:
                count = pe.value_load(g.count[0:1, bass.ds(e, 1)], min_val=0, max_val=T)
                by_width(count, WIDTHS, lambda width: one_pass(e, width))
            for q in range(4):
                x.pe_turn_y(pe, 8 * E + 4, 8 * E + 4, q)

            def body(n, r, e):
                m, fill = n + E, 8 * n + 8 * (E + 1)
                x.pe_list(pe, n + E + 1)
                for q in range(4):
                    x.pe_turn_x(pe, n + E + 1, fill, q)
                for c in range(4):
                    x.pe_gate_up(pe, m, fill + 4, c, CAP)
                for c in range(4):
                    x.pe_down(pe, m, c, CAP)
                for q in range(4):
                    x.pe_turn_y(pe, fill + 4, 8 * m + 8 + 4, q)

            overflow(pe, body)

        @block.scalar
        def _(act):
            act.copy(x.sig[:, 0, 0, 0:1], g.eps[:, 0:1]).then_inc(x.yT_kept, 4)
            for q in range(4):
                x.act_keep_x(act, 0, 0, q, 0)
            with act.Fori(0, E) as e:
                for c in range(4):
                    x.act_sigmoid(act, e, c)
                for c in range(4):
                    x.act_keep_x(act, e + 1, 8 * e + 8, c, 8 * e + 8)
                    x.act_down(act, e, e, c)

            def body(n, r, e):
                m, fill = n + E, 8 * n + 8 * (E + 1)
                for q in range(4):
                    x.act_keep_x(act, n + E + 1, fill, q, 8 * m)
                for c in range(4):
                    x.act_sigmoid(act, m, c)
                for c in range(4):
                    x.act_down(act, m, e, c)

            overflow(act, body)

        @block.vector
        def _(dve):
            dve.memset(x.ps[:, 0:6, :], 0.0).then_inc(x.gu_kept, 8)
            dve.memset(x.list_a[:], 0).then_inc(x.act_step, 2)
            dve.memset(x.y_a[:, 0:1], 0.0).then_inc(x.y_out[0], 16)
            dve.memset(x.y_b[:, 0:1], 0.0).then_inc(x.y_out[1], 16)
            dve.tensor_copy(x.token[:], g.k[:, K_TOK:K_TOK + 2 * NT]).then_inc(x.ready, 1)
            x.dve_find(dve, 0, 0)
            x.dve_list(dve, 0)
            with dve.Fori(0, E) as e:
                x.dve_find(dve, e + 1, e + 1)
                for c in range(4):
                    x.dve_gate_up(dve, e, e, c)
                    if c == 0:
                        x.dve_list(dve, e + 1)
                    x.dve_keep_y(dve, e, 8 * e + 4, c)
            for q in range(4):
                x.dve_keep_y(dve, E, 8 * E + 4, q)

            def body(n, r, e):
                m, fill = n + E, 8 * n + 8 * (E + 1)
                x.dve_find(dve, n + E + 1, e)
                x.dve_list(dve, n + E + 1)
                for c in range(4):
                    x.dve_gate_up(dve, m, e, c)
                for q in range(4):
                    x.dve_keep_y(dve, n + E + 1, fill + 4, q)

            def shift(r):
                dve.wait_ge(x.filled, 16 * r)
                dve.tensor_scalar(g.place[:], g.place[:], -float(CAP), None, ALU.add).then_inc(x.shifted, 1)
                dve.wait_ge(x.shifted, r).then_inc(x.shift_seen, 1)

            overflow(dve, body, shift)


def finish(nc, g, sem):
    with ExitStack() as ph:
        def sb(name, shape, dt=F32):
            return ph.enter_context(nc.sbuf_tensor("fi_" + name, shape, dt))

        w_gate = g.ring[:, 0:4].rearrange("p s n -> p (s n)").rearrange("p (k n) -> p k n", k=KT)
        w_proj = g.ring[:, 4].rearrange("p (k n) -> p k n", k=2)
        post, final = g.ring[:, 5, 0:D], g.ring[:, 5, D:2 * D]
        y = sb("rows", [P, 2, TOPK, D])
        xs = sb("xs", [P, 2, D])
        hT = sb("hT", [P, KT, P])
        pt = sb("p", [P, 2, PLE])
        pT = sb("pT", [P, 2, P])
        pe_n = sb("pe_normed", [P, 2, D])
        sig = sb("sigmoid", [P, D])
        junk = sb("junk", [P, D])
        stat = sb("stat", [P, 6, NT])
        ps = ph.enter_context(nc.psum_tensor("fi_psum", [P, 8, HALF], F32))
        ident = g.k[:, K_ID:K_ID + P]
        p_dram = g.p.rearrange("a b (t p) d -> (a b t) p d", p=P)
        out_dram = g.out.rearrange("a (t p) d -> (a t) p d", p=P)

        w_in_s, bc_in = sem("weights_in"), sem("gains_in")
        p_in, y_in, out_s = [sem(f"p_in{i}") for i in range(2)], [sem(f"rows_in{i}") for i in range(2)], [sem(f"out{i}") for i in range(2)]
        mixed, sq, root, inv, scaled, turned, kept, gated = (sem(n) for n in (
            "mixed", "squares", "roots", "inverses", "scaled", "turned", "kept", "gate_products"))
        p_turned, p_kept, proj, pe_sq, pe_root, pe_inv, pe_done = (sem(n) for n in (
            "p_turned", "p_kept", "projected", "pe_squares", "pe_roots", "pe_inverses", "pe_normed"))
        sig_done, gate_mul, added, o_sq, o_root, o_inv, o_done = (sem(n) for n in (
            "sigmoid", "gate_mul", "added", "out_squares", "out_roots", "out_inverses", "out_normed"))
        block = ph.enter_context(nc.Block())

        @block.sync
        def _(sp):
            sp.dma_start(w_proj, g.w_ple_proj.rearrange("a (k p) n -> p (a k) n", p=P)).then_inc(w_in_s, 16)
            for t in range(2):
                sp.dma_start(pt[:, t], p_dram[t]).then_inc(p_in[t], 16)
            sp.dma_start(w_gate, g.w_ple_gate.rearrange("a (k p) n -> p (a k) n", p=P)).then_inc(w_in_s, 16)
            sp.dma_start(post, g.g_ple_post.rearrange("a d -> (a d)").partition_broadcast(P)).then_inc(bc_in, 16)
            sp.dma_start(final, g.g_final.partition_broadcast(P)).then_inc(bc_in, 16)
            for t in range(2, NT + 2):
                if t < NT:
                    sp.wait_ge(p_turned, t - 1)
                    sp.dma_start(pt[:, t % 2], p_dram[t]).then_inc(p_in[t % 2], 16)
                n = t - 2
                sp.wait_ge(o_done, n + 1)
                sp.dma_start(out_dram[n], xs[:, n % 2]).then_inc(out_s[n % 2], 16)
            for s in out_s:
                sp.wait_ge(s, 16 * NT // 2)

        @block.gpsimd
        def _(pool):
            def gather_rows(source):
                for t in range(NT):
                    if t >= 2:
                        pool.wait_ge(mixed, TOPK * (t - 1))
                    for k in range(TOPK):
                        pool.indirect_dma_start(out=y[:, t % 2, k, :], out_offset=None, in_=source,
                                                in_offset=bass.IndirectOffsetOnAxis(ap=g.slot[:, t, k:k + 1], axis=0)).then_inc(y_in[t % 2], 16)

            most = pool.value_load(g.count[0:1, E:E + 1], min_val=0, max_val=T)
            with pool.If(most <= CAP):
                gather_rows(g.y_dram[0:Y_FIRST, :])
            with pool.Else():
                gather_rows(g.y_dram)
            for s in y_in:
                pool.wait_ge(s, 16 * TOPK * NT // 2)

        @block.tensor
        def _(pe):
            def embed(t):
                pe.wait_ge(p_in[t % 2], 16 * (t // 2 + 1))
                if t >= 1:
                    pe.wait_ge(p_kept, t)
                for k in range(2):
                    mm = pe.transpose(ps[:, 6, k * P:(k + 1) * P], pt[:, t % 2, k * P:(k + 1) * P], ident)
                mm.then_inc(p_turned, 1)
                pe.wait_ge(p_kept, t + 1)
                if t >= 1:
                    pe.wait_ge(pe_done, t)
                for half in range(2):
                    for k in range(2):
                        mm = pe.matmul(ps[:, 4 + half, :], pT[:, k, :], w_proj[:, k, half * HALF:(half + 1) * HALF], start=(k == 0), stop=(k == 1))
                mm.then_inc(proj, 1)

            def gate(t):
                pe.wait_ge(scaled, t + 1)
                for q in range(2):
                    pe.wait_ge(p_kept, min(t + 2, NT))
                    if 2 * t + q >= 1:
                        pe.wait_ge(kept, 2 * t + q)
                    for i in range(4):
                        mm = pe.transpose(ps[:, 7, i * P:(i + 1) * P], xs[:, t % 2, (4 * q + i) * P:(4 * q + i + 1) * P], ident)
                    mm.then_inc(turned, 1)
                pe.wait_ge(kept, 2 * t + 2)
                if t >= 2:
                    pe.wait_ge(sig_done, t - 1)
                for half in range(2):
                    for k in range(KT):
                        mm = pe.matmul(ps[:, 2 * (t % 2) + half, :], hT[:, k, :], w_gate[:, k, half * HALF:(half + 1) * HALF],
                                       start=(k == 0), stop=(k == KT - 1))
                mm.then_inc(gated, 1)

            pe.wait_ge(w_in_s, 32)
            embed(0)
            for t in range(NT):
                if t + 1 < NT:
                    embed(t + 1)
                gate(t)

        @block.scalar
        def _(act):
            def embed(t):
                act.wait_ge(p_turned, t + 1)
                if t >= 1:
                    act.wait_ge(proj, t)
                act.copy(pT[:], ps[:, 6, 0:2 * P].rearrange("p (k c) -> p k c", k=2)).then_inc(p_kept, 1)
                act.wait_ge(proj, t + 1)
                act.activation(junk[:], ps[:, 4:6, :].rearrange("p a c -> p (a c)"), ACT.Square, accum_out=stat[:, 0, t:t + 1]).then_inc(pe_sq, 1)
                act.wait_ge(pe_sq, t + 1)
                act.activation(stat[:, 1, t:t + 1], stat[:, 0, t:t + 1], ACT.Sqrt, scale=1.0 / D, bias=g.eps[:, 0:1]).then_inc(pe_root, 1)

            def tokens(t):
                act.wait_ge(mixed, TOPK * (t + 1))
                act.activation(junk[:], g.h[:, t, :], ACT.Square, accum_out=stat[:, 2, t:t + 1]).then_inc(sq, 1)
                act.wait_ge(sq, t + 1)
                act.activation(stat[:, 3, t:t + 1], stat[:, 2, t:t + 1], ACT.Sqrt, scale=1.0 / D, bias=g.eps[:, 0:1]).then_inc(root, 1)
                for q in range(2):
                    act.wait_ge(turned, 2 * t + q + 1)
                    if t >= 1:
                        act.wait_ge(gated, t)
                    for i in range(4):
                        k = 4 * q + i
                        ins = act.activation(hT[:, k, :], ps[:, 7, i * P:(i + 1) * P], ACT.Copy, scale=g.par[:, R_PLE + k:R_PLE + k + 1])
                    ins.then_inc(kept, 1)

            def last(t):
                act.wait_ge(gated, t + 1)
                if t >= 1:
                    act.wait_ge(gate_mul, t)
                act.activation(sig[:], ps[:, 2 * (t % 2):2 * (t % 2) + 2, :].rearrange("p a c -> p (a c)"), ACT.Sigmoid).then_inc(sig_done, 1)
                act.wait_ge(added, t + 1)
                act.activation(junk[:], g.h[:, t, :], ACT.Square, accum_out=stat[:, 4, t:t + 1]).then_inc(o_sq, 1)
                act.wait_ge(o_sq, t + 1)
                act.activation(stat[:, 5, t:t + 1], stat[:, 4, t:t + 1], ACT.Sqrt, scale=1.0 / D, bias=g.eps[:, 0:1]).then_inc(o_root, 1)

            embed(0)
            for t in range(NT):
                if t + 1 < NT:
                    embed(t + 1)
                tokens(t)
                if t >= 1:
                    last(t - 1)
            last(NT - 1)

        @block.vector
        def _(dve):
            dve.wait_ge(bc_in, 32)

            def embed(t):
                dve.wait_ge(pe_root, t + 1)
                dve.reciprocal(stat[:, 1, t:t + 1], stat[:, 1, t:t + 1]).then_inc(pe_inv, 1)
                dve.wait_ge(pe_inv, t + 1)
                dve.scalar_tensor_tensor(out=pe_n[:, t % 2], in0=ps[:, 4:6, :].rearrange("p a c -> p (a c)"), scalar=stat[:, 1, t:t + 1],
                                         in1=post, op0=ALU.mult, op1=ALU.mult).then_inc(pe_done, 1)

            def tokens(t):
                dve.wait_ge(y_in[t % 2], 16 * TOPK * (t // 2 + 1))
                for k in range(TOPK):
                    if k >= 1:
                        dve.wait_ge(mixed, TOPK * t + k)
                    dve.scalar_tensor_tensor(out=g.h[:, t, :], in0=y[:, t % 2, k, :], scalar=g.share[:, t, k:k + 1], in1=g.h[:, t, :],
                                             op0=ALU.mult, op1=ALU.add).then_inc(mixed, 1)
                dve.wait_ge(root, t + 1)
                dve.reciprocal(stat[:, 3, t:t + 1], stat[:, 3, t:t + 1]).then_inc(inv, 1)
                dve.wait_ge(inv, t + 1)
                if t >= 2:
                    dve.wait_ge(out_s[t % 2], 16 * (t // 2))
                dve.tensor_scalar(xs[:, t % 2], g.h[:, t, :], stat[:, 3, t:t + 1], None, ALU.mult).then_inc(scaled, 1)

            def last(t):
                dve.wait_ge(sig_done, t + 1)
                dve.tensor_tensor(pe_n[:, t % 2], pe_n[:, t % 2], sig[:], ALU.mult).then_inc(gate_mul, 1)
                dve.wait_ge(gate_mul, t + 1)
                dve.tensor_tensor(g.h[:, t, :], g.h[:, t, :], pe_n[:, t % 2], ALU.add).then_inc(added, 1)
                dve.wait_ge(o_root, t + 1)
                dve.reciprocal(stat[:, 5, t:t + 1], stat[:, 5, t:t + 1]).then_inc(o_inv, 1)
                dve.wait_ge(o_inv, t + 1)
                dve.scalar_tensor_tensor(out=xs[:, t % 2], in0=g.h[:, t, :], scalar=stat[:, 5, t:t + 1], in1=final,
                                         op0=ALU.mult, op1=ALU.mult).then_inc(o_done, 1)

            embed(0)
            for t in range(NT):
                tokens(t)
                if t >= 1:
                    last(t - 1)
                if t + 1 < NT:
                    embed(t + 1)
            last(NT - 1)


_INS = ["x", "p", "g_mix", "w_in", "w_gla_gate", "b_gla_gate", "g_gla_out", "w_conv", "gdn_a_log", "gdn_dt_bias", "g_gdn_out",
        "w_out", "g_moe", "w_router", "b_router", "w_gate_up", "b_gate_up", "w_down", "b_down", "g_ple_in", "w_ple_gate",
        "w_ple_proj", "g_ple_post", "g_final"]


class Names:
    pass


def program(nc, arrays, out):
    g = Names()
    g.x = arrays["x"].rearrange("a t d -> (a t) d")
    g.w_in = arrays["w_in"].rearrange("a k n -> (a k) n")
    g.w_conv = arrays["w_conv"].rearrange("a k n -> a (k n)")
    g.w_gate_up = arrays["w_gate_up"].rearrange("a e k n -> (a e) k n")
    g.w_down = arrays["w_down"].rearrange("a e k n -> (a e) k n")
    g.p, g.g_mix, g.w_gla_gate, g.b_gla_gate = arrays["p"], arrays["g_mix"], arrays["w_gla_gate"], arrays["b_gla_gate"]
    g.g_gla_out, g.gdn_a_log, g.gdn_dt_bias, g.g_gdn_out = arrays["g_gla_out"], arrays["gdn_a_log"], arrays["gdn_dt_bias"], arrays["g_gdn_out"]
    g.w_out, g.g_moe, g.w_router, g.b_router = arrays["w_out"], arrays["g_moe"], arrays["w_router"], arrays["b_router"]
    g.b_gate_up, g.b_down, g.g_ple_in, g.w_ple_gate = arrays["b_gate_up"], arrays["b_down"], arrays["g_ple_in"], arrays["w_ple_gate"]
    g.w_ple_proj, g.g_ple_post, g.g_final, g.consts = arrays["w_ple_proj"], arrays["g_ple_post"], arrays["g_final"], arrays["consts"]
    g.out = out
    g.gates_dram = nc.dram_tensor("gates_dram", (2, T, HALF), F32).ap()
    g.xn_dram = nc.dram_tensor("xn_dram", (T, D), F32).ap()
    g.y_dram = nc.dram_tensor("y_dram", (Y_FIRST + (ROUNDS - 1) * Y_ROUND, D), F32).ap()
    with ExitStack() as ctx:
        def sb(name, shape, dt=F32):
            return ctx.enter_context(nc.sbuf_tensor(name, shape, dt))

        g.k = sb("constants", [P, K_END])
        g.eps = sb("eps", [P, 1])
        g.par = sb("parameter_columns", [P, R_END])
        g.setup_done = ctx.enter_context(nc.semaphore("setup_done"))
        g.w_in_ring = [ctx.enter_context(nc.semaphore(f"expert_weights_in{i}")) for i in range(12)]
        with ExitStack() as mixed:
            with ExitStack() as mixers:
                g.dab = mixers.enter_context(nc.sbuf_tensor("dab", [P, NT, 8], F32))
                g.qkvT = mixers.enter_context(nc.sbuf_tensor("qkvT", [P, NQKV, T], F32))
                with ExitStack() as gl:
                    g.gqkT = gl.enter_context(nc.sbuf_tensor("gqkT", [P, 4, T], F32))
                    g.glrT = gl.enter_context(nc.sbuf_tensor("glrT", [16, T], F32))
                    g.gv = gl.enter_context(nc.sbuf_tensor("gv", [P, NT, HALF], F32))
                    with stage_signals(nc, "project") as sem:
                        project(nc, g, sem)
                    g.mixA = mixed.enter_context(nc.sbuf_tensor("mixed_gla", [P, NH, T], F32, side="right"))
                    with stage_signals(nc, "gla") as sem:
                        gla(nc, g, sem)
                g.mixB = mixed.enter_context(nc.sbuf_tensor("mixed_delta", [P, NH, T], F32, side="right"))
                with stage_signals(nc, "delta") as sem:
                    delta(nc, g, sem)
            g.h = sb("h", [P, NT, D])
            g.ring = sb("weight_ring", [P, 12, 2 * D])
            g.place = sb("place", [P, NT, E + 1])
            g.slot = sb("slot", [P, NT, TOPK], U32)
            g.share = sb("share", [P, NT, TOPK])
            g.count = sb("count", [P, E + 1], I32)
            g.b_gu = sb("bias_gate_up", [P, E, 2 * FF // P])
            g.b_dn = sb("bias_down", [P, E, D // P])
            with stage_signals(nc, "route") as sem:
                route(nc, g, sem)
        with stage_signals(nc, "experts") as sem:
            experts(nc, g, sem)
        with stage_signals(nc, "finish") as sem:
            finish(nc, g, sem)


def kernel(**inputs):
    import numpy as _np
    import concourse.bacc as _bacc
    from concourse import mybir as _mybir
    from concourse.bass_utils import run_bass_kernel_spmd as _run

    nc = _bacc.Bacc("TRN2", target_bir_lowering=False, num_devices=1)
    arrays, aps = {}, {}
    given = {name: _np.ascontiguousarray(inputs[name]) for name in _INS}
    given["consts"] = constants()
    for name, a in given.items():
        arrays[f"in_{name}"] = a
        aps[name] = nc.dram_tensor(f"in_{name}", a.shape, _mybir.dt.from_np(a.dtype), kind="ExternalInput").ap()
    out = nc.dram_tensor("out", (1, T, D), F32, kind="ExternalOutput").ap()
    program(nc, aps, out)
    r = _run(nc, [arrays], core_ids=[0])
    return r.results[0]["out"]
```

```python
from contextlib import ExitStack, contextmanager

import numpy as np
import concourse.bass as bass
from concourse import mybir

F32 = mybir.dt.float32
F32R = mybir.dt.float32r
BF16 = mybir.dt.bfloat16
I32 = mybir.dt.int32
U32 = mybir.dt.uint32
ALU = mybir.AluOpType
ACT = mybir.ActivationFunctionType
AX = mybir.AxisListType

P = 128
T, D = 1024, 1024
NT, KT = T // P, D // P
C = 64
NC = T // C
NH = 4
GK = 64
PLE = 256
E, TOPK, FF = 32, 4, 1024
EPS = 1e-6
HALF = 512

C_GQK, C_GV, C_GR, C_GLR, C_QKV, C_DZ, C_DAB = 0, 512, 1024, 1536, 1552, 3088, 3600
NQKV = 12
TAPS = 4

CAP = 192
ROUNDS = -(-T // CAP)
Y_FIRST, Y_ROUND = (E + 1) * CAP, E * CAP
LEVELS = 6
K_ID, K_TRI, K_CHUNK, K_HALF, K_STRICT, K_ONES, K_LEVEL = 0, 128, 256, 384, 640, 768, 896
K_IOTA = K_LEVEL + LEVELS * P
K_TOK = K_IOTA + CAP
K_SLOT = K_TOK + 2 * NT
K_E = K_SLOT + E
K_END = K_E + E
R_MIX, R_PLE, R_BG, R_GLA, R_GDN, R_CONV = 0, 8, 16, 18, 19, 20
R_END = R_CONV + TAPS * NQKV


def constants():
    i = np.arange(P)
    same = (i[:, None] // C) == (i[None, :] // C)
    k = np.zeros((P, K_END), np.float32)
    k[:, K_ID:K_ID + P] = np.eye(P)
    k[:, K_TRI:K_TRI + P] = same & (i[:, None] <= i[None, :])
    k[:, K_CHUNK:K_CHUNK + P] = same
    for r in range(2):
        k[:, K_HALF + r * P:K_HALF + (r + 1) * P] = (i[:, None] // C) == r
    k[:, K_STRICT:K_STRICT + P] = i[:, None] < i[None, :]
    k[:, K_ONES:K_ONES + P] = 1.0
    for l in range(LEVELS):
        m = 1 << l
        block = (i[:, None] // (2 * m)) == (i[None, :] // (2 * m))
        k[:, K_LEVEL + l * P:K_LEVEL + (l + 1) * P] = block & (i[:, None] % (2 * m) < m) & (i[None, :] % (2 * m) >= m)
    k[:, K_IOTA:K_IOTA + CAP] = np.arange(CAP)
    for t in range(NT):
        k[:, K_TOK + 2 * t] = t * P
        k[:, K_TOK + 2 * t + 1] = i
    k[:, K_SLOT:K_SLOT + E] = (np.arange(E) + 1) * CAP
    k[:, K_E:K_E + E] = np.arange(E)
    return k


@contextmanager
def stage_signals(nc, stage):
    sems = []

    def sem(name):
        sems.append(nc.alloc_semaphore(name=f"{stage}_{name}"))
        return sems[-1]

    yield sem
    nc.clear_and_free_semaphores(sems)
    nc.all_engine_barrier()


def project(nc, g, sem):
    WAYS = [("gqk", j, h) for h in range(2) for j in range(4)] + [("glr", 0, h) for h in range(2)]
    WAYS += [("qkv", j, h) for j in range(NQKV) for h in range(2)] + [("dab", 0, 0)]
    WAYS += [(kind, 0, t) for kind in ("gv", "gr", "dz") for t in range(NT)]
    BANKS = 6
    CHUNK_COLS = [C_GQK, C_QKV, C_QKV + HALF, C_QKV + 2 * HALF, C_GV, C_GR, C_DZ]

    def chunk_of(kind, j):
        return {"gqk": 0, "qkv": 1 + j // 4, "gv": 4, "gr": 5, "dz": 6}.get(kind)

    last_unit = {}
    for u, (kind, j, _) in enumerate(WAYS):
        if chunk_of(kind, j) is not None:
            last_unit[chunk_of(kind, j)] = u
    act_units = [u for u, w in enumerate(WAYS) if w[0] not in ("gr", "dz")]
    dve_units = [u for u, w in enumerate(WAYS) if w[0] in ("gr", "dz")]

    with ExitStack() as ph:
        def sb(name, shape, dt=F32):
            return ph.enter_context(nc.sbuf_tensor(name, shape, dt))

        nT = sb("nT", [P, KT, T])
        w = sb("w_in_chunks", [P, 2, KT, HALF])
        w_small = sb("w_in_small", [P, KT, 24])
        work = sb("project_work", [P, 6, T + 4])
        par_rows = sb("par_rows", [R_END, P])
        stat = sb("norm_stat", [P, 3, NT])
        ps = ph.enter_context(nc.psum_tensor("project_psum", [P, 8, HALF], F32))

        x_in = [sem(f"x_in{i}") for i in range(2)]
        w_in_s = [sem(f"w_chunk{i}") for i in range(2)]
        small_in, consts_in, par_in = sem("w_small_in"), sem("consts_in"), sem("par_in")
        squared, mean_done, root_done, rs_done, scaled = (sem(n) for n in ("squared", "mean_done", "root_done", "rs_done", "scaled"))
        turned, norm_ready, par_turned, par_ready = (sem(n) for n in ("x_turned", "norm_ready", "par_turned", "par_ready"))
        unit_done, act_emptied, dve_emptied = sem("unit_done"), sem("act_emptied"), sem("dve_emptied")
        pad_ready, tap_done, sig_done, silu_done = (sem(n) for n in ("pad_ready", "tap_done", "conv_sigmoid", "silu_done"))
        sq_done, ss_done, l2_root, l2_inv, l2_done = (sem(n) for n in ("l2_squares", "l2_sums", "l2_root", "l2_inverse", "l2_done"))
        gate_sig, gate_out = sem("gate_sigmoid"), [sem(f"gate_out{i}") for i in range(2)]

        ident = g.k[:, K_ID:K_ID + P]
        xt = [work[:, i, 0:D] for i in range(2)]
        xs = [work[:, 2 + i, 0:D] for i in range(2)]
        junk = work[:, 4, 0:D]
        raw = [work[:, i, :] for i in range(2)]
        acc = [work[:, 2 + i, 0:T] for i in range(2)]
        sg = work[:, 4, 0:T]
        sq = [work[:, 5, 0:T], work[:, 4, 0:T]]
        rt = [work[:, 2, 0:T], work[:, 3, 0:T]]
        gate = [work[:, i, 0:HALF] for i in range(2)]
        gsig = [work[:, i, HALF:2 * HALF] for i in range(2)]
        w_dram = g.w_in.rearrange("(k p) n -> p k n", p=P)
        x_dram = g.x.rearrange("(t p) d -> t p d", p=P)
        block = ph.enter_context(nc.Block())

        @block.sync
        def _(sp):
            def chunk(c):
                if c >= 2:
                    sp.wait_ge(unit_done, last_unit[c - 2] + 1)
                sp.dma_start(w[:, c % 2], w_dram[:, :, CHUNK_COLS[c]:CHUNK_COLS[c] + HALF]).then_inc(w_in_s[c % 2], 16)

            def x_tile(t):
                if t >= 2:
                    sp.wait_ge(squared, t - 1)
                    sp.wait_ge(scaled, t - 1)
                sp.dma_start(xt[t % 2], x_dram[t]).then_inc(x_in[t % 2], 16)

            x_tile(0)
            sp.dma_start(g.k[:], g.consts).then_inc(consts_in, 16)
            x_tile(1)
            for (row, src, n) in ((R_MIX, g.g_mix, 8), (R_PLE, g.g_ple_in, 8), (R_BG, g.b_gla_gate, 2), (R_GLA, g.g_gla_out, 1),
                                  (R_GDN, g.g_gdn_out, 1), (R_CONV, g.w_conv, TAPS * NQKV)):
                sp.dma_start(par_rows[row:row + n, :], src.rearrange("a (r p) -> (a r) p", p=P)).then_inc(par_in, 16)
            chunk(0)
            for t in range(2, NT):
                x_tile(t)
            with nc.allow_non_contiguous_dma(reason="24 narrow columns of w_in"):
                sp.dma_start(w_small[:, :, 0:16], w_dram[:, :, C_GLR:C_GLR + 16]).then_inc(small_in, 16)
                sp.dma_start(w_small[:, :, 16:24], w_dram[:, :, C_DAB:C_DAB + 8]).then_inc(small_in, 16)
            for c in range(1, 7):
                chunk(c)

        @block.gpsimd
        def _(pool):
            for n, u in enumerate(dve_units):
                kind, _, t = WAYS[u]
                pool.wait_ge(dve_emptied, n + 1)
                dst = g.gates_dram[0 if kind == "gr" else 1].rearrange("(t p) d -> t p d", p=P)[t]
                pool.dma_start(dst, gate[n % 2]).then_inc(gate_out[n % 2], 16)
            for s in gate_out:
                pool.wait_ge(s, 16 * NT)

        @block.tensor
        def _(pe):
            def turn_tile(t):
                pe.wait_ge(scaled, t + 1)
                for q in range(2):
                    n = 2 * t + q
                    if n >= 2:
                        pe.wait_ge(norm_ready, n - 1)
                    for i in range(4):
                        k = 4 * q + i
                        mm = pe.transpose(ps[:, q, i * P:(i + 1) * P], xs[t % 2][:, k * P:(k + 1) * P], ident)
                    mm.then_inc(turned, 1)

            def unit(u):
                kind, j, part = WAYS[u]
                bank = 2 + u % BANKS
                if u >= BANKS:
                    before = u - BANKS
                    if before in act_units:
                        pe.wait_ge(act_emptied, act_units.index(before) + 1)
                    else:
                        pe.wait_ge(dve_emptied, dve_units.index(before) + 1)
                c = chunk_of(kind, j)
                if c is not None:
                    pe.wait_ge(w_in_s[c % 2], 16 * (c // 2 + 1))
                else:
                    pe.wait_ge(small_in, 32)
                if kind in ("gqk", "glr", "qkv"):
                    pe.wait_ge(norm_ready, 8 * (part + 1))
                    M = 16 if kind == "glr" else P
                    for k in range(KT):
                        lhs = w_small[:, k, 0:16] if kind == "glr" else w[:, c % 2, k, (j % 4) * P:(j % 4 + 1) * P]
                        mm = pe.matmul(ps[0:M, bank, :], lhs, nT[:, k, part * HALF:(part + 1) * HALF],
                                       start=(k == 0), stop=(k == KT - 1))
                elif kind == "dab":
                    for t in range(NT):
                        for k in range(KT):
                            mm = pe.matmul(ps[:, bank, 8 * t:8 * t + 8], nT[:, k, t * P:(t + 1) * P], w_small[:, k, 16:24],
                                           start=(k == 0), stop=(k == KT - 1))
                else:
                    for k in range(KT):
                        mm = pe.matmul(ps[:, bank, :], nT[:, k, part * P:(part + 1) * P], w[:, c % 2, k, :],
                                       start=(k == 0), stop=(k == KT - 1))
                mm.then_inc(unit_done, 1)

            def l2_sums(j):
                pe.wait_ge(sq_done, j + 1)
                for h in range(2):
                    if j >= 1:
                        pe.wait_ge(l2_root, 2 * (j - 1) + h + 1)
                    pe.matmul(ps[:, h, :], g.k[:, K_ONES:K_ONES + P], sq[j % 2][:, h * HALF:(h + 1) * HALF],
                              start=True, stop=True).then_inc(ss_done, 1)

            pe.wait_ge(consts_in, 16)
            pe.wait_ge(par_in, 16 * 6)
            pe.transpose(ps[:, 2, 0:R_END], par_rows[:], g.k[0:R_END, K_ID:K_ID + R_END]).then_inc(par_turned, 1)
            for t in range(4):
                turn_tile(t)
            pe.wait_ge(par_ready, 1)
            for u in range(4):
                unit(u)
            for t in range(4, NT):
                turn_tile(t)
            first_gv = WAYS.index(("gv", 0, 0))
            for u in range(4, len(WAYS)):
                unit(u)
                if first_gv + 2 <= u < first_gv + 10:
                    l2_sums(u - first_gv - 2)

        @block.scalar
        def _(act):
            def x_square(t):
                act.wait_ge(x_in[t % 2], 16 * (t // 2 + 1))
                act.activation(junk, xt[t % 2], ACT.Square, accum_out=stat[:, 0, t:t + 1]).then_inc(squared, 1)

            x_square(0)
            for t in range(NT):
                act.wait_ge(mean_done, t + 1)
                act.activation(stat[:, 1, t:t + 1], stat[:, 2, t:t + 1], ACT.Sqrt).then_inc(root_done, 1)
                if t + 1 < NT:
                    x_square(t + 1)

            def l2_square(j):
                act.wait_ge(silu_done, j + 1)
                act.wait_ge(silu_done, NQKV)
                if j >= 2:
                    act.wait_ge(ss_done, 2 * (j - 1))
                act.activation(sq[j % 2], g.qkvT[:, j, :], ACT.Square).then_inc(sq_done, 1)

            def l2_roots(j):
                if j >= 2:
                    act.wait_ge(l2_done, j - 1)
                for h in range(2):
                    act.wait_ge(ss_done, 2 * j + h + 1)
                    act.activation(rt[j % 2][:, h * HALF:(h + 1) * HALF], ps[:, h, :], ACT.Sqrt,
                                   bias=g.eps[:, 0:1]).then_inc(l2_root, 1)

            def conv_sigmoid(j):
                act.wait_ge(tap_done, TAPS * (j + 1))
                if j >= 1:
                    act.wait_ge(silu_done, j)
                act.activation(sg, acc[j % 2], ACT.Sigmoid).then_inc(sig_done, 1)

            act.wait_ge(g.setup_done, 1)
            gates = 0
            for u, (kind, j, part) in enumerate(WAYS):
                bank = 2 + u % BANKS
                src = ps[:, bank, :]
                act.wait_ge(unit_done, u + 1)
                cols = slice(part * HALF, (part + 1) * HALF)
                if kind == "gqk":
                    act.activation(g.gqkT[:, j, cols], src, ACT.Copy,
                                   scale=GK ** -0.5 if j < 2 else 1.0).then_inc(act_emptied, 1)
                elif kind == "glr":
                    act.copy(g.glrT[:, cols], ps[0:16, bank, :]).then_inc(act_emptied, 1)
                elif kind == "qkv":
                    if part == 0:
                        if j >= 2:
                            act.wait_ge(tap_done, TAPS * (j - 1))
                        else:
                            act.wait_ge(pad_ready, 2)
                    act.copy(raw[j % 2][:, 3 + part * HALF:3 + (part + 1) * HALF], src).then_inc(act_emptied, 1)
                    if part == 0 and j >= 1:
                        conv_sigmoid(j - 1)
                elif kind == "dab":
                    act.copy(g.dab[:], ps[:, bank, 0:8 * NT].rearrange("p (t c) -> p t c", t=NT)).then_inc(act_emptied, 1)
                    conv_sigmoid(NQKV - 1)
                    l2_square(0)
                    l2_square(1)
                elif kind == "gv":
                    act.copy(g.gv[:, part, :], src).then_inc(act_emptied, 1)
                    if part >= 2:
                        l2_roots(part - 2)
                        l2_square(part)
                else:
                    if kind == "gr" and part < 2:
                        l2_roots(part + 6)
                    if gates >= 2:
                        act.wait_ge(dve_emptied, gates - 1)
                    act.activation(gsig[gates % 2], src, ACT.Sigmoid).then_inc(gate_sig, 1)
                    gates += 1

        @block.vector
        def _(dve):
            dve.memset(g.eps[:], EPS).then_inc(g.setup_done, 1)
            def keep_norm(t):
                for q in range(2):
                    dve.wait_ge(turned, 2 * t + q + 1)
                    dve.tensor_tensor(nT[:, 4 * q:4 * q + 4, t * P:(t + 1) * P], ps[:, q, :].rearrange("p (k c) -> p k c", k=4),
                                      g.par[:, R_MIX + 4 * q:R_MIX + 4 * q + 4].unsqueeze(2).to_broadcast([P, 4, P]),
                                      ALU.mult).then_inc(norm_ready, 1)

            for t in range(NT):
                dve.wait_ge(squared, t + 1)
                dve.tensor_scalar(stat[:, 2, t:t + 1], stat[:, 0, t:t + 1], 1.0 / D, EPS, ALU.mult, ALU.add).then_inc(mean_done, 1)
                dve.wait_ge(root_done, t + 1)
                dve.reciprocal(stat[:, 1, t:t + 1], stat[:, 1, t:t + 1]).then_inc(rs_done, 1)
                dve.wait_ge(rs_done, t + 1)
                if t >= 2:
                    dve.wait_ge(turned, 2 * (t - 1))
                dve.tensor_scalar(xs[t % 2], xt[t % 2], stat[:, 1, t:t + 1], None, ALU.mult).then_inc(scaled, 1)
                if t == 0:
                    dve.wait_ge(par_turned, 1)
                    dve.tensor_copy(g.par[:], ps[:, 2, 0:R_END]).then_inc(par_ready, 1)
                    dve.wait_ge(par_ready, 1)
                else:
                    keep_norm(t - 1)
            keep_norm(NT - 1)

            for i in range(2):
                dve.memset(raw[i][:, 0:3], 0.0).then_inc(pad_ready, 1)
            for j in range(NQKV):
                for tap in range(TAPS):
                    col = g.par[:, R_CONV + tap * NQKV + j:R_CONV + tap * NQKV + j + 1]
                    seen = raw[j % 2][:, tap:tap + T]
                    if tap == 0:
                        dve.wait_ge(act_emptied, act_units.index(WAYS.index(("qkv", j, 1))) + 1)
                        dve.tensor_scalar(acc[j % 2], seen, col, None, ALU.mult).then_inc(tap_done, 1)
                    else:
                        dve.wait_ge(tap_done, TAPS * j + tap)
                        dve.scalar_tensor_tensor(out=acc[j % 2], in0=seen, scalar=col, in1=acc[j % 2],
                                                 op0=ALU.mult, op1=ALU.add).then_inc(tap_done, 1)
                dve.wait_ge(sig_done, j + 1)
                dve.tensor_tensor(g.qkvT[:, j, :], acc[j % 2], sg, ALU.mult).then_inc(silu_done, 1)

            def l2_scale(j):
                dve.wait_ge(l2_root, 2 * (j + 1))
                dve.reciprocal(rt[j % 2], rt[j % 2]).then_inc(l2_inv, 1)
                dve.wait_ge(l2_inv, j + 1)
                dve.scalar_tensor_tensor(out=g.qkvT[:, j, :], in0=g.qkvT[:, j, :], scalar=P ** -0.5 if j < NH else 1.0,
                                         in1=rt[j % 2], op0=ALU.mult, op1=ALU.mult).then_inc(l2_done, 1)

            def gate_product(n):
                u = dve_units[n]
                dve.wait_ge(gate_sig, n + 1)
                if n >= 2:
                    dve.wait_ge(gate_out[n % 2], 16 * (n // 2))
                dve.tensor_tensor(gate[n % 2], ps[:, 2 + u % BANKS, :], gsig[n % 2], ALU.mult).then_inc(dve_emptied, 1)

            for j in range(6):
                l2_scale(j)
            for n in range(2 * NT):
                if n < 2:
                    l2_scale(6 + n)
                gate_product(n)


def gla(nc, g, sem):
    STEPS = [("diag", p) for p in range(2)] + [(l, p) for l in range(LEVELS) for p in range(2)]

    with ExitStack() as ph:
        def sb(name, shape, dt=F32):
            return ph.enter_context(nc.sbuf_tensor(name, shape, dt))

        w_gate = sb("w_gla_gate", [16, 2 * P])
        b = sb("gla_b", [P, 2, T])
        A = sb("gla_scores", [P, NH, NT, P])
        dist = sb("gla_dist", [P, 2, T])
        Q = sb("gla_q_level", [P, 2, T])
        K = sb("gla_k_level", [P, 2, T])
        qe = sb("gla_q_decayed", [P, NH, T])
        kdn = sb("gla_k_decayed", [P, NT, 2 * P])
        S = sb("gla_states", [P, 2, NC, P])
        dec = sb("gla_chunk_decay", [P, 2, NC])
        stat = sb("gla_stat", [P, 2, NT, NH])
        gate = sb("gla_gate_in", [P, 2, HALF])
        on = sb("gla_out_normed", [P, 2, HALF])
        one = sb("gla_one", [P, 1])
        ps = ph.enter_context(nc.psum_tensor("gla_psum", [P, 8, HALF], F32))

        wg_in, gate_in = sem("w_gate_in"), [sem(f"gate_in{i}") for i in range(2)]
        prep, pre, act_pre, low, logs, run_sum = sem("prepared"), sem("gate_product"), sem("act_softplus"), sem("low"), sem("logs"), sem("running_sum")
        zeroed, dist_done, decay_done, q_done, k_done = sem("zeroed"), sem("distance"), sem("level_decay"), sem("q_level"), sem("k_level")
        score_done, kept = sem("scores"), sem("scores_kept")
        edge_exp, chunk_exp, qe_done, last_dist, kd_done = sem("edge_exp"), sem("chunk_exp"), sem("q_decayed"), sem("last_dist"), sem("k_decayed")
        k_turned, k_natural, added, state_done = sem("k_turned"), sem("k_natural"), sem("state_added"), sem("state_done")
        out_done, squares, roots, inverses, normed, o_turned, o_kept = (sem(n) for n in ("out", "out_squares", "out_roots", "out_inverse", "out_normed", "out_turned", "out_kept"))

        ident = g.k[:, K_ID:K_ID + P]
        block = ph.enter_context(nc.Block())

        def bank_of(step, half, parity):
            return 4 * (step % 2) + 2 * half + parity

        @block.sync
        def _(sp):
            sp.dma_start(w_gate[:], g.w_gla_gate.rearrange("a k n -> (a k) n")).then_inc(wg_in, 16)
            for t in range(NT):
                if t >= 2:
                    sp.wait_ge(normed, NH * (t - 1))
                sp.dma_start(gate[:, t % 2, :], g.gates_dram[0].rearrange("(t p) d -> t p d", p=P)[t]).then_inc(gate_in[t % 2], 16)

        @block.gpsimd
        def _(pool):
            pool.memset(A[:], 0.0).then_inc(zeroed, 1)
            pool.memset(qe[:], 0.0).then_inc(zeroed, 1)
            pool.memset(S[:, :, 0, :], 0.0).then_inc(zeroed, 1)
            for n in range(2, len(STEPS)):
                level, p = STEPS[n]
                pool.wait_ge(decay_done, n - 1)
                if n >= 4:
                    pool.wait_ge(score_done, 4 * (n - 1))
                pool.tensor_tensor(K[:, n % 2, :], g.gqkT[:, 2 + p, :], dist[:, n % 2, :], ALU.mult).then_inc(k_done, 1)

        @block.tensor
        def _(pe):
            pe.wait_ge(wg_in, 16)
            for p in range(2):
                for h in range(2):
                    pe.matmul(ps[:, 4 + 2 * p + h, :], w_gate[:, p * P:(p + 1) * P], g.glrT[:, h * HALF:(h + 1) * HALF],
                              start=True, stop=True).then_inc(pre, 1)
            for n, (level, p) in enumerate(STEPS):
                if n == 1:
                    pe.wait_ge(logs, 2)
                    pe.wait_ge(low, 2)
                if n >= 2:
                    pe.wait_ge(q_done, n - 1)
                    pe.wait_ge(k_done, n - 1)
                    pe.wait_ge(kept, 4 * (n - 1))
                for half in range(2):
                    for parity in range(2):
                        rows = slice(GK * parity, GK * (parity + 1))
                        for i in range(4):
                            t = 4 * half + i
                            cols = slice(t * P, (t + 1) * P)
                            kk, qq = (g.gqkT[rows, 2 + p, cols], g.gqkT[rows, p, cols]) if level == "diag" else (K[rows, n % 2, cols], Q[rows, n % 2, cols])
                            mm = pe.matmul(ps[:, bank_of(n, half, parity), i * P:(i + 1) * P], kk, qq, start=True, stop=True)
                        mm.then_inc(score_done, 1)
            for q in range(4):
                p, half = q // 2, q % 2
                pe.wait_ge(kd_done, p + 1)
                pe.wait_ge(kept, 4 * len(STEPS))
                for i in range(4):
                    t = 4 * half + i
                    mm = pe.transpose(ps[:, q, i * P:(i + 1) * P], K[:, p, t * P:(t + 1) * P], ident)
                mm.then_inc(k_turned, 1)
            for c in range(NC - 1):
                t, r = c // 2, c % 2
                rows = slice(C * r, C * (r + 1))
                if c == 0:
                    pe.wait_ge(k_natural, 4)
                if c >= 4:
                    pe.wait_ge(state_done, 2 * (c - 3))
                for h in range(NH):
                    p, e = h // 2, h % 2
                    mm = pe.matmul(ps[GK * e:GK * (e + 1), c % 4, p * P:(p + 1) * P], kdn[rows, t, p * P + GK * e:p * P + GK * (e + 1)],
                                   g.gv[rows, t, h * P:(h + 1) * P], start=True, stop=True)
                mm.then_inc(added, 1)

            def turn_out(t):
                pe.wait_ge(normed, NH * (t + 1))
                if t >= 2:
                    pe.wait_ge(o_kept, t - 1)
                for h in range(NH):
                    mm = pe.transpose(ps[:, 6 + t % 2, h * P:(h + 1) * P], on[:, t % 2, h * P:(h + 1) * P], ident)
                mm.then_inc(o_turned, 1)

            for t in range(NT):
                if t >= 1:
                    pe.wait_ge(state_done, 2 * min(2 * t + 1, NC - 1))
                else:
                    pe.wait_ge(state_done, 2)
                    pe.wait_ge(qe_done, 4)
                if t >= 2:
                    pe.wait_ge(normed, NH * (t - 1))
                bank = 4 + t % 2
                for h in range(NH):
                    pe.matmul(ps[:, bank, h * P:(h + 1) * P], A[:, h, t, :], g.gv[:, t, h * P:(h + 1) * P],
                              start=(h == 0), stop=False, skip_group_check=True)
                    for r in range(2):
                        mm = pe.matmul(ps[C * r:C * (r + 1), bank, h * P:(h + 1) * P], qe[:, h, t * P + C * r:t * P + C * (r + 1)],
                                       S[:, h // 2, 2 * t + r, :], start=False, stop=(h == NH - 1), skip_group_check=True)
                mm.then_inc(out_done, 1)
                if t >= 1:
                    turn_out(t - 1)
            turn_out(NT - 1)

        @block.scalar
        def _(act):
            act.wait_ge(prep, 1)
            for p in range(2):
                act.wait_ge(pre, 2 * p + 2)
                src = ps[:, 4 + 2 * p:6 + 2 * p, :].rearrange("p a c -> p (a c)")
                act.activation(dist[:, p, :], src, ACT.Abs, bias=g.par[:, R_BG + p:R_BG + p + 1]).then_inc(act_pre, 1)
                act.wait_ge(act_pre, 3 * p + 1)
                act.activation(dist[:, p, :], dist[:, p, :], ACT.Exp, scale=-1.0).then_inc(act_pre, 1)
                act.wait_ge(act_pre, 3 * p + 2)
                act.activation(dist[:, p, :], dist[:, p, :], ACT.Ln, bias=one[:, 0:1]).then_inc(act_pre, 1)
                act.wait_ge(act_pre, 3 * p + 3)
            for n in range(2, len(STEPS)):
                act.wait_ge(dist_done, n - 1)
                act.activation(dist[:, n % 2, :], dist[:, n % 2, :], ACT.Abs).then_inc(edge_exp, 1)
                act.wait_ge(edge_exp, n - 1)
                act.activation(dist[:, n % 2, :], dist[:, n % 2, :], ACT.Exp, scale=-1.0 / 16).then_inc(decay_done, 1)
            act.wait_ge(q_done, len(STEPS) - 2)
            act.wait_ge(k_done, len(STEPS) - 2)
            for p in range(2):
                act.activation(dist[:, p, :], b[:, p, :], ACT.Exp, scale=1.0 / 16).then_inc(chunk_exp, 1)
            act.activation(dec[:], b[:].rearrange("p a (c i) -> p a c i", i=C)[:, :, :, C - 1], ACT.Exp, scale=1.0 / 16).then_inc(chunk_exp, 1)
            for p in range(2):
                act.wait_ge(last_dist, p + 1)
                act.activation(Q[:, p, :], Q[:, p, :], ACT.Exp, scale=1.0 / 16).then_inc(chunk_exp, 1)
            for t in range(NT):
                act.wait_ge(out_done, t + 1)
                for h in range(NH):
                    act.activation(dist[:, 0, h * P:(h + 1) * P], ps[:, 4 + t % 2, h * P:(h + 1) * P], ACT.Square,
                                   accum_out=stat[:, 0, t, h:h + 1]).then_inc(squares, 1)
                act.wait_ge(squares, NH * (t + 1))
                act.activation(stat[:, 1, t, :], stat[:, 0, t, :], ACT.Sqrt, scale=1.0 / P, bias=g.eps[:, 0:1]).then_inc(roots, 1)
                if t >= 1:
                    act.wait_ge(o_turned, t)
                    act.activation(g.mixA[:, :, (t - 1) * P:t * P], ps[:, 6 + (t - 1) % 2, :].rearrange("p (h c) -> p h c", h=NH),
                                   ACT.Copy, scale=g.par[:, R_GLA:R_GLA + 1]).then_inc(o_kept, 1)
            act.wait_ge(o_turned, NT)
            act.activation(g.mixA[:, :, (NT - 1) * P:T], ps[:, 6 + (NT - 1) % 2, :].rearrange("p (h c) -> p h c", h=NH),
                           ACT.Copy, scale=g.par[:, R_GLA:R_GLA + 1]).then_inc(o_kept, 1)

        @block.vector
        def _(dve):
            reset = K[:, 0, :]
            dve.memset(one[:], 1.0).then_inc(prep, 1)
            dve.memset(reset, 1.0).then_inc(prep, 1)
            dve.wait_ge(prep, 2)
            dve.memset(reset.rearrange("p (c i) -> p c i", i=C)[:, :, 0:1], 0.0).then_inc(prep, 1)
            for p in range(2):
                dve.wait_ge(act_pre, 3 * p + 3)
                src = ps[:, 4 + 2 * p:6 + 2 * p, :].rearrange("p a c -> p (a c)")
                dve.tensor_scalar(Q[:, p, :], src, g.par[:, R_BG + p:R_BG + p + 1], 0.0, ALU.add, ALU.min).then_inc(low, 1)
                dve.wait_ge(low, p + 1)
                dve.tensor_tensor(Q[:, p, :], Q[:, p, :], dist[:, p, :], ALU.subtract).then_inc(logs, 1)
                dve.wait_ge(logs, p + 1)
                dve.wait_ge(prep, 3)
                dve.tensor_tensor_scan(b[:, p, :], reset, Q[:, p, :], 0.0, ALU.mult, ALU.add).then_inc(run_sum, 1)
            dve.wait_ge(run_sum, 2)
            dve.wait_ge(zeroed, 3)

            def distance(n):
                level, p = STEPS[n]
                m = 1 << level
                v = b[:, p, :].rearrange("p (a i) -> p a i", i=2 * m)
                if n >= 4:
                    dve.wait_ge(q_done, n - 3)
                    dve.wait_ge(k_done, n - 3)
                dve.tensor_tensor(dist[:, n % 2, :].rearrange("p (a i) -> p a i", i=2 * m), v,
                                  v[:, :, m - 1:m].to_broadcast([P, T // (2 * m), 2 * m]), ALU.subtract).then_inc(dist_done, 1)

            def q_level(n):
                level, p = STEPS[n]
                dve.wait_ge(decay_done, n - 1)
                if n >= 4:
                    dve.wait_ge(score_done, 4 * (n - 1))
                dve.tensor_tensor(Q[:, n % 2, :], g.gqkT[:, p, :], dist[:, n % 2, :], ALU.mult).then_inc(q_done, 1)

            def keep(n):
                level, p = STEPS[n]
                mask = g.k[:, K_ID:K_ID + P] if level == "diag" else g.k[:, K_LEVEL + level * P:K_LEVEL + (level + 1) * P]
                for half in range(2):
                    for parity in range(2):
                        dve.wait_ge(score_done, 4 * n + 2 * half + parity + 1)
                        dve.copy_predicated(A[:, 2 * p + parity, 4 * half:4 * half + 4, :],
                                            mask.bitcast(I32).unsqueeze(1).to_broadcast([P, 4, P]),
                                            ps[:, bank_of(n, half, parity), :].rearrange("p (t c) -> p t c", t=4)).then_inc(kept, 1)

            distance(2)
            distance(3)
            for n in range(len(STEPS)):
                keep(n)
                if n + 2 < len(STEPS):
                    q_level(n + 2)
                if n + 4 < len(STEPS):
                    distance(n + 4)
            for p in range(2):
                v = b[:, p, :].rearrange("p (a i) -> p a i", i=C)
                dve.wait_ge(score_done, 4 * len(STEPS))
                dve.tensor_tensor(Q[:, p, :].rearrange("p (a i) -> p a i", i=C), v[:, :, C - 1:C].to_broadcast([P, NC, C]), v,
                                  ALU.subtract).then_inc(last_dist, 1)
            for p in range(2):
                dve.wait_ge(chunk_exp, p + 1)
                for e in range(2):
                    rows = slice(GK * e, GK * (e + 1))
                    dve.tensor_tensor(qe[rows, 2 * p + e, :], g.gqkT[rows, p, :], dist[rows, p, :], ALU.mult).then_inc(qe_done, 1)
                dve.wait_ge(chunk_exp, 4 + p)
                dve.tensor_tensor(K[:, p, :], g.gqkT[:, 2 + p, :], Q[:, p, :], ALU.mult).then_inc(kd_done, 1)
            for q in range(4):
                p, half = q // 2, q % 2
                dve.wait_ge(k_turned, q + 1)
                dve.tensor_copy(kdn[:, 4 * half:4 * half + 4, p * P:(p + 1) * P], ps[:, q, :].rearrange("p (t c) -> p t c", t=4)).then_inc(k_natural, 1)
            for c in range(NC - 1):
                dve.wait_ge(added, c + 1)
                if c >= 1:
                    dve.wait_ge(state_done, 2 * c)
                for p in range(2):
                    dve.scalar_tensor_tensor(out=S[:, p, c + 1, :], in0=S[:, p, c, :], scalar=dec[:, p, c:c + 1],
                                             in1=ps[:, c % 4, p * P:(p + 1) * P], op0=ALU.mult, op1=ALU.add).then_inc(state_done, 1)
            for t in range(NT):
                dve.wait_ge(roots, t + 1)
                dve.reciprocal(stat[:, 1, t, :], stat[:, 1, t, :]).then_inc(inverses, 1)
                dve.wait_ge(inverses, t + 1)
                dve.wait_ge(gate_in[t % 2], 16 * (t // 2 + 1))
                if t >= 2:
                    dve.wait_ge(o_turned, t - 1)
                for h in range(NH):
                    cols = slice(h * P, (h + 1) * P)
                    dve.scalar_tensor_tensor(out=on[:, t % 2, cols], in0=ps[:, 4 + t % 2, cols], scalar=stat[:, 1, t, h:h + 1],
                                             in1=gate[:, t % 2, cols], op0=ALU.mult, op1=ALU.mult).then_inc(normed, 1)


def delta(nc, g, sem):
    with ExitStack() as ph:
        def sb(name, shape, dt=F32):
            return ph.enter_context(nc.sbuf_tensor("dn_" + name, shape, dt))

        G = NH * P
        E_ = sb("pair_decay", [P, NT, G])
        LT = sb("lower_T", [P, NT, G])
        inv_T = sb("inv_T", [P, NT, G])
        inv = sb("inv", [P, NT, G])
        aqk = sb("scores_T", [P, NT, G])
        bk = sb("beta_k", [P, NT, G])
        tmp = sb("tmp", [P, 6, G])
        small = sb("small", [P, 9, NT, NH])
        S = sb("state", [P, 2, G])
        stat = sb("stat", [P, 2, NT, NH])
        decS = sb("chunk_decay", [P, 2, NT, NH])
        par = sb("head_parameters", [P, 2, NH])
        one = sb("one", [P, 1])
        ps = ph.enter_context(nc.psum_tensor("dn_psum", [P, 8, HALF], F32))
        wT, u = E_, LT
        Y, GN, BETA, BN, EBN, KDS, BKE, SP, AB = range(9)
        ident, tri = g.k[:, K_ID:K_ID + P], g.k[:, K_TRI:K_TRI + P]

        def heads(ap):
            return ap.rearrange("p (h c) -> p h c", h=NH)

        def over(ap):
            return ap.unsqueeze(2).to_broadcast([P, NH, P])

        par_in, gate_in = sem("par_in"), [sem(f"gate_in{i}") for i in range(2)]
        one_set, y_ready, soft, gn_ready, sums, small_ready, small_exp, bke_ready = (sem(n) for n in (
            "one_set", "y_ready", "softplus", "log_decay", "sums", "sums_kept", "sums_exp", "beta_decay"))
        scaled, rows_done, kq_done, kv_turned = sem("scaled_triangles"), sem("rows"), sem("kk_qk"), sem("kv_turned")
        row_exp, apart, pair_exp, prod, masked, qd_done, nat_done, v_done = (sem(n) for n in (
            "row_exp", "apart", "pair_exp", "products", "scores_masked", "q_decayed", "k_natural", "v_natural"))
        cut0, inv0, first_turned, first_kept = sem("first_cut"), sem("inv_T_first"), sem("first_turned"), sem("first_kept")
        cut, x_done, x_kept, z_done, z_used, t_done, t_kept = (sem(n) for n in (
            "cut", "x_done", "x_kept", "z_done", "z_used", "inv_turned", "inv_kept"))
        sol_done, w_kept, u_kept = sem("sol_done"), sem("w_kept"), sem("u_kept")
        s_zero, ws_done, delta_done, upd_done, s_decayed, s_done = (sem(n) for n in (
            "state_zero", "ws_done", "delta", "update", "state_decayed", "state"))
        out_done, squares, roots, inverses, normed, o_turned, o_kept = (sem(n) for n in (
            "out", "out_squares", "out_roots", "out_inverse", "out_normed", "out_turned", "out_kept"))
        ROWS, BROW, KK, QK, KN, VN, TURN = 0, 1, 2, 3, 4, 5, 6
        STEPS = [(l, t) for l in range(1, LEVELS) for t in range(NT)]
        NORM_GATE, NORM_ON = [4, 5], [2, 3]
        block = ph.enter_context(nc.Block())

        @block.sync
        def _(sp):
            sp.dma_start(par[:, 0, :], g.gdn_a_log.rearrange("a h -> (a h)").partition_broadcast(P)).then_inc(par_in, 16)
            sp.dma_start(par[:, 1, :], g.gdn_dt_bias.rearrange("a h -> (a h)").partition_broadcast(P)).then_inc(par_in, 16)
            sp.wait_ge(w_kept, NT)
            for t in range(NT):
                if t >= 2:
                    sp.wait_ge(normed, NH * (t - 1))
                sp.dma_start(tmp[:, NORM_GATE[t % 2], :], g.gates_dram[1].rearrange("(t p) d -> t p d", p=P)[t]).then_inc(gate_in[t % 2], 16)

        @block.gpsimd
        def _(pool):
            pool.memset(S[:, 0, :], 0.0).then_inc(s_zero, 1)
            for t in range(NT):
                pool.wait_ge(prod, 3 * t + 1)
                pool.tensor_tensor(heads(aqk[:, t, :]), heads(aqk[:, t, :]), tri.unsqueeze(1).to_broadcast([P, NH, P]), ALU.mult).then_inc(masked, 1)
                pool.wait_ge(prod, 3 * t + 3)
                if t >= 1:
                    pool.wait_ge(inv0, t)
                pool.tensor_tensor(heads(tmp[:, 5, :]), heads(LT[:, t, :]), g.k[:, K_LEVEL:K_LEVEL + P].unsqueeze(1).to_broadcast([P, NH, P]),
                                   ALU.mult).then_inc(cut0, 1)
                pool.wait_ge(cut0, t + 1)
                pool.tensor_tensor(heads(inv_T[:, t, :]), ident.unsqueeze(1).to_broadcast([P, NH, P]), heads(tmp[:, 5, :]),
                                   ALU.subtract).then_inc(inv0, 1)
            for s, (l, t) in enumerate(STEPS):
                if s == 0:
                    pool.wait_ge(cut0, NT)
                    pool.wait_ge(inv0, NT)
                if s >= 2:
                    pool.wait_ge(x_done, s - 1)
                mask = g.k[:, K_LEVEL + l * P:K_LEVEL + (l + 1) * P]
                pool.tensor_tensor(heads(tmp[:, s % 2, :]), heads(LT[:, t, :]), mask.unsqueeze(1).to_broadcast([P, NH, P]), ALU.mult).then_inc(cut, 1)
            for c in range(NC - 1):
                t, r = c // 2, c % 2
                if c == 0:
                    pool.wait_ge(s_zero, 1)
                else:
                    pool.wait_ge(s_done, c)
                pool.tensor_tensor(heads(S[:, (c + 1) % 2, :]), heads(S[:, c % 2, :]), over(decS[:, r, t, :]), ALU.mult).then_inc(s_decayed, 1)

        @block.tensor
        def _(pe):
            def mm4(bank, lhs, rhs, **kw):
                for h in range(NH):
                    mm = pe.matmul(ps[:, bank, h * P:(h + 1) * P], lhs(h), rhs(h), start=True, stop=True)
                return mm

            pe.wait_ge(gn_ready, 1)
            gn = small[:, GN, :, :].rearrange("p t h -> p (t h)")
            for i, col in enumerate((K_TRI, K_CHUNK, K_HALF, K_HALF + P)):
                pe.matmul(ps[:, 7, 32 * i:32 * i + 32], g.k[:, col:col + P], gn, start=True, stop=True).then_inc(sums, 1)
            ones = g.k[:, K_ONES:K_ONES + P]
            for t in range(NT):
                cols = slice(t * P, (t + 1) * P)
                pe.wait_ge(scaled, 2 * t + 1)
                if t >= 1:
                    pe.wait_ge(row_exp, t)
                    pe.wait_ge(apart, NH * t)
                pe.matmul(ps[:, ROWS, :], ones, tmp[:, 0, :], start=True, stop=True).then_inc(rows_done, 1)
                pe.wait_ge(scaled, 2 * t + 2)
                if t >= 1:
                    pe.wait_ge(prod, 3 * t)
                pe.matmul(ps[:, BROW, :], ones, tmp[:, 1, :], start=True, stop=True).then_inc(rows_done, 1)
                mm4(KK, lambda h: g.qkvT[:, NH + h, cols], lambda h: g.qkvT[:, NH + h, cols]).then_inc(kq_done, 1)
                mm4(QK, lambda h: g.qkvT[:, NH + h, cols], lambda h: g.qkvT[:, h, cols]).then_inc(kq_done, 1)
                if t >= 1:
                    pe.wait_ge(nat_done, 2 * NH * t)
                    pe.wait_ge(v_done, NH * t)
                for bank, at in ((KN, NH), (VN, 2 * NH)):
                    for h in range(NH):
                        mm = pe.transpose(ps[:, bank, h * P:(h + 1) * P], g.qkvT[:, at + h, cols], ident)
                    mm.then_inc(kv_turned, 1)
            for t in range(NT):
                pe.wait_ge(inv0, t + 1)
                if t >= 2:
                    pe.wait_ge(first_kept, t - 1)
                for h in range(NH):
                    mm = pe.transpose(ps[:, TURN + t % 2, h * P:(h + 1) * P], inv_T[:, t, h * P:(h + 1) * P], ident)
                mm.then_inc(first_turned, 1)

            def part(ap, h):
                return ap[:, h * P:(h + 1) * P]

            N = len(STEPS)
            for s in range(N + 2):
                if s < N:
                    l, t = STEPS[s]
                    pe.wait_ge(cut, s + 1)
                    if s < NT:
                        pe.wait_ge(first_kept, t + 1)
                    else:
                        pe.wait_ge(t_kept, s - NT + 1)
                    if s >= 2:
                        pe.wait_ge(x_kept, s - 1)
                    mm4(s % 2, lambda h: part(tmp[:, s % 2, :], h), lambda h: part(inv[:, t, :], h)).then_inc(x_done, 1)
                if 1 <= s <= N:
                    q = s - 1
                    l, t = STEPS[q]
                    pe.wait_ge(x_kept, q + 1)
                    if q >= 2:
                        pe.wait_ge(z_used, q - 1)
                    mm4(2 + q % 2, lambda h: part(tmp[:, 2 + q % 2, :], h), lambda h: part(inv_T[:, t, :], h)).then_inc(z_done, 1)
                if s >= 2 and STEPS[s - 2][0] < LEVELS - 1:
                    q = s - 2
                    l, t = STEPS[q]
                    pe.wait_ge(z_used, q + 1)
                    if q >= 2:
                        pe.wait_ge(t_kept, q - 1)
                    for h in range(NH):
                        mm = pe.transpose(ps[:, 4 + q % 2, h * P:(h + 1) * P], part(inv_T[:, t, :], h), ident)
                    mm.then_inc(t_done, 1)
            for t in range(NT):
                cols = slice(t * P, (t + 1) * P)
                if t == 0:
                    pe.wait_ge(z_used, N)
                    pe.wait_ge(t_kept, N - NT)
                    pe.wait_ge(nat_done, 2 * NH * NT)
                if t >= 2:
                    pe.wait_ge(w_kept, t - 1)
                    pe.wait_ge(u_kept, t - 1)
                mm4(4 + t % 2, lambda h: part(bk[:, t, :], h), lambda h: part(inv_T[:, t, :], h)).then_inc(sol_done, 1)
                mm4(6 + t % 2, lambda h: part(inv_T[:, t, :], h), lambda h: g.qkvT[:, 2 * NH + h, cols]).then_inc(sol_done, 1)

            def turn_out(t):
                pe.wait_ge(normed, NH * (t + 1))
                if t >= 1:
                    pe.wait_ge(o_kept, t)
                for h in range(NH):
                    mm = pe.transpose(ps[:, 6, h * P:(h + 1) * P], part(tmp[:, NORM_ON[t % 2], :], h), ident)
                mm.then_inc(o_turned, 1)

            for c in range(NC):
                t, r = c // 2, c % 2
                rows = slice(C * r, C * (r + 1))
                cols = slice(t * P + C * r, t * P + C * (r + 1))
                if c == 0:
                    pe.wait_ge(s_zero, 1)
                    pe.wait_ge(w_kept, NT)
                    pe.wait_ge(u_kept, NT)
                    pe.wait_ge(qd_done, NT)
                else:
                    pe.wait_ge(s_done, c)
                if c >= 2:
                    pe.wait_ge(delta_done, c - 1)
                state = S[:, c % 2, :]
                for h in range(NH):
                    mm = pe.matmul(ps[rows, c % 2, h * P:(h + 1) * P], wT[:, t, h * P + C * r:h * P + C * (r + 1)], part(state, h),
                                   start=True, stop=True)
                mm.then_inc(ws_done, 1)
                if r == 0 and t >= 2:
                    pe.wait_ge(normed, NH * (t - 1))
                for h in range(NH):
                    mm = pe.matmul(ps[rows, 4 + t % 2, h * P:(h + 1) * P], g.qkvT[:, h, cols], part(state, h),
                                   start=(h == 0), stop=False, skip_group_check=True)
                pe.wait_ge(delta_done, c + 1)
                if c < NC - 1:
                    if c >= 2:
                        pe.wait_ge(s_done, c - 1)
                    for h in range(NH):
                        mm = pe.matmul(ps[:, 2 + c % 2, h * P:(h + 1) * P], g.qkvT[rows, NH + h, t * P:(t + 1) * P],
                                       tmp[rows, t % 2, h * P:(h + 1) * P], start=True, stop=True)
                    mm.then_inc(upd_done, 1)
                if r == 0 and t >= 2:
                    turn_out(t - 2)
                if r == 1:
                    pe.wait_ge(masked, NT)
                    for h in range(NH):
                        mm = pe.matmul(ps[:, 4 + t % 2, h * P:(h + 1) * P], part(aqk[:, t, :], h), part(tmp[:, t % 2, :], h),
                                       start=False, stop=(h == NH - 1), skip_group_check=True)
                    mm.then_inc(out_done, 1)
            turn_out(NT - 2)
            turn_out(NT - 1)

        @block.scalar
        def _(act):
            act.wait_ge(y_ready, 1)
            act.wait_ge(one_set, 1)
            act.activation(small[:, BETA], g.dab[:, :, NH:2 * NH], ACT.Sigmoid).then_inc(soft, 1)
            act.activation(small[:, AB], small[:, Y], ACT.Abs).then_inc(soft, 1)
            act.wait_ge(soft, 2)
            act.activation(small[:, AB], small[:, AB], ACT.Exp, scale=-1.0).then_inc(soft, 1)
            act.wait_ge(soft, 3)
            act.activation(small[:, AB], small[:, AB], ACT.Ln, bias=one[:, 0:1]).then_inc(soft, 1)
            act.activation(par[:, 0, :], par[:, 0, :], ACT.Exp).then_inc(soft, 1)
            act.wait_ge(small_ready, 2)
            act.activation(small[:, EBN], small[:, BN], ACT.Exp).then_inc(small_exp, 1)
            act.activation(small[:, KDS], small[:, KDS], ACT.Exp).then_inc(small_exp, 1)
            act.activation(decS[:].rearrange("p r t h -> p (r t h)"), ps[:, 7, 64:128], ACT.Exp).then_inc(small_exp, 1)
            for t in range(NT):
                act.wait_ge(rows_done, 2 * t + 1)
                if t >= 2:
                    act.wait_ge(qd_done, t - 1)
                act.activation(tmp[:, 2 + t % 2, :], ps[:, ROWS, :], ACT.Exp).then_inc(row_exp, 1)
                act.wait_ge(apart, NH * (t + 1))
                act.activation(E_[:, t, :], E_[:, t, :], ACT.Exp).then_inc(pair_exp, 1)
                act.wait_ge(kv_turned, 2 * t + 1)
                if t == 0:
                    act.wait_ge(bke_ready, 1)
                for h in range(NH):
                    act.activation(bk[:, t, h * P:(h + 1) * P], ps[:, KN, h * P:(h + 1) * P], ACT.Copy,
                                   scale=small[:, BKE, t, h:h + 1]).then_inc(nat_done, 1)
                    act.activation(g.qkvT[:, NH + h, t * P:(t + 1) * P], ps[:, KN, h * P:(h + 1) * P], ACT.Copy,
                                   scale=small[:, KDS, t, h:h + 1]).then_inc(nat_done, 1)
                act.wait_ge(kv_turned, 2 * t + 2)
                for h in range(NH):
                    act.activation(g.qkvT[:, 2 * NH + h, t * P:(t + 1) * P], ps[:, VN, h * P:(h + 1) * P], ACT.Copy,
                                   scale=small[:, BETA, t, h:h + 1]).then_inc(v_done, 1)
            for t in range(NT):
                act.wait_ge(first_turned, t + 1)
                act.copy(inv[:, t, :], ps[:, TURN + t % 2, :]).then_inc(first_kept, 1)
            N = len(STEPS)
            for s in range(N + 2):
                if s < N:
                    act.wait_ge(x_done, s + 1)
                    if s >= 2:
                        act.wait_ge(z_done, s - 1)
                    act.copy(tmp[:, 2 + s % 2, :], ps[:, s % 2, :]).then_inc(x_kept, 1)
                if s >= 2 and STEPS[s - 2][0] < LEVELS - 1:
                    q = s - 2
                    act.wait_ge(t_done, q + 1)
                    act.copy(inv[:, STEPS[q][1], :], ps[:, 4 + q % 2, :]).then_inc(t_kept, 1)
            for t in range(NT):
                act.wait_ge(sol_done, 2 * t + 1)
                act.copy(wT[:, t, :], ps[:, 4 + t % 2, :]).then_inc(w_kept, 1)

            def keep_out(t):
                act.wait_ge(o_turned, t + 1)
                act.activation(g.mixB[:, :, t * P:(t + 1) * P], heads(ps[:, 6, :]), ACT.Copy, scale=g.par[:, R_GDN:R_GDN + 1]).then_inc(o_kept, 1)

            for t in range(NT):
                act.wait_ge(out_done, t + 1)
                for h in range(NH):
                    act.activation(bk[:, 0, h * P:(h + 1) * P], ps[:, 4 + t % 2, h * P:(h + 1) * P], ACT.Square,
                                   accum_out=stat[:, 0, t, h:h + 1]).then_inc(squares, 1)
                act.wait_ge(squares, NH * (t + 1))
                act.activation(stat[:, 1, t, :], stat[:, 0, t, :], ACT.Sqrt, scale=1.0 / P, bias=g.eps[:, 0:1]).then_inc(roots, 1)
                if t >= 1:
                    keep_out(t - 1)
            keep_out(NT - 1)

        @block.vector
        def _(dve):
            dve.memset(one[:], 1.0).then_inc(one_set, 1)
            dve.wait_ge(par_in, 32)
            dve.tensor_tensor(small[:, Y], g.dab[:, :, 0:NH], par[:, 1:2, :].to_broadcast([P, NT, NH]), ALU.add).then_inc(y_ready, 1)
            dve.wait_ge(soft, 5)
            dve.scalar_tensor_tensor(out=small[:, SP], in0=small[:, Y], scalar=0.0, in1=small[:, AB], op0=ALU.max, op1=ALU.add).then_inc(y_ready, 1)
            dve.wait_ge(y_ready, 2)
            dve.scalar_tensor_tensor(out=small[:, GN], in0=small[:, SP], scalar=-1.0, in1=par[:, 0:1, :].to_broadcast([P, NT, NH]),
                                     op0=ALU.mult, op1=ALU.mult).then_inc(gn_ready, 1)
            dve.wait_ge(sums, 4)
            dve.tensor_copy(small[:, BN].rearrange("p t h -> p (t h)"), ps[:, 7, 0:32]).then_inc(small_ready, 1)
            dve.wait_ge(small_ready, 1)
            dve.tensor_tensor(small[:, KDS].rearrange("p t h -> p (t h)"), ps[:, 7, 32:64], small[:, BN].rearrange("p t h -> p (t h)"),
                              ALU.subtract).then_inc(small_ready, 1)
            dve.wait_ge(small_exp, 3)
            dve.tensor_tensor(small[:, BKE], small[:, EBN], small[:, BETA], ALU.mult).then_inc(bke_ready, 1)
            dve.wait_ge(bke_ready, 1)

            def scale(t):
                for slot, what, by in ((0, tri, GN), (1, ident, BETA)):
                    if t >= 1:
                        dve.wait_ge(rows_done, 2 * t - 1 + slot)
                    dve.tensor_tensor(heads(tmp[:, slot, :]), what.unsqueeze(1).to_broadcast([P, NH, P]), over(small[:, by, t, :]),
                                      ALU.mult).then_inc(scaled, 1)

            scale(0)
            for t in range(NT):
                cols = slice(t * P, (t + 1) * P)
                dve.wait_ge(row_exp, t + 1)
                for h in range(NH):
                    dve.tensor_scalar(E_[:, t, h * P:(h + 1) * P], ps[:, ROWS, h * P:(h + 1) * P], small[:, BN, t, h:h + 1], 0.0,
                                      ALU.subtract, ALU.min).then_inc(apart, 1)
                if t + 1 < NT:
                    scale(t + 1)
                dve.wait_ge(kq_done, 2 * t + 2)
                dve.wait_ge(row_exp, t + 1)
                dve.tensor_tensor(g.qkvT[:, 0:NH, cols], g.qkvT[:, 0:NH, cols], heads(tmp[:, 2 + t % 2, :]), ALU.mult).then_inc(qd_done, 1)
                dve.wait_ge(pair_exp, t + 1)
                dve.wait_ge(rows_done, 2 * t + 2)
                dve.tensor_tensor(aqk[:, t, :], ps[:, QK, :], E_[:, t, :], ALU.mult).then_inc(prod, 1)
                if t >= 1:
                    dve.wait_ge(prod, 3 * t)
                dve.tensor_tensor(tmp[:, 4, :], ps[:, BROW, :], E_[:, t, :], ALU.mult).then_inc(prod, 1)
                dve.wait_ge(prod, 3 * t + 2)
                dve.tensor_tensor(LT[:, t, :], ps[:, KK, :], tmp[:, 4, :], ALU.mult).then_inc(prod, 1)
            for s, (l, t) in enumerate(STEPS):
                dve.wait_ge(z_done, s + 1)
                if s >= NT and l < LEVELS:
                    dve.wait_ge(t_done, s - NT + 1)
                dve.tensor_tensor(inv_T[:, t, :], inv_T[:, t, :], ps[:, 2 + s % 2, :], ALU.subtract).then_inc(z_used, 1)
            for t in range(NT):
                dve.wait_ge(sol_done, 2 * t + 2)
                dve.tensor_copy(u[:, t, :], ps[:, 6 + t % 2, :]).then_inc(u_kept, 1)

            def norm_out(t):
                dve.wait_ge(roots, t + 1)
                dve.reciprocal(stat[:, 1, t, :], stat[:, 1, t, :]).then_inc(inverses, 1)
                dve.wait_ge(inverses, t + 1)
                dve.wait_ge(gate_in[t % 2], 16 * (t // 2 + 1))
                if t >= 2:
                    dve.wait_ge(o_turned, t - 1)
                for h in range(NH):
                    cols = slice(h * P, (h + 1) * P)
                    dve.scalar_tensor_tensor(out=tmp[:, NORM_ON[t % 2], cols], in0=ps[:, 4 + t % 2, cols], scalar=stat[:, 1, t, h:h + 1],
                                             in1=tmp[:, NORM_GATE[t % 2], cols], op0=ALU.mult, op1=ALU.mult).then_inc(normed, 1)

            dve.wait_ge(u_kept, NT)
            dve.wait_ge(s_zero, 1)
            for c in range(NC):
                t, r = c // 2, c % 2
                rows = slice(C * r, C * (r + 1))
                dve.wait_ge(ws_done, c + 1)
                if r == 0 and t >= 2:
                    dve.wait_ge(out_done, t - 1)
                dve.tensor_tensor(tmp[rows, t % 2, :], u[rows, t, :], ps[rows, c % 2, :], ALU.subtract).then_inc(delta_done, 1)
                if c < NC - 1:
                    dve.wait_ge(s_decayed, c + 1)
                    dve.wait_ge(upd_done, c + 1)
                    dve.tensor_tensor(S[:, (c + 1) % 2, :], S[:, (c + 1) % 2, :], ps[:, 2 + c % 2, :], ALU.add).then_inc(s_done, 1)
                if r == 0 and t >= 1:
                    norm_out(t - 1)
            norm_out(NT - 1)

def route(nc, g, sem):
    with ExitStack() as ph:
        def sb(name, shape, dt=F32):
            return ph.enter_context(nc.sbuf_tensor("rt_" + name, shape, dt))

        w_out = g.ring_b[:, 2:6].rearrange("p s n -> p (s n)").rearrange("p (k n) -> p k n", k=KT)
        w_router = sb("w_router", [P, KT, E])
        xt = sb("x", [P, 2, D])
        xn = sb("xn", [P, 2, D])
        xnT = sb("xnT", [P, KT, P])
        gain = sb("g_moe", [P, D])
        b_router = sb("b_router", [P, E])
        rows = xnT[:, 0:6]
        stat = sb("stat", [P, 3, NT])
        logit = sb("logit", [P, NT, E])
        top, neg, hot = g.top, g.neg, g.hot
        top_e = sb("top_e", [P, NT, 8], U32)
        top_f = sb("top_f", [P, NT, TOPK])
        chosen = sb("chosen", [P, NT, E])
        spot = sb("spot", [P, E])
        ps = ph.enter_context(nc.psum_tensor("rt_psum", [P, 8, HALF], F32))
        ident = g.k[:, K_ID:K_ID + P]

        w_out_in = [sem(f"w_out_in{i}") for i in range(KT // 2)]
        w_in_s, bc_in, rows_in = sem("router_in"), sem("broadcasts_in"), sem("bias_rows_in")
        x_in, xn_out = [sem(f"x_in{i}") for i in range(2)], [sem(f"xn_out{i}") for i in range(2)]
        b_turned, b_kept = sem("bias_turned"), sem("bias_kept")
        proj, summed, squared, rooted, inv_done, normed = (sem(n) for n in ("projected", "summed", "squared", "rooted", "inverse", "normed"))
        turned, kept, logits, logit_sb, top_done, index_done, index_f, hot_done, chosen_done = (sem(n) for n in (
            "turned", "kept", "logits", "logit_kept", "top", "top_index", "top_index_f", "hot", "chosen"))
        places, spot_done, place_done, neg_done, exp_done, list_done = (sem(n) for n in (
            "places", "spot", "place_kept", "neg_top", "exp_top", "dummy_place"))
        totals, total_done = sem("totals"), sem("counts")
        block = ph.enter_context(nc.Block())

        @block.sync
        def _(sp):
            for i, s in enumerate(w_out_in):
                sp.dma_start(w_out[:, 2 * i:2 * i + 2, :], g.w_out.rearrange("a (k p) n -> p (a k) n", p=P)[:, 2 * i:2 * i + 2, :]).then_inc(s, 16)
            for t in range(2):
                sp.dma_start(xt[:, t], g.x.rearrange("(t p) d -> t p d", p=P)[t]).then_inc(x_in[t], 16)
            sp.dma_start(w_router[:], g.w_router.rearrange("a (k p) n -> p (a k) n", p=P)).then_inc(w_in_s, 16)
            sp.dma_start(gain[:], g.g_moe.rearrange("a d -> (a d)").partition_broadcast(P)).then_inc(bc_in, 16)
            sp.dma_start(b_router[:], g.b_router.rearrange("a d -> (a d)").partition_broadcast(P)).then_inc(bc_in, 16)
            sp.dma_start(rows[:, 0:4], g.b_gate_up.rearrange("a e (j c) -> (a e j) c", c=P).rearrange("(q r) c -> r q c", r=P)).then_inc(rows_in, 16)
            sp.dma_start(rows[:, 4:6], g.b_down.rearrange("a e (j c) -> (a e j) c", c=P).rearrange("(q r) c -> r q c", r=P)).then_inc(rows_in, 16)
            for i in range(8):
                sp.dma_start(ring_slot(g, i).rearrange("p (k n) -> p k n", k=KT), weight_source(g, 0, i)).then_inc(g.w_in_ring[i], 16)
            for t in range(NT):
                if t >= 2:
                    sp.wait_ge(summed, t - 1)
                    sp.dma_start(xt[:, t % 2], g.x.rearrange("(t p) d -> t p d", p=P)[t]).then_inc(x_in[t % 2], 16)
                if t >= 1:
                    sp.wait_ge(normed, t)
                    sp.dma_start(g.xn_dram.rearrange("(t p) d -> t p d", p=P)[t - 1], xn[:, (t - 1) % 2]).then_inc(xn_out[(t - 1) % 2], 16)
            sp.wait_ge(normed, NT)
            sp.dma_start(g.xn_dram.rearrange("(t p) d -> t p d", p=P)[NT - 1], xn[:, (NT - 1) % 2]).then_inc(xn_out[(NT - 1) % 2], 16)
            for s in xn_out:
                sp.wait_ge(s, 16 * NT // 2)

        @block.tensor
        def _(pe):
            def turn_biases():
                pe.wait_ge(rows_in, 32)
                for q in range(6):
                    mm = pe.transpose(ps[:, 6 + q // 4, (q % 4) * P:(q % 4 + 1) * P], rows[:, q], ident)
                mm.then_inc(b_turned, 1)

            def project_tile(t):
                if t >= 2:
                    pe.wait_ge(summed, t - 1)
                for k in range(KT):
                    if t == 0 and k % 2 == 0:
                        pe.wait_ge(w_out_in[k // 2], 16)
                    mix = (g.mixA if k < NH else g.mixB)[:, k % NH, t * P:(t + 1) * P]
                    for half in range(2):
                        mm = pe.matmul(ps[:, 2 * (t % 2) + half, :], mix, w_out[:, k, half * HALF:(half + 1) * HALF],
                                       start=(k == 0), stop=(k == KT - 1))
                mm.then_inc(proj, 1)

            def turn_tile(t):
                pe.wait_ge(normed, t + 1)
                if t >= 1:
                    pe.wait_ge(kept, 2 * t)
                for q in range(2):
                    for i in range(4):
                        mm = pe.transpose(ps[:, 4 + q, i * P:(i + 1) * P], xn[:, t % 2, (4 * q + i) * P:(4 * q + i + 1) * P], ident)
                    mm.then_inc(turned, 1)

            def router_tile(t):
                pe.wait_ge(kept, 2 * (t + 1))
                if t == 0:
                    pe.wait_ge(b_kept, 2)
                    pe.wait_ge(w_in_s, 16)
                else:
                    pe.wait_ge(logit_sb, t)
                for k in range(KT):
                    mm = pe.matmul(ps[:, 6, 0:E], xnT[:, k, :], w_router[:, k, :], start=(k == 0), stop=(k == KT - 1))
                mm.then_inc(logits, 1)

            def place_tile(t):
                pe.wait_ge(chosen_done, t + 1)
                if t >= 1:
                    pe.wait_ge(spot_done, t)
                for s in range(t + 1):
                    tri = K_STRICT if s == t else K_ONES
                    mm = pe.matmul(ps[:, 7, 0:E], g.k[:, tri:tri + P], chosen[:, s, :], start=(s == 0), stop=(s == t))
                mm.then_inc(places, 1)

            project_tile(0)
            turn_biases()
            project_tile(1)
            for t in range(NT):
                turn_tile(t)
                if t + 2 < NT:
                    project_tile(t + 2)
                router_tile(t)
                if t >= 1:
                    place_tile(t - 1)
            place_tile(NT - 1)
            pe.wait_ge(spot_done, NT)
            for s in range(NT):
                mm = pe.matmul(ps[:, 7, 0:E], g.k[:, K_ONES:K_ONES + P], chosen[:, s, :], start=(s == 0), stop=(s == NT - 1))
            mm.then_inc(totals, 1)

        @block.scalar
        def _(act):
            def keep_turned(t):
                for q in range(2):
                    act.wait_ge(turned, 2 * t + q + 1)
                    if t >= 1:
                        act.wait_ge(logits, t)
                    act.copy(xnT[:, 4 * q:4 * q + 4, :], ps[:, 4 + q, :].rearrange("p (k c) -> p k c", k=4)).then_inc(kept, 1)

            for t in range(NT):
                act.wait_ge(summed, t + 1)
                if t >= 2:
                    act.wait_ge(turned, 2 * (t - 1))
                    act.wait_ge(xn_out[t % 2], 16 * (t // 2))
                act.activation(xn[:, t % 2], g.h[:, t, :], ACT.Square, accum_out=stat[:, 0, t:t + 1]).then_inc(squared, 1)
                act.wait_ge(squared, t + 1)
                act.activation(stat[:, 1, t:t + 1], stat[:, 0, t:t + 1], ACT.Sqrt, scale=1.0 / D, bias=g.eps[:, 0:1]).then_inc(rooted, 1)
                keep_turned(t)
            for t in range(NT):
                act.wait_ge(neg_done, t + 1)
                act.activation(top[:, t, 0:TOPK], top[:, t, 0:TOPK], ACT.Exp, bias=neg[:, t, 0:1], accum_out=neg[:, t, 1:2]).then_inc(exp_done, 1)

        @block.vector
        def _(dve):
            dve.wait_ge(bc_in, 32)
            iota_e = g.k[:, K_E:K_E + E]

            def norm(t):
                dve.wait_ge(proj, t + 1)
                dve.wait_ge(x_in[t % 2], 16 * (t // 2 + 1))
                dve.tensor_tensor(g.h[:, t, :], ps[:, 2 * (t % 2):2 * (t % 2) + 2, :].rearrange("p a c -> p (a c)"), xt[:, t % 2],
                                  ALU.add).then_inc(summed, 1)
                dve.wait_ge(rooted, t + 1)
                dve.reciprocal(stat[:, 1, t:t + 1], stat[:, 1, t:t + 1]).then_inc(inv_done, 1)
                dve.wait_ge(inv_done, t + 1)
                dve.scalar_tensor_tensor(out=xn[:, t % 2], in0=g.h[:, t, :], scalar=stat[:, 1, t:t + 1], in1=gain[:],
                                         op0=ALU.mult, op1=ALU.mult).then_inc(normed, 1)

            def choose(t):
                dve.wait_ge(logits, t + 1)
                dve.tensor_tensor(logit[:, t, :], ps[:, 6, 0:E], b_router[:], ALU.add).then_inc(logit_sb, 1)
                dve.wait_ge(logit_sb, t + 1)
                dve.max(top[:, t, :], logit[:, t, :]).then_inc(top_done, 1)
                dve.wait_ge(top_done, t + 1)
                dve.max_index(top_e[:, t, :], top[:, t, :], logit[:, t, :]).then_inc(index_done, 1)
                dve.wait_ge(index_done, t + 1)
                dve.tensor_scalar(neg[:, t, 0:1], top[:, t, 0:1], -1.0, None, ALU.mult).then_inc(neg_done, 1)
                dve.tensor_copy(top_f[:, t, :], top_e[:, t, 0:TOPK]).then_inc(index_f, 1)
                dve.wait_ge(index_f, t + 1)
                dve.tensor_tensor(hot[:, t], iota_e.unsqueeze(1).to_broadcast([P, TOPK, E]), top_f[:, t, :].unsqueeze(2).to_broadcast([P, TOPK, E]),
                                  ALU.is_equal).then_inc(hot_done, 1)
                dve.wait_ge(hot_done, t + 1)
                dve.tensor_reduce(chosen[:, t, :], hot[:, t].rearrange("p k e -> p e k"), AX.X, ALU.add).then_inc(chosen_done, 1)

            def place(t):
                dve.wait_ge(places, t + 1)
                if t >= 1:
                    dve.wait_ge(place_done, t)
                dve.scalar_tensor_tensor(out=spot[:], in0=ps[:, 7, 0:E], scalar=1.0, in1=chosen[:, t, :], op0=ALU.add, op1=ALU.mult).then_inc(spot_done, 1)
                dve.wait_ge(spot_done, t + 1)
                dve.tensor_scalar(g.place[:, t, 0:E], spot[:], -1.0, None, ALU.add).then_inc(place_done, 1)

            dve.memset(g.place[:, :, E:E + 1], -1.0).then_inc(list_done, 1)
            norm(0)
            dve.wait_ge(b_turned, 1)
            dve.tensor_copy(g.b_gu[:].rearrange("p e j -> p (e j)"), ps[:, 6, :]).then_inc(b_kept, 1)
            dve.tensor_copy(g.b_dn[:].rearrange("p e j -> p (e j)"), ps[:, 7, 0:2 * P]).then_inc(b_kept, 1)
            for t in range(NT):
                if t + 1 < NT:
                    norm(t + 1)
                choose(t)
                if t >= 1:
                    place(t - 1)
            place(NT - 1)
            dve.wait_ge(totals, 1)
            dve.tensor_copy(g.count[:, 0:E], ps[:, 7, 0:E]).then_inc(total_done, 1)
            with nc.allow_low_precision(reason="whole numbers below 2**24"):
                dve.tensor_reduce(g.count[:, E:E + 1], ps[:, 7, 0:E], AX.X, ALU.max).then_inc(total_done, 1)


RING_A = 6


def ring_slot(g, i):
    return g.ring_a[:, i] if i < RING_A else g.ring_b[:, i - RING_A]


def weight_source(g, e, i):
    if i < 8:
        col = (i % 2) * FF + (i // 2) * 256
        return g.w_gate_up[e].rearrange("(k p) n -> p k n", p=P)[:, :, col:col + 256]
    return g.w_down[e].rearrange("(k p) n -> p k n", p=P)[:, :, (i - 8) * 256:(i - 7) * 256]


class Experts:

    GATE_UP = [(0, 1), (2, 3)]
    DOWN = (4, 5)
    TURN, LIST = 6, 7

    def __init__(self, nc, g, sem, ph):
        self.nc, self.g = nc, g

        def sb(name, shape, dt=F32):
            return ph.enter_context(nc.sbuf_tensor("ex_" + name, shape, dt))

        self.xT = sb("xT", [P, KT, CAP])
        self.hT = sb("hT", [P, FF // P, CAP])
        self.yT = sb("yT", [P, KT, CAP])
        self.step = sb("step", [P, 2, NT, E])
        self.weigh = sb("weigh", [P, NT, TOPK, E])
        self.rows_a = sb("rows_a", [P, D])
        self.rows_b = sb("rows_b", [CAP - P, D])
        self.y_a = sb("y_a", [P, D])
        self.y_b = sb("y_b", [CAP - P, D])
        self.mark = sb("mark", [P, NT, CAP], BF16)
        self.token = sb("token", [P, 2 * NT], BF16)
        self.list_a = sb("list_a", [P, 1], U32)
        self.list_b = sb("list_b", [CAP - P, 1], U32)
        self.gate = sb("gate", [P, 2, 2, CAP])
        self.up = sb("up", [P, 2, 2, CAP])
        self.sig = sb("sig", [P, 2, 2, CAP])
        self.ps = ph.enter_context(nc.psum_tensor("ex_psum", [P, 8, HALF], F32))
        self.marked = sem("marked")
        self.list_summed = sem("list_summed")
        self.listed = sem("listed")
        self.rows_in = [sem("rows_a_in"), sem("rows_b_in")]
        self.turned = sem("bank6_filled")
        self.turn_kept = sem("bank6_emptied")
        self.gu_done = sem("gate_up_done")
        self.gu_kept = sem("gate_up_kept")
        self.sig_done = sem("sigmoid")
        self.act_step = sem("activation_steps")
        self.h_done = sem("hT")
        self.dn_done = sem("down_done")
        self.yT_kept = sem("yT_kept")
        self.y_out = [sem("y_a_out"), sem("y_b_out")]
        self.ready = sem("ready")
        self.rows_free, self.bank6_free, self.pass_stored, self.fill_seen, self.shift_seen = (
            sem(n) for n in ("gather_rows_free", "bank6_free", "pass_stored", "fill_seen", "shift_seen"))
        self.shifted = sem("places_shifted")
        self.slot_step, self.slot_prod, self.slot_done = sem("slot_steps"), sem("slot_products"), sem("slots")
        self.share_inv, self.share_done = sem("share_inverse"), sem("shares")
        self.filled = sem("round_rows_filled")
        self.ident = g.k[:, K_ID:K_ID + P]

    def dve_find(self, dve, x, e):
        dve.wait_ge(self.list_summed, x)
        dve.tensor_tensor(self.mark[:], self.g.k[:, K_IOTA:K_IOTA + CAP].unsqueeze(1).to_broadcast([P, NT, CAP]),
                          self.g.place[:, :, bass.ds(e, 1)].to_broadcast([P, NT, CAP]), ALU.is_equal).then_inc(self.marked, 1)

    def gather(self, pool, x, fill):
        pool.wait_ge(self.listed, 2 * x + 2)
        pool.wait_ge(self.turned, fill).then_inc(self.rows_free, 1)
        for rows, index, n in ((self.rows_a, self.list_a, 0), (self.rows_b, self.list_b, 1)):
            pool.indirect_dma_start(out=rows[:], out_offset=None, in_=self.g.xn_dram,
                                    in_offset=bass.IndirectOffsetOnAxis(ap=index[:, 0:1], axis=0)).then_inc(self.rows_in[n], 16)

    def pe_list(self, pe, x):
        pe.wait_ge(self.marked, x + 1)
        pe.wait_ge(self.listed, 2 * x)
        for width, lo, at in ((P, 0, 0), (CAP - P, P, 2)):
            for t in range(NT):
                mm = pe.matmul(self.ps[0:width, self.LIST, at:at + 2], self.mark[:, t, lo:lo + width],
                               self.token[:, 2 * t:2 * t + 2], start=(t == 0), stop=(t == NT - 1))
        mm.then_inc(self.list_summed, 1)

    def dve_list(self, dve, x):
        dve.wait_ge(self.list_summed, x + 1)
        for r in self.rows_in:
            dve.wait_ge(r, 16 * x)
        for width, to, at in ((P, self.list_a, 0), (CAP - P, self.list_b, 2)):
            with self.nc.allow_low_precision(reason="token numbers, summed in float32"):
                dve.tensor_reduce(to[0:width, 0:1], self.ps[0:width, self.LIST, at:at + 2], AX.X, ALU.add).then_inc(self.listed, 1)

    def dve_slots(self, dve):
        g, place_of = self.g, self.g.place[:, :, 0:E]
        dve.tensor_tensor(self.step[:, 0], place_of, g.k[:, K_SLOT:K_SLOT + E].unsqueeze(1).to_broadcast([P, NT, E]),
                          ALU.add).then_inc(self.slot_step, 1)
        for r in range(1, ROUNDS):
            dve.tensor_scalar(self.step[:, 1], place_of, float(r * CAP), float(Y_ROUND - CAP), ALU.is_ge, ALU.mult).then_inc(self.slot_step, 1)
            dve.wait_ge(self.slot_step, 2 * r)
            dve.tensor_tensor(self.step[:, 0], self.step[:, 0], self.step[:, 1], ALU.add).then_inc(self.slot_step, 1)
            dve.wait_ge(self.slot_step, 2 * r + 1)
        for k in range(TOPK):
            dve.tensor_tensor(self.weigh[:, :, k, :], g.hot[:, :, k, :], self.step[:, 0], ALU.mult).then_inc(self.slot_prod, 1)
        dve.wait_ge(self.slot_prod, TOPK)
        with self.nc.allow_low_precision(reason="whole numbers below 2**24, summed in float32"):
            dve.tensor_reduce(g.slot[:].rearrange("p t k -> p (t k)"), self.weigh[:].rearrange("p t k e -> p (t k) e"), AX.X,
                              ALU.add).then_inc(self.slot_done, 1)
        dve.reciprocal(g.neg[:, :, 1:2], g.neg[:, :, 1:2]).then_inc(self.share_inv, 1)
        dve.wait_ge(self.share_inv, 1)
        dve.tensor_tensor(g.share[:], g.top[:, :, 0:TOPK], g.neg[:, :, 1:2].to_broadcast([P, NT, TOPK]), ALU.mult).then_inc(self.share_done, 1)

    def turned_x(self, q):
        return self.ps[:, self.TURN, 0:2 * CAP] if q < 3 else self.ps[:, self.LIST, 8:8 + 2 * CAP]

    def pe_turn_x(self, pe, x, fill, q):
        if q == 0:
            for r in self.rows_in:
                pe.wait_ge(r, 16 * x + 16)
        pe.wait_ge(self.turn_kept, fill + (q if q < 3 else 2))
        into = self.turned_x(q)
        for i in range(2):
            k = 2 * q + i
            pe.transpose(into[:, i * CAP:i * CAP + P], self.rows_a[:, k * P:(k + 1) * P], self.ident)
            mm = pe.transpose(into[:, i * CAP + P:(i + 1) * CAP], self.rows_b[:, k * P:(k + 1) * P],
                              self.g.k[0:CAP - P, K_ID:K_ID + CAP - P])
        mm.then_inc(self.turned, 1)

    def act_keep_x(self, act, x, fill, q, after):
        act.wait_ge(self.turned, fill + q + 1)
        act.wait_ge(self.gu_done, after)
        act.copy(self.xT[:, 2 * q:2 * q + 2, :], self.turned_x(q).rearrange("p (i c) -> p i c", i=2)).then_inc(self.turn_kept, 1)

    def pe_gate_up(self, pe, m, fill_x, c, width):
        gate_bank, up_bank = self.GATE_UP[c % 2]
        if c == 0:
            pe.wait_ge(self.turn_kept, fill_x)
        pe.wait_ge(self.gu_kept, 16 * m + 4 * c + 4)
        for half, bank in ((0, gate_bank), (1, up_bank)):
            slot = 2 * c + half
            w = ring_slot(self.g, slot).rearrange("p (k n) -> p k n", k=KT)
            pe.wait_ge(self.g.w_in_ring[slot], 16 * m + 16)
            for i in range(2):
                for k in range(KT):
                    mm = pe.matmul(self.ps[:, bank, i * CAP:i * CAP + width], w[:, k, i * P:(i + 1) * P], self.xT[:, k, 0:width],
                                   start=(k == 0), stop=(k == KT - 1))
            mm.then_inc(self.gu_done, 1)

    def dve_gate_up(self, dve, m, e, c):
        gate_bank, up_bank = self.GATE_UP[c % 2]
        gate, up = self.gate[:, c % 2], self.up[:, c % 2]
        dve.wait_ge(self.gu_done, 8 * m + 2 * c + 1)
        for i in range(2):
            bias = self.g.b_gu[:, bass.ds(e, 1), 2 * c + i:2 * c + i + 1].rearrange("p a b -> p (a b)")
            dve.tensor_scalar(gate[:, i], self.ps[:, gate_bank, i * CAP:(i + 1) * CAP], bias, 7.0, ALU.add, ALU.min).then_inc(self.gu_kept, 1)
        dve.wait_ge(self.gu_done, 8 * m + 2 * c + 2)
        for i in range(2):
            bias = self.g.b_gu[:, bass.ds(e, 1), 8 + 2 * c + i:8 + 2 * c + i + 1].rearrange("p a b -> p (a b)")
            dve.tensor_scalar(up[:, i], self.ps[:, up_bank, i * CAP:(i + 1) * CAP], bias, -7.0, ALU.add, ALU.max).then_inc(self.gu_kept, 1)
        dve.wait_ge(self.gu_kept, 16 * m + 4 * c + 4 + 8)
        dve.tensor_scalar(up, up, 7.0, 1.0, ALU.min, ALU.add).then_inc(self.act_step, 1)
        dve.wait_ge(self.sig_done, 4 * m + c + 1)
        dve.tensor_tensor(gate, gate, self.sig[:, c % 2], ALU.mult).then_inc(self.act_step, 1)
        dve.wait_ge(self.act_step, 8 * m + 2 * c + 4)
        if c == 0:
            dve.wait_ge(self.yT_kept, 8 * m + 4)
        dve.tensor_tensor(self.hT[:, 2 * c:2 * c + 2, :], up, gate, ALU.mult).then_inc(self.h_done, 1)

    def act_sigmoid(self, act, m, c):
        act.wait_ge(self.gu_kept, 16 * m + 4 * c + 2 + 8)
        act.wait_ge(self.act_step, 8 * m + 2 * c + 2)
        act.activation(self.sig[:, c % 2], self.gate[:, c % 2], ACT.Sigmoid, scale=1.702).then_inc(self.sig_done, 1)

    def pe_down(self, pe, m, c, width):
        w = ring_slot(self.g, 8 + c).rearrange("p (k n) -> p k n", k=KT)
        bank = self.DOWN[c % 2]
        pe.wait_ge(self.g.w_in_ring[8 + c], 16 * m + 16)
        pe.wait_ge(self.yT_kept, 8 * m + 2 * c + 2)
        for k in range(KT):
            if c == 0 and k % 2 == 0:
                pe.wait_ge(self.h_done, 4 * m + k // 2 + 1)
            for i in range(2):
                mm = pe.matmul(self.ps[:, bank, i * CAP:i * CAP + width], w[:, k, i * P:(i + 1) * P], self.hT[:, k, 0:width],
                               start=(k == 0 and i == 0), stop=(k == KT - 1), skip_group_check=True)
        mm.then_inc(self.dn_done, 1)

    def act_down(self, act, m, e, c):
        act.wait_ge(self.dn_done, 4 * m + c + 1)
        for i in range(2):
            bias = self.g.b_dn[:, bass.ds(e, 1), 2 * c + i:2 * c + i + 1].rearrange("p a b -> p (a b)")
            act.activation(self.yT[:, 2 * c + i, :], self.ps[:, self.DOWN[c % 2], i * CAP:(i + 1) * CAP], ACT.Identity,
                           bias=bias).then_inc(self.yT_kept, 1)

    def pe_turn_y(self, pe, fill, kept, q):
        if q == 0:
            pe.wait_ge(self.yT_kept, kept)
        if q < 2:
            pe.wait_ge(self.turn_kept, fill + q)
        else:
            pe.wait_ge(self.turn_kept, fill + q).then_inc(self.bank6_free, 1)
        tokens = slice(0, P) if q < 2 else slice(P, CAP)
        n = P if q < 2 else CAP - P
        for i in range(4):
            mm = pe.transpose(self.ps[0:n, self.TURN, i * P:(i + 1) * P], self.yT[:, 4 * (q % 2) + i, tokens], self.ident)
        mm.then_inc(self.turned, 1)

    def dve_keep_y(self, dve, y, fill, q):
        dve.wait_ge(self.turned, fill + q + 1)
        n, to = (P, self.y_a) if q < 2 else (CAP - P, self.y_b)
        dve.wait_ge(self.y_out[q // 2], 16 * y + 16)
        dve.tensor_copy(to[0:n, (q % 2) * HALF:(q % 2 + 1) * HALF], self.ps[0:n, self.TURN, :]).then_inc(self.turn_kept, 1)

    def store(self, sp, fill, dst_a, dst_b):
        sp.wait_ge(self.turn_kept, fill + 4)
        sp.dma_start(dst_a, self.y_a[:]).then_inc(self.y_out[0], 16)
        sp.dma_start(dst_b, self.y_b[:]).then_inc(self.y_out[1], 16)


WIDTHS = tuple(range(P, CAP + 1, 8))
DOWN_THEN_TURNS = ((0, (0,)), (1, (1,)), (2, (2, 3)), (3, ()))


def experts(nc, g, sem):
    with ExitStack() as ph:
        x = Experts(nc, g, sem, ph)
        block = ph.enter_context(nc.Block())

        def rows(region):
            part = g.y_dram.rearrange("(r n) d -> r n d", n=CAP)[bass.ds(region, 1)].rearrange("a n d -> (a n) d")
            return part[0:P, :], part[P:CAP, :]

        def load(sp, e, i):
            if i < 8:
                src = g.w_gate_up[bass.ds(e, 1)].rearrange("a (k p) n -> p (a k) n", p=P)[:, :, (i % 2) * FF + (i // 2) * 256:(i % 2) * FF + (i // 2) * 256 + 256]
            else:
                src = g.w_down[bass.ds(e, 1)].rearrange("a (k p) n -> p (a k) n", p=P)[:, :, (i - 8) * 256:(i - 7) * 256]
            sp.dma_start(ring_slot(g, i).rearrange("p (k n) -> p k n", k=KT), src).then_inc(g.w_in_ring[i], 16)

        def overflow(eng, body, start=None, end=None):
            most = eng.value_load(g.count[0:1, E:E + 1], min_val=0, max_val=T)
            with eng.If(most > CAP):
                n_reg = eng.alloc_register("n_" + str(eng.engine).split(".")[-1])
                eng.reg_mov(n_reg, 0)
                with eng.Fori(1, ROUNDS) as r:
                    if start is not None:
                        start(r)
                    with eng.Fori(0, E) as e:
                        count = eng.value_load(g.count[0:1, bass.ds(e, 1)], min_val=0, max_val=T)
                        with eng.If(count > r * CAP):
                            n = eng.snap(n_reg, min_val=0, max_val=E * ROUNDS)
                            body(n, r, e)
                            eng.reg_add(n_reg, n_reg, 1)
                if end is not None:
                    end()

        @block.sync
        def _(sp):
            for i in range(8, 12):
                load(sp, 0, i)
            with sp.Fori(0, E - 1) as e:
                for i in range(12):
                    if i < 8:
                        sp.wait_ge(x.gu_done, 8 * e + i + 1)
                    else:
                        sp.wait_ge(x.dn_done, 4 * e + i - 7)
                    load(sp, e + 1, i)
                    if i == 7:
                        x.store(sp, 8 * e + 4, *rows(e))

            def load_embedding():
                w_gate, w_proj, post, final = g.ple_weights
                sp.dma_start(w_gate, g.w_ple_gate.rearrange("a (k p) n -> p (a k) n", p=P)).then_inc(g.ple_in, 16)
                sp.wait_ge(x.gu_done, 8 * (E - 1) + 6)
                sp.dma_start(w_proj, g.w_ple_proj.rearrange("a (k p) n -> p (a k) n", p=P)).then_inc(g.ple_in, 16)
                sp.dma_start(post, g.g_ple_post.rearrange("a d -> (a d)").partition_broadcast(P)).then_inc(g.ple_in, 16)
                sp.dma_start(final, g.g_final.partition_broadcast(P)).then_inc(g.ple_in, 16)

            most = sp.value_load(g.count[0:1, E:E + 1], min_val=0, max_val=T)
            sp.wait_ge(x.gu_done, 8 * (E - 1) + 4)
            with sp.If(most <= CAP):
                load_embedding()
            for y in range(E - 1, E + 1):
                x.store(sp, 8 * y + 4, *rows(y))

            def body(n, r, e):
                sp.wait_ge(x.dn_done, 4 * n + 4 * E)
                for i in range(12):
                    load(sp, e, i)
                x.store(sp, 8 * n + 8 * (E + 1) + 4, *rows(r * E + e + 1))
                sp.wait_ge(x.y_out[0], 16 * n + 16 * (E + 3))
                sp.wait_ge(x.y_out[1], 16 * n + 16 * (E + 3)).then_inc(x.pass_stored, 1)

            def fill(r):
                into = g.y_dram[Y_FIRST:, :].rearrange("(r n p) d -> r p n d", r=ROUNDS - 1, p=P)[bass.ds(r - 1, 1)]
                sp.dma_start(into.rearrange("a p n d -> (a p) n d"),
                             x.y_a[:].unsqueeze(1).to_broadcast([P, Y_ROUND // P, D])).then_inc(x.filled, 16)
                sp.wait_ge(x.filled, 16 * r).then_inc(x.fill_seen, 1)

            overflow(sp, body, fill, load_embedding)
            for s in x.y_out:
                sp.wait_ge(s, 16 * (E + 2))

        @block.gpsimd
        def _(pool):
            x.gather(pool, 0, 0)
            with pool.Fori(0, E) as e:
                x.gather(pool, e + 1, 8 * e + 4)

            def body(n, r, e):
                x.gather(pool, n + E + 1, 8 * n + 8 * (E + 1))
                for s in x.rows_in:
                    pool.wait_ge(s, 16 * n + 16 * (E + 2))

            overflow(pool, body)
            for s in x.rows_in:
                pool.wait_ge(s, 16 * (E + 1))

        @block.tensor
        def _(pe):
            pe.wait_ge(x.ready, 1)
            x.pe_list(pe, 0)
            for q in range(4):
                x.pe_turn_x(pe, 0, 0, q)

            def one_pass(e, width):
                for c in range(4):
                    x.pe_gate_up(pe, e, 8 * e + 4, c, width)
                    if c == 0:
                        x.pe_list(pe, e + 1)
                    x.pe_turn_y(pe, 8 * e + 4, 8 * e + 4, c)
                for c, turns in DOWN_THEN_TURNS:
                    x.pe_down(pe, e, c, width)
                    for q in turns:
                        x.pe_turn_x(pe, e + 1, 8 * e + 8, q)

            def by_width(count, widths, body):
                if len(widths) == 1:
                    body(widths[0])
                    return
                mid = len(widths) // 2
                with pe.If(count <= widths[mid - 1]):
                    by_width(count, widths[:mid], body)
                with pe.Else():
                    by_width(count, widths[mid:], body)

            with pe.Fori(0, E) as e:
                count = pe.value_load(g.count[0:1, bass.ds(e, 1)], min_val=0, max_val=T)
                by_width(count, WIDTHS, lambda width: one_pass(e, width))
            for q in range(4):
                x.pe_turn_y(pe, 8 * E + 4, 8 * E + 4, q)

            def body(n, r, e):
                m, fill = n + E, 8 * n + 8 * (E + 1)
                x.pe_list(pe, n + E + 1)
                for q in range(4):
                    x.pe_turn_x(pe, n + E + 1, fill, q)
                for c in range(4):
                    x.pe_gate_up(pe, m, fill + 4, c, CAP)
                for c in range(4):
                    x.pe_down(pe, m, c, CAP)
                for q in range(4):
                    x.pe_turn_y(pe, fill + 4, 8 * m + 8 + 4, q)

            overflow(pe, body)

        @block.scalar
        def _(act):
            act.copy(x.sig[:, 0, 0, 0:1], g.eps[:, 0:1]).then_inc(x.yT_kept, 4)
            for q in range(4):
                x.act_keep_x(act, 0, 0, q, 0)
            with act.Fori(0, E) as e:
                for c in range(4):
                    x.act_sigmoid(act, e, c)
                for c, turns in DOWN_THEN_TURNS:
                    x.act_down(act, e, e, c)
                    for q in turns:
                        x.act_keep_x(act, e + 1, 8 * e + 8, q, 8 * e + 8)

            def body(n, r, e):
                m, fill = n + E, 8 * n + 8 * (E + 1)
                for q in range(4):
                    x.act_keep_x(act, n + E + 1, fill, q, 8 * m)
                for c in range(4):
                    x.act_sigmoid(act, m, c)
                for c in range(4):
                    x.act_down(act, m, e, c)

            overflow(act, body)

        @block.vector
        def _(dve):
            dve.memset(x.list_a[:], 0).then_inc(x.act_step, 2)
            dve.memset(x.y_a[:, 0:1], 0.0).then_inc(x.y_out[0], 16)
            dve.memset(x.y_b[:, 0:1], 0.0).then_inc(x.y_out[1], 16)
            dve.tensor_copy(x.token[:], g.k[:, K_TOK:K_TOK + 2 * NT]).then_inc(x.ready, 1)
            x.dve_find(dve, 0, 0)
            x.dve_list(dve, 0)
            dve.memset(x.ps[:, 0:6, :], 0.0).then_inc(x.gu_kept, 8)
            x.dve_slots(dve)
            with dve.Fori(0, E) as e:
                x.dve_find(dve, e + 1, e + 1)
                for c in range(4):
                    x.dve_gate_up(dve, e, e, c)
                    if c == 0:
                        x.dve_list(dve, e + 1)
                    x.dve_keep_y(dve, e, 8 * e + 4, c)
            for q in range(4):
                x.dve_keep_y(dve, E, 8 * E + 4, q)

            def body(n, r, e):
                m, fill = n + E, 8 * n + 8 * (E + 1)
                x.dve_find(dve, n + E + 1, e)
                x.dve_list(dve, n + E + 1)
                for c in range(4):
                    x.dve_gate_up(dve, m, e, c)
                for q in range(4):
                    x.dve_keep_y(dve, n + E + 1, fill + 4, q)

            def shift(r):
                dve.wait_ge(x.filled, 16 * r)
                dve.tensor_scalar(g.place[:], g.place[:], -float(CAP), None, ALU.add).then_inc(x.shifted, 1)
                dve.wait_ge(x.shifted, r).then_inc(x.shift_seen, 1)

            overflow(dve, body, shift)


def split_product(pe, out, left_hi, left_lo, right_hi, right_lo, tiles):
    terms = ((left_hi, right_hi), (left_hi, right_lo), (left_lo, right_hi))
    for k in range(tiles):
        for n, (left, right) in enumerate(terms):
            mm = pe.matmul(out, left(k), right(k), start=(k == 0 and n == 0), stop=(k == tiles - 1 and n == 2))
    return mm


def finish(nc, g, sem):
    AHEAD = 2
    with ExitStack() as ph:
        def sb(name, shape, dt=F32):
            return ph.enter_context(nc.sbuf_tensor("fi_" + name, shape, dt))

        w_gate, w_proj, post, final = g.ple_weights
        w_hi, w_lo = sb("w_gate_hi", [P, KT, D], F32R), sb("w_gate_lo", [P, KT, D], F32R)
        y = [sb("rows", [P, TOPK, D]), g.ring_a[:, 0:2].rearrange("p s (k n) -> p (s k) n", n=D)]
        normed = g.ring_a[:, 2].rearrange("p (t n) -> p t n", n=D)
        pe_n = g.ring_a[:, 3].rearrange("p (t n) -> p t n", n=D)
        h_hi, h_lo = sb("h_hi", [P, 2, KT, P], F32R), sb("h_lo", [P, 2, KT, P], F32R)
        pt = sb("p", [P, NT, PLE])
        pT = sb("pT", [P, 2, T])
        junk = sb("junk", [P, D], BF16)
        stat = sb("stat", [P, 6, NT])
        ps = ph.enter_context(nc.psum_tensor("fi_psum", [P, 8, HALF], F32))
        ident = g.k[:, K_ID:K_ID + P]
        out_dram = g.out.rearrange("a (t p) d -> (a t) p d", p=P)

        p_in = sem("p_in")
        y_in, out_s = [sem(f"rows_in{i}") for i in range(2)], [sem(f"out{i}") for i in range(2)]
        p_turned, p_kept, w_hi_done, w_lo_done = (sem(n) for n in ("p_turned", "p_kept", "weights_hi", "weights_lo"))
        mixed, turned, h_hi_done, h_lo_done, gated = (sem(n) for n in ("mixed", "turned", "h_hi", "h_lo", "gate_products"))
        sq, root, inv = (sem(n) for n in ("squares", "roots", "inverses"))
        proj, pe_sq, pe_root, pe_inv, pe_done = (sem(n) for n in ("projected", "pe_squares", "pe_roots", "pe_inverses", "pe_normed"))
        sig_done, gate_mul, added, o_sq, o_root, o_inv, o_done = (sem(n) for n in (
            "sigmoid", "gate_mul", "added", "out_squares", "out_roots", "out_inverses", "out_normed"))
        block = ph.enter_context(nc.Block())

        @block.sync
        def _(sp):
            sp.dma_start(pt[:], g.p.rearrange("a b (t p) d -> p (a b t) d", p=P)).then_inc(p_in, 16)
            for t in range(NT):
                sp.wait_ge(o_done, t + 1)
                sp.dma_start(out_dram[t], normed[:, t % 2]).then_inc(out_s[t % 2], 16)
            for s in out_s:
                sp.wait_ge(s, 16 * NT // 2)

        @block.gpsimd
        def _(pool):
            def gather_rows(source):
                for t in range(NT):
                    if t >= 2:
                        pool.wait_ge(mixed, TOPK * (t - 1))
                    if t == 1:
                        pool.wait_ge(w_lo_done, KT // 2)
                    for k in range(TOPK):
                        pool.indirect_dma_start(out=y[t % 2][:, k, :], out_offset=None, in_=source,
                                                in_offset=bass.IndirectOffsetOnAxis(ap=g.slot[:, t, k:k + 1], axis=0)).then_inc(y_in[t % 2], 16)

            most = pool.value_load(g.count[0:1, E:E + 1], min_val=0, max_val=T)
            with pool.If(most <= CAP):
                gather_rows(g.y_dram[0:Y_FIRST, :])
            with pool.Else():
                gather_rows(g.y_dram)
            for s in y_in:
                pool.wait_ge(s, 16 * TOPK * NT // 2)

        @block.tensor
        def _(pe):
            def embed(t):
                if t >= 1:
                    pe.wait_ge(pe_done, t)
                for half in range(2):
                    for k in range(2):
                        mm = pe.matmul(ps[:, 4 + half, :], pT[:, k, t * P:(t + 1) * P], w_proj[:, k, half * HALF:(half + 1) * HALF], start=(k == 0), stop=(k == 1))
                mm.then_inc(proj, 1)

            def turn(t):
                pe.wait_ge(mixed, TOPK * (t + 1))
                for q in range(2):
                    if t >= 1:
                        pe.wait_ge(h_lo_done, 2 * (t - 1) + q + 1)
                    for i in range(4):
                        mm = pe.transpose(ps[:, 6 + q, i * P:(i + 1) * P], g.h[:, t, (4 * q + i) * P:(4 * q + i + 1) * P], ident)
                    mm.then_inc(turned, 1)

            def gate(t):
                pe.wait_ge(h_lo_done, 2 * t + 2)
                if t == 0:
                    pe.wait_ge(w_lo_done, KT)
                    pe.wait_ge(p_kept, 4)
                if t >= 2:
                    pe.wait_ge(gate_mul, t - 1)
                for half in range(2):
                    if half == 1 and t + 1 < NT:
                        turn(t + 1)
                    cols = slice(half * HALF, (half + 1) * HALF)
                    mm = split_product(pe, ps[:, 2 * (t % 2) + half, :], lambda k: h_hi[:, t % 2, k, :], lambda k: h_lo[:, t % 2, k, :],
                                       lambda k: w_hi[:, k, cols], lambda k: w_lo[:, k, cols], KT)
                mm.then_inc(gated, 1)

            pe.wait_ge(p_in, 16)
            for n in range(4):
                for i in range(4):
                    t, k = (n % 2) * 4 + i, n // 2
                    mm = pe.transpose(ps[:, n, i * P:(i + 1) * P], pt[:, t, k * P:(k + 1) * P], ident)
                mm.then_inc(p_turned, 1)
            pe.wait_ge(g.ple_in, 64)
            pe.wait_ge(p_kept, 4)
            embed(0)
            turn(0)
            embed(1)
            for t in range(NT):
                gate(t)
                if t + AHEAD < NT:
                    embed(t + AHEAD)

        @block.scalar
        def _(act):
            def embed(t):
                act.wait_ge(proj, t + 1)
                act.activation(junk[:], ps[:, 4:6, :].rearrange("p a c -> p (a c)"), ACT.Square, accum_out=stat[:, 0, t:t + 1]).then_inc(pe_sq, 1)
                act.wait_ge(pe_sq, t + 1)
                act.activation(stat[:, 1, t:t + 1], stat[:, 0, t:t + 1], ACT.Sqrt, scale=1.0 / D, bias=g.eps[:, 0:1]).then_inc(pe_root, 1)

            def keep_hi(t):
                if t >= 2:
                    act.wait_ge(gated, t - 1)
                for q in range(2):
                    act.wait_ge(turned, 2 * t + q + 1)
                    act.copy(h_hi[:, t % 2, 4 * q:4 * q + 4, :], ps[:, 6 + q, :].rearrange("p (k c) -> p k c", k=4)).then_inc(h_hi_done, 1)

            def squares(t):
                act.wait_ge(mixed, TOPK * (t + 1))
                act.activation(junk[:], g.h[:, t, :], ACT.Square, accum_out=stat[:, 2, t:t + 1]).then_inc(sq, 1)
                act.wait_ge(sq, t + 1)
                act.activation(stat[:, 3, t:t + 1], stat[:, 2, t:t + 1], ACT.Sqrt, scale=1.0 / D, bias=g.eps[:, 0:1]).then_inc(root, 1)

            def sigmoid(t):
                act.wait_ge(gated, t + 1)
                act.wait_ge(inv, t + 1)
                products = ps[:, 2 * (t % 2):2 * (t % 2) + 2, :].rearrange("p a c -> p (a c)")
                act.activation(products, products, ACT.Sigmoid, scale=stat[:, 3, t:t + 1]).then_inc(sig_done, 1)

            def out_squares(t):
                act.wait_ge(added, t + 1)
                act.activation(junk[:], g.h[:, t, :], ACT.Square, accum_out=stat[:, 4, t:t + 1]).then_inc(o_sq, 1)
                act.wait_ge(o_sq, t + 1)
                act.activation(stat[:, 5, t:t + 1], stat[:, 4, t:t + 1], ACT.Sqrt, scale=1.0 / D, bias=g.eps[:, 0:1]).then_inc(o_root, 1)

            act.wait_ge(g.ple_in, 64)
            for k in range(KT):
                if k == KT // 2:
                    for n in range(4):
                        act.wait_ge(p_turned, n + 1)
                        act.copy(pT[:, n // 2, (n % 2) * HALF:(n % 2 + 1) * HALF], ps[:, n, :]).then_inc(p_kept, 1)
                act.activation(w_hi[:, k, :], w_gate[:, k, :], ACT.Copy, scale=g.par[:, R_PLE + k:R_PLE + k + 1]).then_inc(w_hi_done, 1)
                if k == 6:
                    embed(0)
            keep_hi(0)
            squares(0)
            embed(1)
            for t in range(NT):
                if t + 1 < NT:
                    keep_hi(t + 1)
                    squares(t + 1)
                sigmoid(t)
                if t + AHEAD < NT:
                    embed(t + AHEAD)
                out_squares(t)

        @block.vector
        def _(dve):
            def embed(t):
                dve.wait_ge(pe_root, t + 1)
                dve.reciprocal(stat[:, 1, t:t + 1], stat[:, 1, t:t + 1]).then_inc(pe_inv, 1)
                dve.wait_ge(pe_inv, t + 1)
                if t >= AHEAD:
                    dve.wait_ge(added, t - AHEAD + 1)
                dve.scalar_tensor_tensor(out=pe_n[:, t % AHEAD], in0=ps[:, 4:6, :].rearrange("p a c -> p (a c)"), scalar=stat[:, 1, t:t + 1],
                                         in1=post, op0=ALU.mult, op1=ALU.mult).then_inc(pe_done, 1)

            def mix(t):
                dve.wait_ge(y_in[t % 2], 16 * TOPK * (t // 2 + 1))
                for k in range(TOPK):
                    if k >= 1:
                        dve.wait_ge(mixed, TOPK * t + k)
                    dve.scalar_tensor_tensor(out=g.h[:, t, :], in0=y[t % 2][:, k, :], scalar=g.share[:, t, k:k + 1], in1=g.h[:, t, :],
                                             op0=ALU.mult, op1=ALU.add).then_inc(mixed, 1)

            def keep_lo(t):
                if t >= 2:
                    dve.wait_ge(gated, t - 1)
                for q in range(2):
                    ks = slice(4 * q, 4 * q + 4)
                    dve.wait_ge(h_hi_done, 2 * t + q + 1)
                    dve.tensor_tensor(h_lo[:, t % 2, ks, :], ps[:, 6 + q, :].rearrange("p (k c) -> p k c", k=4),
                                      h_hi[:, t % 2, ks, :].bitcast(F32), ALU.subtract).then_inc(h_lo_done, 1)

            def inverse(t):
                dve.wait_ge(root, t + 1)
                dve.reciprocal(stat[:, 3, t:t + 1], stat[:, 3, t:t + 1]).then_inc(inv, 1)

            def gate(t):
                dve.wait_ge(sig_done, t + 1)
                dve.tensor_tensor(pe_n[:, t % AHEAD], pe_n[:, t % AHEAD], ps[:, 2 * (t % 2):2 * (t % 2) + 2, :].rearrange("p a c -> p (a c)"),
                                  ALU.mult).then_inc(gate_mul, 1)
                dve.wait_ge(gate_mul, t + 1)
                dve.wait_ge(turned, 2 * t + 2)
                dve.wait_ge(sq, t + 1)
                dve.tensor_tensor(g.h[:, t, :], g.h[:, t, :], pe_n[:, t % AHEAD], ALU.add).then_inc(added, 1)

            def norm(t):
                dve.wait_ge(o_root, t + 1)
                dve.reciprocal(stat[:, 5, t:t + 1], stat[:, 5, t:t + 1]).then_inc(o_inv, 1)
                dve.wait_ge(o_inv, t + 1)
                if t >= 2:
                    dve.wait_ge(out_s[t % 2], 16 * (t // 2))
                dve.scalar_tensor_tensor(out=normed[:, t % 2], in0=g.h[:, t, :], scalar=stat[:, 5, t:t + 1], in1=final,
                                         op0=ALU.mult, op1=ALU.mult).then_inc(o_done, 1)

            dve.wait_ge(g.ple_in, 64)
            for k in range(KT):
                if k == KT // 2:
                    mix(0)
                dve.wait_ge(w_hi_done, k + 1)
                dve.scalar_tensor_tensor(out=w_lo[:, k, :], in0=w_gate[:, k, :], scalar=g.par[:, R_PLE + k:R_PLE + k + 1],
                                         in1=w_hi[:, k, :].bitcast(F32), op0=ALU.mult, op1=ALU.subtract).then_inc(w_lo_done, 1)
            keep_lo(0)
            inverse(0)
            dve.wait_ge(w_lo_done, KT)
            embed(0)
            embed(1)
            mix(1)
            for t in range(NT):
                if t + 1 < NT:
                    keep_lo(t + 1)
                    inverse(t + 1)
                if t + 2 < NT:
                    mix(t + 2)
                gate(t)
                if t + AHEAD < NT:
                    embed(t + AHEAD)
                norm(t)


_INS = ["x", "p", "g_mix", "w_in", "w_gla_gate", "b_gla_gate", "g_gla_out", "w_conv", "gdn_a_log", "gdn_dt_bias", "g_gdn_out",
        "w_out", "g_moe", "w_router", "b_router", "w_gate_up", "b_gate_up", "w_down", "b_down", "g_ple_in", "w_ple_gate",
        "w_ple_proj", "g_ple_post", "g_final"]


class Names:
    pass


def program(nc, arrays, out):
    g = Names()
    g.x = arrays["x"].rearrange("a t d -> (a t) d")
    g.w_in = arrays["w_in"].rearrange("a k n -> (a k) n")
    g.w_conv = arrays["w_conv"].rearrange("a k n -> a (k n)")
    g.w_gate_up = arrays["w_gate_up"].rearrange("a e k n -> (a e) k n")
    g.w_down = arrays["w_down"].rearrange("a e k n -> (a e) k n")
    g.p, g.g_mix, g.w_gla_gate, g.b_gla_gate = arrays["p"], arrays["g_mix"], arrays["w_gla_gate"], arrays["b_gla_gate"]
    g.g_gla_out, g.gdn_a_log, g.gdn_dt_bias, g.g_gdn_out = arrays["g_gla_out"], arrays["gdn_a_log"], arrays["gdn_dt_bias"], arrays["g_gdn_out"]
    g.w_out, g.g_moe, g.w_router, g.b_router = arrays["w_out"], arrays["g_moe"], arrays["w_router"], arrays["b_router"]
    g.b_gate_up, g.b_down, g.g_ple_in, g.w_ple_gate = arrays["b_gate_up"], arrays["b_down"], arrays["g_ple_in"], arrays["w_ple_gate"]
    g.w_ple_proj, g.g_ple_post, g.g_final, g.consts = arrays["w_ple_proj"], arrays["g_ple_post"], arrays["g_final"], arrays["consts"]
    g.out = out
    g.gates_dram = nc.dram_tensor("gates_dram", (2, T, HALF), F32).ap()
    g.xn_dram = nc.dram_tensor("xn_dram", (T, D), F32).ap()
    g.y_dram = nc.dram_tensor("y_dram", (Y_FIRST + (ROUNDS - 1) * Y_ROUND, D), F32).ap()
    with ExitStack() as ctx:
        def sb(name, shape, dt=F32):
            return ctx.enter_context(nc.sbuf_tensor(name, shape, dt))

        g.k = sb("constants", [P, K_END])
        g.eps = sb("eps", [P, 1])
        g.par = sb("parameter_columns", [P, R_END])
        g.setup_done = ctx.enter_context(nc.semaphore("setup_done"))
        g.ple_in = ctx.enter_context(nc.semaphore("embedding_weights_in"))
        g.w_in_ring = [ctx.enter_context(nc.semaphore(f"expert_weights_in{i}")) for i in range(12)]
        with ExitStack() as mixed:
            with ExitStack() as mixers:
                g.dab = mixers.enter_context(nc.sbuf_tensor("dab", [P, NT, 8], F32))
                g.qkvT = mixers.enter_context(nc.sbuf_tensor("qkvT", [P, NQKV, T], F32))
                with ExitStack() as gl:
                    g.gqkT = gl.enter_context(nc.sbuf_tensor("gqkT", [P, 4, T], F32))
                    g.glrT = gl.enter_context(nc.sbuf_tensor("glrT", [16, T], F32))
                    g.gv = gl.enter_context(nc.sbuf_tensor("gv", [P, NT, HALF], F32))
                    with stage_signals(nc, "project") as sem:
                        project(nc, g, sem)
                    g.mixA = mixed.enter_context(nc.sbuf_tensor("mixed_gla", [P, NH, T], F32, side="right"))
                    with stage_signals(nc, "gla") as sem:
                        gla(nc, g, sem)
                g.mixB = mixed.enter_context(nc.sbuf_tensor("mixed_delta", [P, NH, T], F32, side="right"))
                with stage_signals(nc, "delta") as sem:
                    delta(nc, g, sem)
            g.h = sb("h", [P, NT, D])
            g.ring_a = sb("weight_ring_a", [P, RING_A, 2 * D])
            g.ple_weights = (g.ring_a[:, 0:4].rearrange("p s n -> p (s n)").rearrange("p (k n) -> p k n", k=KT),
                             g.ring_a[:, 4].rearrange("p (k n) -> p k n", k=2), g.ring_a[:, 5, 0:D], g.ring_a[:, 5, D:2 * D])
            g.place = sb("place", [P, NT, E + 1])
            g.top = sb("top", [P, NT, 8])
            g.neg = sb("neg", [P, NT, 2])
            g.slot = sb("slot", [P, NT, TOPK], U32)
            g.share = sb("share", [P, NT, TOPK])
            g.count = sb("count", [P, E + 1], I32)
            g.b_gu = sb("bias_gate_up", [P, E, 2 * FF // P])
            g.b_dn = sb("bias_down", [P, E, D // P])
            routed = ctx.enter_context(ExitStack())
            g.hot = routed.enter_context(nc.sbuf_tensor("hot", [P, NT, TOPK, E], F32))
            g.ring_b = routed.enter_context(nc.sbuf_tensor("weight_ring_b", [P, 12 - RING_A, 2 * D], F32))
            with stage_signals(nc, "route") as sem:
                route(nc, g, sem)
        with stage_signals(nc, "experts") as sem:
            experts(nc, g, sem)
        routed.close()
        with stage_signals(nc, "finish") as sem:
            finish(nc, g, sem)


def kernel(**inputs):
    import numpy as _np
    import concourse.bacc as _bacc
    from concourse import mybir as _mybir
    from concourse.bass_utils import run_bass_kernel_spmd as _run

    nc = _bacc.Bacc("TRN2", target_bir_lowering=False, num_devices=1)
    arrays, aps = {}, {}
    given = {name: _np.ascontiguousarray(inputs[name]) for name in _INS}
    given["consts"] = constants()
    for name, a in given.items():
        arrays[f"in_{name}"] = a
        aps[name] = nc.dram_tensor(f"in_{name}", a.shape, _mybir.dt.from_np(a.dtype), kind="ExternalInput").ap()
    out = nc.dram_tensor("out", (1, T, D), F32, kind="ExternalOutput").ap()
    program(nc, aps, out)
    r = _run(nc, [arrays], core_ids=[0])
    return r.results[0]["out"]
```
